# Optimizing a Trainium2 kernel written in Bass

```python
import jax, jax.numpy as jnp
from jax import lax
import numpy as np

D_MODEL = 1024
BATCH = 1
SEQ = 1024
DEPTH = 1

GRID_W = 64
CTX_LEN = 256
HEAD_DIM = 64
A_HEADS = 8
A_KV_HEADS = 2
A_WINDOW = 128
A_BLOCK = 128
B_HEADS = 8
NA_MAX_KH = 8
NA_KW = 16
NA_ROW_BLOCK = 2
A_WIDTH = A_HEADS * HEAD_DIM
A_KV_WIDTH = A_KV_HEADS * HEAD_DIM
B_WIDTH = B_HEADS * HEAD_DIM
MIX_WIDTH = A_WIDTH + B_WIDTH
IN_COLS = A_WIDTH + 2 * A_KV_WIDTH + 3 * B_WIDTH
FFN_HIDDEN = -(-8 * D_MODEL // (3 * 256)) * 256
N_MOD = 6
ROPE_BASE = 10000.0
EPS = 1e-6


def _rms_norm(x, g):
    xf = x.astype(jnp.float32)
    y = xf * lax.rsqrt(jnp.mean(xf * xf, axis=-1, keepdims=True) + EPS)
    return (y * g.astype(jnp.float32)).astype(x.dtype)

def _modulate(h, shift, scale):
    return h * (1 + scale) + shift

def _axial_rope(x, rows, cols):
    half = HEAD_DIM // 2
    quarter = half // 2
    inv_freq = 1.0 / (ROPE_BASE ** (jnp.arange(quarter, dtype=jnp.float32) / quarter))

    def rot(xh, pos):
        ang = pos.astype(jnp.float32)[:, None] * inv_freq[None, :]
        cos = jnp.cos(ang)[None, :, None, :]
        sin = jnp.sin(ang)[None, :, None, :]
        x1 = xh[..., :quarter].astype(jnp.float32)
        x2 = xh[..., quarter:].astype(jnp.float32)
        return jnp.concatenate([x1 * cos - x2 * sin, x1 * sin + x2 * cos], axis=-1)

    out = jnp.concatenate([rot(x[..., :half], rows), rot(x[..., half:], cols)], axis=-1)
    return out.astype(x.dtype)

def _in_proj(h, w_in):
    B, L, _ = h.shape
    p = h @ w_in
    offs = np.cumsum([A_WIDTH, A_KV_WIDTH, A_KV_WIDTH, B_WIDTH, B_WIDTH])
    q_a, k_a, v_a, q_b, k_b, v_b = jnp.split(p, offs, axis=-1)
    hd = lambda t, n: t.reshape(B, L, n, HEAD_DIM)
    return (hd(q_a, A_HEADS), hd(k_a, A_KV_HEADS), hd(v_a, A_KV_HEADS),
            hd(q_b, B_HEADS), hd(k_b, B_HEADS), hd(v_b, B_HEADS))

def _band_mask(S):
    nb = S // A_BLOCK
    span = A_BLOCK + 2 * A_WINDOW
    qpos = np.arange(nb)[:, None, None] * A_BLOCK + np.arange(A_BLOCK)[None, :, None]
    kpos = np.arange(nb)[:, None, None] * A_BLOCK - A_WINDOW + np.arange(span)[None, None, :]
    return (np.abs(kpos - qpos) <= A_WINDOW) & (kpos >= 0) & (kpos < S)

def _window_gqa_latent(q, k, v, k_ctx, v_ctx, sink):
    B, S = q.shape[:2]
    nb = S // A_BLOCK
    G = A_HEADS // A_KV_HEADS
    n_side = A_WINDOW // A_BLOCK
    scale = HEAD_DIM ** -0.5
    pad = ((0, 0), (A_WINDOW, A_WINDOW), (0, 0), (0, 0))
    kp = jnp.pad(k, pad).reshape(B, nb + 2 * n_side, A_BLOCK, A_KV_HEADS, HEAD_DIM)
    vp = jnp.pad(v, pad).reshape(B, nb + 2 * n_side, A_BLOCK, A_KV_HEADS, HEAD_DIM)
    kb = jnp.concatenate([kp[:, o:o + nb] for o in range(2 * n_side + 1)], axis=2)
    vb = jnp.concatenate([vp[:, o:o + nb] for o in range(2 * n_side + 1)], axis=2)
    span = kb.shape[2]
    qb = q.reshape(B, nb, A_BLOCK, A_KV_HEADS, G, HEAD_DIM)
    mask = jnp.asarray(_band_mask(S))[:, None, None]
    s_loc = jnp.einsum('bnqkgd,bnjkd->bnkgqj', qb, kb).astype(jnp.float32) * scale
    s_loc = jnp.where(mask, s_loc, -jnp.inf)
    s_ctx = jnp.einsum('bnqkgd,bjkd->bnkgqj', qb, k_ctx).astype(jnp.float32) * scale
    sink_col = jnp.broadcast_to(sink.astype(jnp.float32).reshape(1, 1, A_KV_HEADS, G, 1, 1),
                                s_loc.shape[:-1] + (1,))
    p = jax.nn.softmax(jnp.concatenate([s_loc, s_ctx, sink_col], axis=-1), axis=-1)
    L = k_ctx.shape[1]
    p_loc = p[..., :span].astype(v.dtype)
    p_ctx = p[..., span:span + L].astype(v.dtype)
    o = (jnp.einsum('bnkgqj,bnjkd->bnqkgd', p_loc, vb)
         + jnp.einsum('bnkgqj,bjkd->bnqkgd', p_ctx, v_ctx))
    return o.reshape(B, S, A_WIDTH)

def _na_pattern(rows):
    kh = min(NA_MAX_KH, rows)
    n_blk = rows // NA_ROW_BLOCK
    n_kr = min(NA_ROW_BLOCK + kh - 1, rows)
    r0 = np.arange(n_blk) * NA_ROW_BLOCK
    row_start = lambda r: np.clip(r - kh // 2, 0, rows - kh)
    k_start = np.minimum(row_start(r0), rows - n_kr)
    key_rows = k_start[:, None] + np.arange(n_kr)[None, :]
    qi = np.arange(NA_ROW_BLOCK * GRID_W)
    q_r = r0[:, None] + qi[None, :] // GRID_W
    q_c = qi % GRID_W
    kj = np.arange(n_kr * GRID_W)
    k_r = key_rows[:, kj // GRID_W]
    k_c = kj % GRID_W
    rs = row_start(q_r)
    cs = np.clip(q_c - NA_KW // 2, 0, GRID_W - NA_KW)
    row_ok = (k_r[:, None, :] >= rs[:, :, None]) & (k_r[:, None, :] < rs[:, :, None] + kh)
    col_ok = (k_c[None, :] >= cs[:, None]) & (k_c[None, :] < cs[:, None] + NA_KW)
    mask = row_ok & col_ok[None]
    dr = np.clip(k_r[:, None, :] - q_r[:, :, None] + NA_MAX_KH - 1, 0, 2 * NA_MAX_KH - 2)
    dc = np.broadcast_to(np.clip(k_c[None, :] - q_c[:, None] + NA_KW - 1, 0, 2 * NA_KW - 2)[None],
                         mask.shape)
    return key_rows, mask, dr, dc

def _neighbourhood_latent(q, k, v, k_ctx, v_ctx, rpb):
    B, S = q.shape[:2]
    rows = S // GRID_W
    key_rows, mask, dr, dc = _na_pattern(rows)
    n_blk, n_kr = key_rows.shape
    scale = HEAD_DIM ** -0.5
    idx = jnp.asarray(key_rows)
    kg = k.reshape(B, rows, GRID_W, B_HEADS, HEAD_DIM)[:, idx].reshape(
        B, n_blk, n_kr * GRID_W, B_HEADS, HEAD_DIM)
    vg = v.reshape(B, rows, GRID_W, B_HEADS, HEAD_DIM)[:, idx].reshape(
        B, n_blk, n_kr * GRID_W, B_HEADS, HEAD_DIM)
    qb = q.reshape(B, n_blk, NA_ROW_BLOCK * GRID_W, B_HEADS, HEAD_DIM)
    bias = jnp.transpose(rpb[:, jnp.asarray(dr), jnp.asarray(dc)], (1, 0, 2, 3)).astype(jnp.float32)
    s_loc = jnp.einsum('bnqhd,bnjhd->bnhqj', qb, kg).astype(jnp.float32) * scale + bias
    s_loc = jnp.where(jnp.asarray(mask)[:, None], s_loc, -jnp.inf)
    s_ctx = jnp.einsum('bnqhd,bjhd->bnhqj', qb, k_ctx).astype(jnp.float32) * scale
    p = jax.nn.softmax(jnp.concatenate([s_loc, s_ctx], axis=-1), axis=-1)
    kb_len = kg.shape[2]
    p_loc = p[..., :kb_len].astype(v.dtype)
    p_ctx = p[..., kb_len:].astype(v.dtype)
    o = (jnp.einsum('bnhqj,bnjhd->bnqhd', p_loc, vg)
         + jnp.einsum('bnhqj,bjhd->bnqhd', p_ctx, v_ctx))
    return o.reshape(B, S, B_WIDTH)

def _ctx_self_attention(q, k, v, n_kv, sink=None):
    B, L, H, _ = q.shape
    G = H // n_kv
    qg = q.reshape(B, L, n_kv, G, HEAD_DIM)
    s = jnp.einsum('blkgd,bjkd->bkglj', qg, k).astype(jnp.float32) * HEAD_DIM ** -0.5
    if sink is not None:
        sink_col = jnp.broadcast_to(sink.astype(jnp.float32).reshape(1, n_kv, G, 1, 1), s.shape[:-1] + (1,))
        s = jnp.concatenate([s, sink_col], axis=-1)
    p = jax.nn.softmax(s, axis=-1)[..., :L].astype(v.dtype)
    o = jnp.einsum('bkglj,bjkd->blkgd', p, v)
    return o.reshape(B, L, H * HEAD_DIM)

def _merge(o_a, o_b, g_a, g_b, w_out):
    return jnp.concatenate([_rms_norm(o_a, g_a), _rms_norm(o_b, g_b)], axis=-1) @ w_out

def _swiglu(h, w_gate, w_up, w_down):
    return (jax.nn.silu(h @ w_gate) * (h @ w_up)) @ w_down

def first_inputs(seed: int = 0) -> dict:
    key = jax.random.key(seed)
    ks = jax.random.split(key, 24)
    nrm = lambda k, shape: jax.random.normal(k, shape, dtype=jnp.float32)
    gain = lambda k, shape: 1.0 + 0.05 * nrm(k, shape)
    D = D_MODEL
    return {
        "x": nrm(ks[0], (BATCH, SEQ, D)),
        "c": nrm(ks[1], (BATCH, D)),
        "ctx": nrm(ks[2], (BATCH, CTX_LEN, D)),
        "c_ctx": nrm(ks[3], (D,)),
        "w_mod": nrm(ks[4], (DEPTH, D, N_MOD * D)) * (0.5 * D ** -0.5),
        "b_mod": 0.01 * nrm(ks[5], (DEPTH, N_MOD * D)),
        "norm1_g": gain(ks[6], (DEPTH, D)),
        "w_in": nrm(ks[7], (DEPTH, D, IN_COLS)) * D ** -0.5,
        "qn_a": gain(ks[8], (DEPTH, HEAD_DIM)),
        "kn_a": gain(ks[9], (DEPTH, HEAD_DIM)),
        "sink_a": 0.5 * nrm(ks[10], (DEPTH, A_HEADS)),
        "qn_b": gain(ks[11], (DEPTH, HEAD_DIM)),
        "kn_b": gain(ks[12], (DEPTH, HEAD_DIM)),
        "rpb_b": 0.1 * nrm(ks[13], (DEPTH, B_HEADS, 2 * NA_MAX_KH - 1, 2 * NA_KW - 1)),
        "on_a": gain(ks[14], (DEPTH, A_WIDTH)),
        "on_b": gain(ks[15], (DEPTH, B_WIDTH)),
        "w_out": nrm(ks[16], (DEPTH, MIX_WIDTH, D)) * MIX_WIDTH ** -0.5,
        "norm2_g": gain(ks[17], (DEPTH, D)),
        "w_gate": nrm(ks[18], (DEPTH, D, FFN_HIDDEN)) * D ** -0.5,
        "w_up": nrm(ks[19], (DEPTH, D, FFN_HIDDEN)) * D ** -0.5,
        "w_down": nrm(ks[20], (DEPTH, FFN_HIDDEN, D)) * FFN_HIDDEN ** -0.5,
    }

def first_block(x, c, ctx, c_ctx, w_mod, b_mod, norm1_g, w_in, qn_a, kn_a, sink_a, qn_b, kn_b,
              rpb_b, on_a, on_b, w_out, norm2_g, w_gate, w_up, w_down):
    S = x.shape[1]
    t = jnp.arange(S)
    row_pos = t // GRID_W
    col_pos = t % GRID_W
    for l in range(DEPTH):
        mod = (jax.nn.silu(c) @ w_mod[l] + b_mod[l])[:, None, :]
        mod_c = (jax.nn.silu(c_ctx) @ w_mod[l] + b_mod[l])[None, None, :]
        sh1, sc1, g1, sh2, sc2, g2 = jnp.split(mod, N_MOD, axis=-1)
        csh1, csc1, cg1, csh2, csc2, cg2 = jnp.split(mod_c, N_MOD, axis=-1)

        h = _modulate(_rms_norm(x, norm1_g[l]), sh1, sc1)
        hc = _modulate(_rms_norm(ctx, norm1_g[l]), csh1, csc1)
        q_a, k_a, v_a, q_b, k_b, v_b = _in_proj(h, w_in[l])
        q_ac, k_ac, v_ac, q_bc, k_bc, v_bc = _in_proj(hc, w_in[l])

        q_a = _axial_rope(_rms_norm(q_a, qn_a[l]), row_pos, col_pos)
        k_a = _axial_rope(_rms_norm(k_a, kn_a[l]), row_pos, col_pos)
        q_ac, k_ac = _rms_norm(q_ac, qn_a[l]), _rms_norm(k_ac, kn_a[l])
        q_b, k_b = _rms_norm(q_b, qn_b[l]), _rms_norm(k_b, kn_b[l])
        q_bc, k_bc = _rms_norm(q_bc, qn_b[l]), _rms_norm(k_bc, kn_b[l])

        o_a = _window_gqa_latent(q_a, k_a, v_a, k_ac, v_ac, sink_a[l])
        o_b = _neighbourhood_latent(q_b, k_b, v_b, k_bc, v_bc, rpb_b[l])
        x_new = x + g1 * _merge(o_a, o_b, on_a[l], on_b[l], w_out[l])
        h2 = _modulate(_rms_norm(x_new, norm2_g[l]), sh2, sc2)
        x_new = x_new + g2 * _swiglu(h2, w_gate[l], w_up[l], w_down[l])

        if l < DEPTH - 1:
            o_ac = _ctx_self_attention(q_ac, k_ac, v_ac, A_KV_HEADS, sink_a[l])
            o_bc = _ctx_self_attention(q_bc, k_bc, v_bc, B_HEADS)
            ctx = ctx + cg1 * _merge(o_ac, o_bc, on_a[l], on_b[l], w_out[l])
            hc2 = _modulate(_rms_norm(ctx, norm2_g[l]), csh2, csc2)
            ctx = ctx + cg2 * _swiglu(hc2, w_gate[l], w_up[l], w_down[l])
        x = x_new
    return x


CHUNK = 64
D_MIX = D_MODEL
D_A = D_MIX // 2
D_B = D_MIX - D_A
A_HEADS_2 = 4
A_HEAD_DIM = D_A // A_HEADS_2
B_HEADS_2 = 4
B_DK = D_B // 2
B_DV = D_B
B_HEAD_K = B_DK // B_HEADS_2
B_HEAD_V = B_DV // B_HEADS_2
B_GATE_RANK = 16
B_GATE_TAU = 16.0
D_FF = 4 * D_MODEL
D_IN = 2 * D_A + 2 * B_DK + 2 * B_DV + B_GATE_RANK


def rmsnorm(x, g):
    xf = x.astype(jnp.float32)
    xf = xf * lax.rsqrt(jnp.mean(xf * xf, axis=-1, keepdims=True) + EPS)
    return (xf * g.astype(jnp.float32)).astype(x.dtype)

def layernorm(x, g, b):
    xf = x.astype(jnp.float32)
    mu = jnp.mean(xf, axis=-1, keepdims=True)
    xc = xf - mu
    xf = xc * lax.rsqrt(jnp.mean(xc * xc, axis=-1, keepdims=True) + EPS)
    return (xf * g.astype(jnp.float32) + b.astype(jnp.float32)).astype(x.dtype)

def gmlp_mixer(zu, zv, ln_g, ln_b, ws, bs, out_g):
    bsz, s, _ = zu.shape
    u = jax.nn.gelu(zu)
    v = layernorm(jax.nn.gelu(zv), ln_g, ln_b)
    n_blk = s // A_BLOCK
    v = v.reshape(bsz, n_blk, A_BLOCK, A_HEADS_2, A_HEAD_DIM)
    pos = jnp.arange(A_BLOCK) // CHUNK
    mask = pos[:, None] >= pos[None, :]
    w = jnp.where(mask[None], ws, jnp.zeros_like(ws))
    mixed = jnp.einsum('hij,bnjhc->bnihc', w, v) + jnp.transpose(bs)[None, None, :, :, None]
    out = u * mixed.reshape(bsz, s, D_A)
    return rmsnorm(out, out_g)

def gla_mixer(zq, zk, zv, zg, zlr, gate_w, gate_b, out_g):
    dt = zq.dtype
    bsz, s, _ = zq.shape
    n_c = s // CHUNK
    f32 = jnp.float32
    q = zq.astype(f32) * (B_HEAD_K ** -0.5)
    k = zk.astype(f32)
    v = zv.astype(f32)
    log_a = jax.nn.log_sigmoid(zlr.astype(f32) @ gate_w.astype(f32) + gate_b.astype(f32)) / B_GATE_TAU

    def to_chunks(t, d):
        return jnp.transpose(t.reshape(bsz, n_c, CHUNK, B_HEADS_2, d), (0, 3, 1, 2, 4))

    q, k, log_a = to_chunks(q, B_HEAD_K), to_chunks(k, B_HEAD_K), to_chunks(log_a, B_HEAD_K)
    v = to_chunks(v, B_HEAD_V)
    cum = jnp.cumsum(log_a, axis=-2)
    last = cum[..., -1:, :]
    qe = q * jnp.exp(cum)
    ke = k * jnp.exp(-cum)
    kd = k * jnp.exp(last - cum)

    tril = jnp.tril(jnp.ones((CHUNK, CHUNK), dtype=bool))
    scores = jnp.einsum('bhnid,bhnjd->bhnij', qe, ke)
    scores = jnp.where(tril, scores, 0.0)
    o_intra = jnp.einsum('bhnij,bhnjv->bhniv', scores, v)

    upd = jnp.einsum('bhnjd,bhnjv->bhndv', kd, v)
    dec = jnp.exp(last[..., 0, :])

    def step(state, inp):
        d_c, u_c = inp
        return d_c[..., None] * state + u_c, state

    s0 = jnp.zeros((bsz, B_HEADS_2, B_HEAD_K, B_HEAD_V), f32)
    _, s_prev = lax.scan(step, s0, (jnp.moveaxis(dec, 2, 0), jnp.moveaxis(upd, 2, 0)))
    s_prev = jnp.moveaxis(s_prev, 0, 2)
    o_inter = jnp.einsum('bhnid,bhndv->bhniv', qe, s_prev)

    o = jnp.transpose(o_intra + o_inter, (0, 2, 3, 1, 4))
    o = o.reshape(bsz, s, B_HEADS_2, B_HEAD_V)
    o = rmsnorm(o, out_g.reshape(B_HEADS_2, B_HEAD_V)).reshape(bsz, s, B_DV)
    return (o * jax.nn.silu(zg.astype(f32))).astype(dt)

def second_inputs(seed: int = 0) -> dict:
    key = jax.random.key(seed)
    ks = jax.random.split(key, 20)
    n = jax.random.normal

    def gain(k, d):
        return 1.0 + 0.05 * n(k, (DEPTH, d), jnp.float32)

    return {
        "x": n(ks[0], (BATCH, SEQ, D_MODEL), jnp.float32),
        "pre_mix_g": gain(ks[1], D_MODEL),
        "w_in": n(ks[2], (DEPTH, D_MODEL, D_IN), jnp.float32) * D_MODEL ** -0.5,
        "gmlp_ln_g": gain(ks[3], D_A),
        "gmlp_ln_b": 0.02 * n(ks[4], (DEPTH, D_A), jnp.float32),
        "gmlp_ws": n(ks[5], (DEPTH, A_HEADS_2, A_BLOCK, A_BLOCK), jnp.float32) * A_BLOCK ** -0.5,
        "gmlp_bs": 1.0 + 0.1 * n(ks[6], (DEPTH, A_HEADS_2, A_BLOCK), jnp.float32),
        "gmlp_out_g": gain(ks[7], D_A),
        "gla_gate_w": n(ks[8], (DEPTH, B_GATE_RANK, B_DK), jnp.float32) * B_GATE_RANK ** -0.5,
        "gla_gate_b": 0.5 * n(ks[9], (DEPTH, B_DK), jnp.float32),
        "gla_out_g": gain(ks[10], B_DV),
        "w_out": n(ks[11], (DEPTH, D_MIX, D_MODEL), jnp.float32) * D_MIX ** -0.5,
        "post_mix_g": gain(ks[12], D_MODEL),
        "pre_ff_g": gain(ks[13], D_MODEL),
        "w_ff1": n(ks[14], (DEPTH, D_MODEL, D_FF), jnp.float32) * D_MODEL ** -0.5,
        "w_ff2": n(ks[15], (DEPTH, D_FF, D_MODEL), jnp.float32) * D_FF ** -0.5,
        "post_ff_g": gain(ks[16], D_MODEL),
    }

def second_block(x, pre_mix_g, w_in, gmlp_ln_g, gmlp_ln_b, gmlp_ws, gmlp_bs, gmlp_out_g,
              gla_gate_w, gla_gate_b, gla_out_g, w_out, post_mix_g, pre_ff_g,
              w_ff1, w_ff2, post_ff_g):
    cuts = [D_A, 2 * D_A, 2 * D_A + B_DK, 2 * D_A + 2 * B_DK,
            2 * D_A + 2 * B_DK + B_DV, 2 * D_A + 2 * B_DK + 2 * B_DV]
    h = x
    for l in range(DEPTH):
        y = rmsnorm(h, pre_mix_g[l])
        z = y @ w_in[l]
        zu, zv, zq, zk, zvb, zg, zlr = jnp.split(z, cuts, axis=-1)
        a = gmlp_mixer(zu, zv, gmlp_ln_g[l], gmlp_ln_b[l], gmlp_ws[l], gmlp_bs[l], gmlp_out_g[l])
        b = gla_mixer(zq, zk, zvb, zg, zlr, gla_gate_w[l], gla_gate_b[l], gla_out_g[l])
        m = jnp.concatenate([a, b], axis=-1) @ w_out[l]
        h = h + rmsnorm(m, post_mix_g[l])
        f = rmsnorm(h, pre_ff_g[l]) @ w_ff1[l]
        f = jnp.square(jax.nn.relu(f)) @ w_ff2[l]
        h = h + rmsnorm(f, post_ff_g[l])
    return h


def setup_inputs(seed=0):
    out = dict(first_inputs(seed))
    for name, value in second_inputs(seed + 1).items():
        if name != "x":
            out[name + "_2"] = value
    return out


def reference(
    x, c, ctx, c_ctx, w_mod, b_mod, norm1_g, w_in, qn_a, kn_a, sink_a, qn_b, kn_b, rpb_b, on_a,
    on_b, w_out, norm2_g, w_gate, w_up, w_down, pre_mix_g_2, w_in_2, gmlp_ln_g_2, gmlp_ln_b_2,
    gmlp_ws_2, gmlp_bs_2, gmlp_out_g_2, gla_gate_w_2, gla_gate_b_2, gla_out_g_2, w_out_2,
    post_mix_g_2, pre_ff_g_2, w_ff1_2, w_ff2_2, post_ff_g_2,
):
    x = first_block(
        x, c, ctx, c_ctx, w_mod, b_mod, norm1_g, w_in, qn_a, kn_a, sink_a, qn_b, kn_b, rpb_b,
        on_a, on_b, w_out, norm2_g, w_gate, w_up, w_down,
    )
    return second_block(
        x, pre_mix_g_2, w_in_2, gmlp_ln_g_2, gmlp_ln_b_2, gmlp_ws_2, gmlp_bs_2, gmlp_out_g_2,
        gla_gate_w_2, gla_gate_b_2, gla_out_g_2, w_out_2, post_mix_g_2, pre_ff_g_2, w_ff1_2,
        w_ff2_2, post_ff_g_2,
    )


_drawn_inputs = setup_inputs


def setup_inputs(seed=0):
    import zlib

    import numpy as np

    out = dict(_drawn_inputs(seed))
    spreads = {}
    factors = {'norm1_g': 4.218,
     'qn_a': 8.0,
     'kn_a': 8.0,
     'sink_a': 8.0,
     'qn_b': 8.0,
     'kn_b': 8.0,
     'rpb_b': 8.0,
     'on_a': 3.521,
     'on_b': 3.519,
     'norm2_g': 2.826,
     'gmlp_ln_g_2': 19.262,
     'gmlp_ln_b_2': 45.446,
     'gla_out_g_2': 10.122,
     'gmlp_bs_2': 8.0,
     'gmlp_out_g_2': 6.361,
     'post_mix_g_2': 2.957,
     'pre_ff_g_2': 2.773,
     'post_ff_g_2': 3.1}
    for name, (base, spread) in spreads.items():
        noise = np.random.default_rng([zlib.crc32(name.encode()), seed]).standard_normal(out[name].shape)
        drawn = base * np.exp(spread * noise) if base else spread * noise
        out[name] = __import__('jax').numpy.asarray(drawn.astype(out[name].dtype))
    for name, factor in factors.items():
        out[name] = (out[name] * factor).astype(out[name].dtype)
    return out
```

```python
from contextlib import ExitStack

import numpy as np

import concourse.bass as bass
from concourse import mybir

F32 = mybir.dt.float32
F32R = mybir.dt.float32r
ALU = mybir.AluOpType
ACT = mybir.ActivationFunctionType
AX_X = mybir.AxisListType.X
ds = bass.ds

P = 128
D = 1024
S = 1024
CTX = 256
NT = S // P
NC = CTX // P
KT = D // P
HD = 64
A_KV = 128
AW = 512
KVW = A_KV + AW
GRID = 64
PN = 256
F1 = 2816
F2 = 4096
CH1, CH2 = F1 // PN, F2 // PN
EPS = 1e-6
BIG = 1e30
PAIRS = 4
RB = 31
NE = 14
NI = 9
RPW = (NE - 1) * RB + GRID
RPH = 15 * RB
RPAD = 64


def bcast(ap, axis, n):
    shape = list(ap.shape)
    return ap.unsqueeze(axis).broadcast_to(shape[:axis] + [n] + shape[axis:])


def program(nc, t, out):
    BASE, TOP = 16512, 229344
    place = [BASE]

    def at(name, shape, dt, offset):
        return nc.alloc_sbuf_tensor_at(name, [P] + shape, dt, offset=offset)

    def region(size):
        offset = place[0]
        place[0] += (size + 31) // 32 * 32
        assert place[0] <= TOP, (place[0], TOP)
        return offset

    def fixed(name, shape, dt=F32):
        n = 4
        for x in shape:
            n *= x
        return at(name, shape, dt, region(n))

    ident = fixed("ident", [P])
    pick_x = fixed("pick_x", [P])
    pick_c = fixed("pick_c", [P])
    head_gain = fixed("head_gain", [4, HD])
    neg_sink = fixed("neg_sink", [8])
    row_mask = fixed("row_mask", [NI])
    col_mask = fixed("col_mask", [GRID])
    neg_half = fixed("neg_half", [40])
    cond = fixed("cond", [2, KT])
    sumsq = fixed("sumsq", [16])
    msq = fixed("msq", [16])
    rstd = fixed("rstd", [16])
    junk = at("junk", [D], mybir.dt.bfloat16, region(2 * D))
    hsum = fixed("hsum", [10, 4])
    hms = fixed("hms", [10, 4])
    hrs = fixed("hrs", [10, 4])
    rope_at = place[0]
    rope = fixed("rope", [2, NT, HD])
    mod_b = fixed("mod_b", [PN])
    zero_row = fixed("zero_row", [RPAD])
    ring = region(40 * 1024)
    ht = region(64 * 1024)
    nat = region(4 * (NT * D + 2 * 10 * KVW))
    xnr = region(2 * D * 4)

    stage = at("stage", [2048], F32, ring)
    w_hi = at("w_hi", [2, 2048], F32R, ring + 8192)
    w_lo = at("w_lo", [2, 2048], F32R, ring + 8192 * 3)
    ht_hi = at("ht_hi", [KT, S], F32R, ht)
    ht_lo = at("ht_lo", [KT, S], F32R, ht + 32768)
    mod_w = at("mod_w", [8, 2048], F32, ht)
    xn = at("xn", [2, D], F32, xnr)
    rot = at("rot", [4, PN], F32, xnr)
    hsq = at("hsq", [2, PN], F32, xnr + 4096)
    mod_q = at("mod_q", [PN], F32, xnr + 6144)
    mod_row = at("mod_row", [PN], F32, xnr + 7168)
    mod_part = at("mod_part", [2, PN], F32, xnr)
    q_nat = at("q_nat", [NT, D], F32, nat)
    k_off = nat + NT * D * 4
    v_off = k_off + 10 * KVW * 4
    k_nat = at("k_nat", [10, KVW], F32, k_off)
    v_nat = at("v_nat", [10, KVW], F32, v_off)
    mod_1 = at("mod_1", [4, D], F32, k_off)
    norm1 = at("norm1", [D], F32, v_off)
    ctx_in = at("ctx_in", [NC, D], F32, v_off + 4096)
    shift_x, gain_x, shift_c, gain_c = (mod_1[:, j, :] for j in range(4))
    kt = at("kt", [10, S + CTX], F32R, ht)
    probs = at("probs", [2, CTX + NI * GRID], F32, ring)
    prob_t = [at("prob_t0", [2, 7 * P], F32, ring + 6656), at("prob_t1", [2, 7 * P], F32, xnr)]
    masked = at("masked", [2, NI * GRID], F32, ring + 13824)
    edge = at("edge", [2, NE, GRID], F32, ring + 18432)
    inner = at("inner", [2, NI, GRID], F32, ring + 25600)
    o_t = at("o_t", [P], F32, ring + 30208)
    band = at("band", [3, P], F32, ring + 30720)
    small = at("small", [2, 8], F32, ring + 32256)
    v_pair = at("v_pair", [10, P], F32, ring + 32320)
    den = at("den", [2, 2, 4], F32, ring + 37440)
    dsum = at("dsum", [2], F32, ring + 37504)
    rden = at("rden", [2, 2], F32, ring + 37536)
    q_split = at("q_split", [2, 2, 2, P], F32, ht + 51200)
    q_t = at("q_t", [2, 2, 2, P], F32R, ht + 55296)
    k_split = at("k_split", [2, 10, P], F32, ring)
    raw_bias = at("raw_bias", [8, RPW], F32, k_off)
    x_again = at("x_again", [2, NT, PN], F32, k_off)
    mod_2 = at("mod_2", [4, D], F32, k_off + 16384)
    on_ab = at("on_ab", [D], F32, k_off + 32768)
    norm2 = at("norm2", [D], F32, k_off + 36864)
    silu = at("silu", [2, S], F32, k_off)
    act_f = at("act_f", [2, S], F32, k_off + 8192)
    act_hi = at("act_hi", [2, S], F32R, k_off + 32768)
    act_lo = at("act_lo", [2, S], F32R, k_off + 32768 + 8192)

    rpb_pad = nc.dram_tensor("rpb_pad", [RPAD + 8 * RPH + RPAD], F32, kind="Internal").ap()
    RPL = RPAD + 8 * RPH + RPAD
    rpb_skew = nc.dram_tensor("rpb_skew", [GRID * (RPL + 1)], F32, kind="Internal").ap()
    mod_dram = nc.dram_tensor("mod_dram", [4, D], F32, kind="Internal").ap()

    ctx = ExitStack()
    with ctx:
        ps = ctx.enter_context(nc.psum_tensor("ps", [P, 8, 512], F32))

        def sem(name):
            return ctx.enter_context(nc.semaphore(name))

        consts_in = sem("consts_in")
        mod1_in = sem("mod1_in")
        modw_in = [sem(f"modw_in{j}") for j in range(8)]
        ctx_landed = sem("ctx_landed")
        x_in = [sem(f"x_in{j}") for j in range(NT)]
        cond_in, pe_consts_in = sem("cond_in"), sem("pe_consts_in")
        banks_clear = sem("banks_clear")
        ready = sem("ready")
        cond_done = sem("cond_done")
        part_done, part_evac, mod_done, mod_added = sem("part_done"), sem("part_evac"), sem("mod_done"), sem("mod_added")
        w_landed, w_hi_done, w_lo_done = sem("w_landed"), sem("w_hi_done"), sem("w_lo_done")
        ss_done, ms_done, rs_done = sem("ss_done"), sem("ms_done"), sem("rs_done")
        xs_done = sem("xs_done")
        xn_done, tr_done, th_done, tl_done = sem("xn_done"), sem("tr_done"), sem("th_done"), sem("tl_done")
        dense_done, dense_evac = sem("dense_done"), sem("dense_evac")
        hsum_done, hms_done, hrs_done = sem("hsum_done"), sem("hms_done"), sem("hrs_done")
        modb_in, neg_done = sem("modb_in"), sem("neg_done")
        hn_done, hg_done, roped = sem("hn_done"), sem("hg_done"), sem("roped")
        skewed, pad_done, bias_in = sem("skewed"), sem("pad_done"), sem("bias_in")
        mod2_landed, modx_part, modx_q, modx_row, modx_b, modx_out, modx_stored = (
            sem(x) for x in ("mod2_landed", "modx_part", "modx_q", "modx_row", "modx_b", "modx_out", "modx_stored"))
        ks_hi, ks_lo, kt_tr, kt_a, kt_v = sem("ks_hi"), sem("ks_lo"), sem("kt_tr"), sem("kt_a"), sem("kt_v")
        band_in = sem("band_in")
        (qs_step, qt_done, qt_ready, s_done, mn_step, min_done, exp_done, pt0_done, pt1_done, pt0_evac, pt1_evac, vp_ready,
         pv_done, ot_evac, on_done, on_evac, dn_step, tab_done) = (sem(x) for x in (
             "qs_step", "qt_done", "qt_ready", "s_done", "mn_step", "min_done", "exp_done", "pt0_done", "pt1_done",
             "pt0_evac", "pt1_evac", "vp_ready", "pv_done", "ot_evac", "on_done", "on_evac", "dn_step", "tab_done"))

        P_C, P_X, P_O = 0, 5, 14
        P_F = 18
        P_Z = P_F + 3 * CH1
        P_M = P_Z + 10
        P_G = P_M + 4
        P_END = P_G + 2 * CH2
        T_C, T_X, T_O, T_H, T_Z, T_M, T_G, T_E = 0, 2, 10, 18, 26, 34, 42, 50

        def panel_of(w, col):
            return w[0].rearrange("(k p) n -> p k n", p=P)[:, :, col:col + PN] if isinstance(col, int) else \
                w[0].rearrange("(k p) n -> p k n", p=P)[:, :, ds(col, PN)]

        def stage_up():
            return stage[:, :].rearrange("p (k n) -> p k n", k=KT)

        CTX_COLS = [512, 1280, 1536, 1792, 2048]

        done = ExitStack()
        block = done.enter_context(nc.Block())

        def load_weights(sp, p, source, dst=None):
            if not isinstance(p, int) or p > 0:
                sp.wait_ge(w_lo_done, p)
            sp.dma_start(stage_up() if dst is None else dst, source).then_inc(w_landed, 16)

        def mod_panel(m):
            return t["w_mod"][0].rearrange("(p k) n -> p k n", k=KT)[:, :, 2 * D + m * PN:2 * D + (m + 1) * PN]

        def mod_flat(m):
            return mod_dram.rearrange("a b -> (a b)")[m * PN:(m + 1) * PN].unsqueeze(0)

        def sync_x(sp):
            for p in range(8):
                for m in (2 * p, 2 * p + 1):
                    if m == 2 * p:
                        sp.wait_ge(w_lo_done, P_X + p + 2)
                    else:
                        sp.wait_ge(modx_part, m)
                    sp.dma_start(stage_up(), mod_panel(m)).then_inc(mod2_landed, 16)
                    if m:
                        sp.wait_ge(modx_row, m)
                        sp.dma_start(mod_flat(m - 1), mod_row[0:1, :]).then_inc(modx_stored, 16)
                    sp.dma_start(mod_b[0:1, :], t["b_mod"][0:1, 2 * D + m * PN:2 * D + (m + 1) * PN]).then_inc(modb_in, 16)
                if p < 7:
                    sp.wait_ge(modx_part, 2 * p + 2)
                    sp.dma_start(stage_up(), panel_of(t["w_in"], (p + 2) * PN)).then_inc(w_landed, 16)
            sp.wait_ge(modx_row, 16)
            sp.dma_start(mod_flat(15), mod_row[0:1, :]).then_inc(modx_stored, 16)

        def norm_pool(pool, n, before, width, groups=1):
            h = (n + 1) // 2
            for g in range(2):
                a, b = g * h, g * h + h
                calls = 2 * STAGE_OF[before] + g
                pool.wait_ge(ss_done, before + b)
                if calls == 0:
                    pool.wait_ge(ready, 1)
                if calls > 0:
                    pool.wait_ge(rs_done, calls)
                pa, pb = groups * a, groups * b
                pool.tensor_scalar(msq[:, pa:pb], sumsq[:, pa:pb], 1.0 / width, EPS, ALU.mult, ALU.add).then_inc(ms_done, 1)
                pool.wait_ge(ms_done, calls + 1)
                pool.wait_ge(xn_done, before)
                pool.tensor_tensor(rstd[:, pa:pb], msq[:, pa:pb], neg_half[:, pa:pb], ALU.pow).then_inc(rs_done, 1)

        STAGE_OF = {T_C: 0, T_X: 1, T_O: 2, T_H: 3, T_Z: 4, T_M: 5, T_G: 6, T_E: 7}

        def norm_sums(act, n, before, source, wait):
            for j in range(n):
                wait(act, j)
                if before + j:
                    act.wait_ge(ss_done, before + j)
                if j == 0 and before:
                    act.wait_ge(ms_done, 2 * STAGE_OF[before])
                act.activation(junk[:, :], source(j), ACT.Square, accum_out=sumsq[:, j:j + 1]).then_inc(ss_done, 1)

        def turn_act(act, n, before, used):
            if used is not None:
                act.wait_ge(*panel_used(used))
            with act.Fori(0, n // 2) as i:
                for b in range(2):
                    j = 2 * i + b
                    act.wait_ge(tr_done, before + 1)
                    act.wait_ge(tr_done, before + j + 1)
                    act.activation(ht_hi[:, :, ds(j * P, P)], turned(b), ACT.Copy).then_inc(th_done, 1)

        def turned(b):
            return ps[:, 4 + 2 * b:6 + 2 * b, :].rearrange("p a (k n) -> p (a k) n", n=P)

        def turn_pe(pe, n, before):
            with pe.Fori(0, n // 2) as i:
                for b in range(2):
                    j = 2 * i + b
                    pe.wait_ge(xn_done, before + j + 1)
                    if before:
                        pe.wait_ge(tl_done, before + j - 1)
                    elif b == 0:
                        pe.wait_ge(mod_added, 16)
                    for k in range(KT):
                        mm = pe.transpose(ps[:, 4 + 2 * b + k // 4, (k % 4) * P:(k % 4 + 1) * P],
                                          xn[:, b, k * P:(k + 1) * P], ident[:, :])
                    mm.then_inc(tr_done, 1)

        def turn_dve(dve, n, before, source, gain, shift=None, shifts=0):
            with dve.Fori(0, n // 2) as i:
                for b in range(2):
                    j = 2 * i + b
                    dve.wait_ge(rs_done, 2 * STAGE_OF[before] + 2)
                    if before:
                        dve.wait_ge(tr_done, before + j - 1)
                    last = dve.scalar_tensor_tensor(out=xn[:, b, :], in0=source(j), scalar=rstd[:, ds(j, 1)],
                                                    in1=gain, op0=ALU.mult, op1=ALU.mult)
                    if shift is not None:
                        last.then_inc(xs_done, 1)
                        dve.wait_ge(xs_done, shifts + j + 1)
                        last = dve.tensor_tensor(xn[:, b, :], xn[:, b, :], shift, ALU.add)
                    last.then_inc(xn_done, 1)
                for b in range(2):
                    j = 2 * i + b
                    dve.wait_ge(th_done, before + j + 1)
                    dve.tensor_tensor(ht_lo[:, :, ds(j * P, P)], turned(b),
                                      ht_hi[:, :, ds(j * P, P)].bitcast(F32), ALU.subtract).then_inc(tl_done, 1)

        def panel_used(p):
            if p < P_X:
                return dense_done, NC * (p + 1)
            if p < P_O:
                return dense_done, D_X + NT * (p - P_X + 1)
            if p < P_F:
                return dense_done, D_O + NT * (p - P_O + 1)
            return later_used(p)

        def split_hi(act, p, slot, used=None, scaled=None):
            act.wait_ge(w_landed, 16 * (p + 1))
            if used is None and p >= 2:
                used = panel_used(p - 2)
            if used is not None:
                act.wait_ge(*used)
            if scaled is not None:
                act.wait_ge(w_scaled, scaled)
            act.activation(w_hi[:, slot, :], stage[:, :], ACT.Copy).then_inc(w_hi_done, 1)

        def split_lo(dve, p, slot):
            dve.wait_ge(w_hi_done, p + 1)
            dve.tensor_tensor(w_lo[:, slot, :], stage[:, :], w_hi[:, slot, :].bitcast(F32), ALU.subtract).then_inc(w_lo_done, 1)

        def rows_pe(pe, p, slot, tiles, tiles_before, d0, lag=4):
            pe.wait_ge(w_lo_done, p + 1)
            wh, wl = (w[:, slot, :].rearrange("p (k n) -> p k n", k=KT) for w in (w_hi, w_lo))
            for j in range(tiles):
                pe.wait_ge(tl_done, tiles_before + j + 1)
                if not isinstance(d0, int) or d0 + j >= lag:
                    pe.wait_ge(dense_evac, d0 + j + 1 - lag)
                bank = bank_of(j)
                for k in range(KT):
                    a, b = ht_hi[:, k, j * P:(j + 1) * P], ht_lo[:, k, j * P:(j + 1) * P]
                    pe.matmul(bank, a, wh[:, k, :], start=(k == 0), stop=False)
                    pe.matmul(bank, a, wl[:, k, :], start=False, stop=False)
                    mm = pe.matmul(bank, b, wh[:, k, :], start=False, stop=(k == KT - 1))
                mm.then_inc(dense_done, 1)
                yield j

        def bank_of(j):
            return ps[:, j % 4, 0:PN]

        X_PANELS = [("q", 0, PN, 0, True), ("q", PN, PN, 0, True), ("k", 0, A_KV, 1, True),
                    ("q", AW, PN, 2, False), ("q", AW + PN, PN, 2, False),
                    ("k", A_KV, PN, 3, False), ("k", A_KV + PN, PN, 3, False),
                    ("v", A_KV, PN, None, False), ("v", A_KV + PN, PN, None, False)]
        C_PANELS = [("k", 0, A_KV, 1, False), ("k", A_KV, PN, 3, False), ("k", A_KV + PN, PN, 3, False),
                    ("v", A_KV, PN, None, False), ("v", A_KV + PN, PN, None, False)]
        D_X = NC * len(C_PANELS)
        D_O = D_X + NT * len(X_PANELS)

        def each_tile(eng, tiles):
            if tiles < 4:
                for j in range(tiles):
                    yield j, j
            else:
                with eng.Fori(0, tiles // 4) as i:
                    for b in range(4):
                        yield 4 * i + b, b

        def heads_act(act, panel, p_next, tiles, t0, d0, sq0):
            kind, col, width, gain, _ = panel
            if p_next is not None:
                split_hi(act, p_next, p_next % 2)
            for j, b in each_tile(act, tiles):
                act.wait_ge(dense_done, d0 + 1)
                act.wait_ge(dense_done, d0 + j + 1)
                bank = ps[:, b, 0:PN]
                if kind == "v":
                    act.activation(row_tile(v_nat, t0 + j, col, PN), bank, ACT.Copy).then_inc(dense_evac, 1)
                    continue
                if width < PN:
                    act.activation(row_tile(v_nat, t0 + j, 0, A_KV), ps[:, b, A_KV:PN], ACT.Copy)
                act.activation(row_tile(q_nat if kind == "q" else k_nat, t0 + j, col, width), ps[:, b, 0:width], ACT.Copy)
                if not (isinstance(j, int) and sq0 + j < 2):
                    act.wait_ge(hsum_done, sq0 + j - 1)
                act.activation(hsq[:, b % 2, 0:width], ps[:, b, 0:width], ACT.Square).then_inc(dense_evac, 1)

        def row_tile(nat, j, col, width):
            if isinstance(j, int):
                return nat[:, j, col:col + width]
            return nat[:, ds(j, 1), col:col + width].squeeze(1)

        def head_rows(panel, tiles, t0):
            kind, col, width, _, _ = panel
            return (q_nat if kind == "q" else k_nat)[:, t0:t0 + tiles, col:col + width].rearrange("p t (h d) -> p t h d", d=HD)

        def heads_scale(dve, panel, tiles, t0, n):
            rows = head_rows(panel, tiles, t0)
            dve.wait_ge(hrs_done, n + 1)
            dve.tensor_tensor(rows, rows, bcast(hrs[:, 0:tiles, 0:panel[2] // HD], 3, HD), ALU.mult).then_inc(hn_done, 1)

        def heads_dve(dve, panel, before, p_next, tiles, t0, d0, sq0, n, mods=None):
            if p_next is not None:
                split_lo(dve, p_next, p_next % 2)
            if before is not None:
                heads_scale(dve, before, tiles, t0, n - 1)
            kind, col, width, gain, _ = panel
            for j in range(tiles):
                if kind != "v":
                    dve.wait_ge(dense_evac, d0 + j + 1)
                    if j == 0 and n:
                        dve.wait_ge(hms_done, n)
                    dve.tensor_reduce(hsum[:, j, 0:width // HD],
                                      hsq[:, j % 2, 0:width].rearrange("p (h d) -> p h d", d=HD),
                                      AX_X, ALU.add).then_inc(hsum_done, 1)
                if mods is not None and j % 2:
                    mods(j)

        pool_steps = [0]

        def pool_heads(pool, panel, tiles, t0, n, sums):
            kind, col, width, gain, turn = panel
            H = width // HD
            pool.wait_ge(hsum_done, sums)
            if n:
                pool.wait_ge(hrs_done, n)
            pool.tensor_scalar(hms[:, 0:tiles, 0:H], hsum[:, 0:tiles, 0:H], 1.0 / HD, EPS, ALU.mult, ALU.add).then_inc(hms_done, 1)
            pool.wait_ge(hms_done, n + 1)
            if n:
                pool.wait_ge(hn_done, n)
            half = neg_half[:, 0:tiles * H].rearrange("p (t h) -> p t h", h=H)
            pool.tensor_tensor(hrs[:, 0:tiles, 0:H], hms[:, 0:tiles, 0:H], half, ALU.pow).then_inc(hrs_done, 1)
            rows = head_rows(panel, tiles, t0)
            pool.wait_ge(hn_done, n + 1)
            if n == 0:
                pool.wait_ge(neg_done, 3)
            pool.tensor_tensor(rows, rows, bcast(bcast(head_gain[:, gain, :], 1, tiles), 2, H), ALU.mult).then_inc(hg_done, 1)
            if not turn:
                return
            for g in range(0, tiles, 4):
                if g == 0:
                    pool.wait_ge(hg_done, n + 1)
                    pool.wait_ge(tl_done, T_O)
                if pool_steps[0]:
                    pool.wait_ge(roped, pool_steps[0])
                part = rows[:, g:g + 4]
                out4 = rot[:, :, 0:width].rearrange("p t (h d) -> p t h d", d=HD)
                for half in range(2):
                    for pos in range(2):
                        a, b = half * 32 + pos * 16, half * 32 + (1 - pos) * 16
                        pool.tensor_tensor(out4[:, :, :, a:a + 16], part[:, :, :, b:b + 16],
                                           bcast(rope[:, 1, g:g + 4, a:a + 16], 2, H), ALU.mult).then_inc(roped, 1)
                pool.wait_ge(roped, pool_steps[0] + 4)
                pool.tensor_tensor(part, part, bcast(rope[:, 0, g:g + 4, :], 2, H), ALU.mult).then_inc(roped, 1)
                pool.wait_ge(roped, pool_steps[0] + 5)
                pool.tensor_tensor(part, part, out4, ALU.add).then_inc(roped, 1)
                pool_steps[0] += 6

        ROPED = 6 * 2 * 3

        def modx_pe_part(pe, m, first):
            pe.wait_ge(mod2_landed, 16 * (m + 1))
            if first:
                pe.wait_ge(tl_done, T_O)
            w = stage_up()
            for k in range(KT):
                g = k % 4
                mm = pe.matmul(ps[32 * g:32 * g + 2, 4, 0:PN], cond[:, :, k], w[:, k, :], start=(k < 4), stop=(k >= 4))
            mm.then_inc(modx_part, 1)

        def modx_pe_sum(pe, m):
            pe.wait_ge(modx_q, m + 1)
            pe.matmul(ps[0:1, 5, 0:PN], pick_x[:, 0:1], mod_q[:, :], start=True, stop=True).then_inc(modx_b, 1)

        def modx_dve_part(dve, m):
            dve.wait_ge(modx_part, m + 1)
            if m == 0:
                dve.wait_ge(tl_done, T_O)
            else:
                dve.wait_ge(modx_b, m)
            dve.tensor_copy(mod_q[:, :], ps[:, 4, 0:PN]).then_inc(modx_q, 1)

        def modx_dve_row(dve, m):
            dve.wait_ge(modx_b, m + 1)
            dve.wait_ge(modb_in, 16 * (m + 1))
            if m:
                dve.wait_ge(modx_stored, 16 * m)
            dve.tensor_tensor(mod_row[0:1, :], ps[0:1, 5, 0:PN], mod_b[0:1, :], ALU.add).then_inc(modx_row, 1)

        def keys_pe(pe):
            def tile(j, b, late):
                pe.wait_ge(ks_lo, j + 1)
                if late:
                    pe.wait_ge(kt_a, j - 1)
                    pe.wait_ge(kt_v, j - 1)
                else:
                    pe.wait_ge(dense_evac, D_O)
                for h in range(10):
                    mm = pe.transpose(ps[:, 3 * b + h // 4, (h % 4) * P:(h % 4 + 1) * P], k_split[:, b, h, :], ident[:, :])
                mm.then_inc(kt_tr, 1)
            tile(0, 0, False)
            tile(1, 1, False)
            with pe.Fori(1, 5) as i:
                for b in range(2):
                    tile(2 * i + b, b, True)

        def keys_act(act):
            def hi(j, b, late):
                if late:
                    act.wait_ge(kt_tr, 1)
                    act.wait_ge(kt_tr, j - 1)
                act.activation(k_split[:, b, :, 0:HD].bitcast(F32R),
                               row_tile(k_nat, j, 0, KVW).rearrange("p (h d) -> p h d", d=HD), ACT.Copy).then_inc(ks_hi, 1)

            def out(j, b):
                act.wait_ge(kt_tr, 1)
                act.wait_ge(kt_tr, j + 1)
                act.activation(kt[:, 0:4, ds(j * P, P)], ps[:, 3 * b, :].rearrange("p (h n) -> p h n", n=P), ACT.Copy).then_inc(kt_a, 1)

            act.wait_ge(*panel_used(P_O - 1))
            act.wait_ge(hg_done, 10)
            act.wait_ge(roped, ROPED)
            hi(0, 0, False)
            hi(1, 1, False)
            out(0, 0)
            out(1, 1)
            with act.Fori(1, 5) as i:
                for b in range(2):
                    hi(2 * i + b, b, True)
                for b in range(2):
                    out(2 * i + b, b)

        def keys_dve(dve):
            def lo(j, b):
                dve.wait_ge(ks_hi, j + 1)
                dve.tensor_tensor(k_split[:, b, :, HD:P], row_tile(k_nat, j, 0, KVW).rearrange("p (h d) -> p h d", d=HD),
                                  k_split[:, b, :, 0:HD], ALU.subtract).then_inc(ks_lo, 1)

            def out(j, b):
                dve.wait_ge(kt_tr, j + 1)
                dve.tensor_copy(kt[:, 4:8, ds(j * P, P)], ps[:, 3 * b + 1, :].rearrange("p (h n) -> p h n", n=P))
                dve.tensor_copy(kt[:, 8:10, ds(j * P, P)], ps[:, 3 * b + 2, 0:2 * P].rearrange("p (h n) -> p h n", n=P)).then_inc(kt_v, 1)

            dve.wait_ge(hg_done, 10)
            dve.wait_ge(roped, ROPED)
            with dve.Fori(0, 5) as i:
                for b in range(2):
                    lo(2 * i + b, b)
                for b in range(2):
                    out(2 * i + b, b)

        def pool_x(pool):
            for q, panel in enumerate(X_PANELS[:7]):
                pool_heads(pool, panel, NT, 0, 3 + q, 6 + NT * (q + 1))
            attention_pool(pool)

        def pool_c(pool):
            for q, panel in enumerate(C_PANELS[:3]):
                pool_heads(pool, panel, NC, NT, q, NC * (q + 1))

        A, B = 0, 1
        NB = NT

        def unit(ph, i, n):
            return 32 * ph + NB * i + n

        def local(ph, n):
            if ph == A:
                first, last = max(n - 1, 0), min(n + 1, NT - 1)
                return first, P * (last - first + 1), first - (n - 1)
            if n < 2:
                return 0, 8 * GRID, 7 - 2 * n - 1
            if n >= 6:
                return 4, 8 * GRID, 8 - 2 * n + 7 - 1
            return n - 2, NI * GRID, None

        def chunks(ph, n):
            first, width, _ = local(ph, n)
            return [(NT, P), (NT + 1, P)] + [(first + c, min(P, width - c * P)) for c in range((width + P - 1) // P)]

        def late_groups(ph, i, n, j=0):
            if ph == A:
                return 12 * i + 2 * max(0, min(n, 7) - 1) + (j if 1 <= n <= 6 else 0)
            return 48 + 16 * i + 2 * n + j

        def late(ph, n):
            return len(chunks(ph, n)) > 4

        def after(i, n, k):
            return (i, n + k) if n + k < NB else (i + 1, n + k - NB)

        def before(i, n):
            return (i, n - 1) if n else (i - 1, NB - 1)

        def keys_of(ph, i, j, a, width):
            if ph == A:
                h = i // 2
            else:
                h = 2 + 2 * i + j
            if isinstance(h, int):
                return kt[:, h, a:a + width]
            return kt[:, ds(h, 1), a:a + width].squeeze(1)

        def pe_turn_q(pe, ph, i, n):
            u = unit(ph, i, n)
            pe.wait_ge(qs_step, u + 1)
            if not isinstance(u, int) or u > 0:
                pe.wait_ge(qt_ready, u)
            for j in range(2):
                for o in range(2):
                    mm = pe.transpose(ps[:, 6, (2 * j + o) * P:(2 * j + o + 1) * P], q_split[:, n % 2, j, o, :], ident[:, :])
            mm.then_inc(qt_done, 1)

        def pe_scores(pe, ph, i, n, j):
            u = unit(ph, i, n)
            first, width, _ = local(ph, n)
            pe.wait_ge(qt_ready, u + 1)
            if True:
                if isinstance(u, int) and u == 0:
                    if True:
                        pe.wait_ge(kt_a, 10)
                        pe.wait_ge(kt_v, 10)
                else:
                    pe.wait_ge(exp_done, 2 * u - 1 + j)
                parts = [(ps[:, 2 * j, 0:CTX], S, CTX)]
                if ph == A:
                    parts.append((ps[:, 2 * j + 1, 0:width], first * P, width))
                else:
                    parts.append((ps[:, 2 * j, CTX:2 * CTX], first * P, 256))
                    parts.append((ps[:, 2 * j + 1, 0:width - 256], first * P + 256, width - 256))
                for dst, a, w in parts:
                    for o in range(2):
                        mm = pe.matmul(dst, q_t[:, n % 2, j, o, :], keys_of(ph, i, j, a, w), start=(o == 0), stop=(o == 1))
                mm.then_inc(s_done, 1)

        def pe_turn_p(pe, ph, i, n, j):
            u = unit(ph, i, n)
            every = chunks(ph, n)
            pe.wait_ge(exp_done, 2 * u + j + 1)
            if not isinstance(u, int) or 2 * u + j > 0:
                pe.wait_ge(pt0_evac, 2 * u + j)
            for c, (_, rows) in enumerate(every[:4]):
                mm = pe.transpose(ps[0:rows, 4, c * P:(c + 1) * P], probs[:, j, c * P:c * P + rows], ident[:, :])
            mm.then_inc(pt0_done, 1)
            if late(ph, n):
                g = late_groups(ph, i, n, j)
                if not isinstance(g, int) or g > 0:
                    pe.wait_ge(pt1_evac, g)
                for c, (_, rows) in enumerate(every[4:]):
                    mm = pe.transpose(ps[0:rows, 5, c * P:(c + 1) * P], probs[:, j, (4 + c) * P:(4 + c) * P + rows], ident[:, :])
                mm.then_inc(pt1_done, 1)

        def pe_values(pe, ph, i, n):
            u = unit(ph, i, n)
            pe.wait_ge(pt0_evac, 2 * u + 2)
            if late(ph, n):
                pe.wait_ge(pt1_evac, late_groups(ph, i, n) + 2)
            pe.wait_ge(vp_ready, 4 * ph + i + 1)
            if not isinstance(u, int) or u > 0:
                pe.wait_ge(on_evac, u)
            every = chunks(ph, n)
            for c, (tile, rows) in enumerate(every):
                for j in range(2):
                    mm = pe.matmul(ps[HD * j:HD * j + HD, 7, 0:P], v_pair[0:rows, tile, HD * j:HD * j + HD],
                                   prob_t[n % 2][0:rows, j, c * P:(c + 1) * P], start=(c == 0), stop=(c == len(every) - 1))
            mm.then_inc(pv_done, 1)

        def pe_turn_o(pe, ph, i, n):
            pe.wait_ge(ot_evac, unit(ph, i, n) + 1)
            pe.transpose(ps[:, 7, P:2 * P], o_t[:, :], ident[:, :]).then_inc(on_done, 1)

        def attention_pe(pe):
            for ph in (A, B):
                pe_turn_q(pe, ph, 0, 0)
                pe_turn_q(pe, ph, 0, 1)
                pe_scores(pe, ph, 0, 0, 0)
                pe_scores(pe, ph, 0, 0, 1)

                def pair(i, first, last):
                    for n in range(NB):
                        ahead, behind = not (last and n + 1 >= NB), not (first and n == 0)
                        pe_turn_p(pe, ph, i, n, 0)
                        if ahead:
                            pe_scores(pe, ph, *after(i, n, 1), 0)
                        if behind:
                            pe_values(pe, ph, *before(i, n))
                        if not (last and n + 2 >= NB):
                            pe_turn_q(pe, ph, *after(i, n, 2))
                        pe_turn_p(pe, ph, i, n, 1)
                        if ahead:
                            pe_scores(pe, ph, *after(i, n, 1), 1)
                        if behind:
                            pe_turn_o(pe, ph, *before(i, n))
                each_pair(pe, ph, pair)
                pe_values(pe, ph, PAIRS - 1, NB - 1)
                pe_turn_o(pe, ph, PAIRS - 1, NB - 1)

        def each_pair(eng, ph, pair):
            pair(0, True, False)
            with eng.Fori(1, PAIRS - 1) as i:
                pair(i, False, False)
            pair(PAIRS - 1, False, True)

        def act_q(act, ph, i, n):
            u = unit(ph, i, n)
            act.wait_ge(qt_done, u + 1)
            if not isinstance(u, int) or u >= 2:
                act.wait_ge(s_done, 2 * u - 2)
            act.activation(q_t[:, n % 2, :, :, :].rearrange("p a b n -> p (a b n)"), ps[:, 6, :], ACT.Copy).then_inc(qt_ready, 1)

        def act_exp(act, ph, i, n, j):
            u = unit(ph, i, n)
            _, width, _ = local(ph, n)
            act.wait_ge(min_done, 2 * u + j + 1)
            if not isinstance(u, int) or u > 0:
                pi, pn = (i, n - 1) if n else (i - 1, NB - 1)
                pp = ph
                if n == 0 and isinstance(i, int) and i == 0:
                    pp, pi = A, PAIRS - 1
                if late(pp, pn):
                    act.wait_ge(pt1_done, late_groups(pp, pi, pn, j) + 1)
                else:
                    act.wait_ge(pt0_done, 2 * u - 1 + j)
            low = small[:, j, 2:3]
            act.activation(probs[:, j, 0:CTX], ps[:, 2 * j, 0:CTX], ACT.Exp, bias=low, scale=-1.0,
                           accum_out=den[:, n % 2, j, 0:1])
            if ph == A:
                h = 2 * i + j
                act.activation(den[:, n % 2, j, 2:3], neg_sink[:, ds(h, 1)], ACT.Exp, bias=low, scale=-1.0)
            act.activation(probs[:, j, CTX:CTX + width], masked[:, j, 0:width], ACT.Exp, bias=low, scale=-1.0,
                           accum_out=den[:, n % 2, j, 1:2]).then_inc(exp_done, 1)

        def act_p(act, ph, i, n, j):
            if not late(ph, n):
                return
            u = unit(ph, i, n)
            act.wait_ge(pt1_done, late_groups(ph, i, n, j) + 1)
            if not isinstance(u, int) or u > 1:
                act.wait_ge(pv_done, u - 1)
            cols = P * (len(chunks(ph, n)) - 4)
            act.activation(prob_t[n % 2][:, j, 4 * P:4 * P + cols], ps[:, 5, 0:cols], ACT.Copy).then_inc(pt1_evac, 1)

        def act_v(act, ph, i):
            if ph == B or not isinstance(i, int) or i > 0:
                act.wait_ge(pv_done, NB)
                act.wait_ge(pv_done, 32 * ph + NB * i)
            if ph == A:
                col = (i // 2) * HD
                for j in range(2):
                    ins = act.activation(v_pair[:, :, HD * j:HD * j + HD], v_nat[:, :, ds(col, HD)], ACT.Copy)
            else:
                ins = act.activation(v_pair[:, :, :], v_nat[:, :, ds(A_KV + P * i, P)], ACT.Copy)
            ins.then_inc(vp_ready, 1)

        def attention_act(act):
            for ph in (A, B):
                act_q(act, ph, 0, 0)
                act_q(act, ph, 0, 1)
                act_exp(act, ph, 0, 0, 0)
                act_exp(act, ph, 0, 0, 1)

                def pair(i, first, last):
                    for n in range(NB):
                        for j in range(2):
                            act_p(act, ph, i, n, j)
                            if not (last and n + 1 >= NB):
                                act_exp(act, ph, *after(i, n, 1), j)
                            if j == 0 and not (last and n + 2 >= NB):
                                act_q(act, ph, *after(i, n, 2))
                        if n == 0:
                            act_v(act, ph, i)
                each_pair(act, ph, pair)

        def dve_min(dve, ph, i, n, j):
            u = unit(ph, i, n)
            first, width, at0 = local(ph, n)
            dve.wait_ge(s_done, 2 * u + j + 1)
            if ph == B:
                dve.wait_ge(tab_done, 4 * (i + 1))
            dve.tensor_reduce(small[:, j, 0:1], ps[:, 2 * j, 0:CTX], AX_X, ALU.min)
            dve.drain()
            scores = (ps[:, 2 * j + 1, 0:width] if ph == A else
                      ps[:, 2 * j:2 * j + 2, :].rearrange("p a n -> p (a n)")[:, CTX:CTX + width])
            if ph == A:
                h = 2 * i + j
                dve.tensor_tensor(small[:, j, 1:2], small[:, j, 0:1], neg_sink[:, ds(h, 1)], ALU.min)
                dve.drain()
                start = small[:, j, 1:2]
                table = band[:, :, :].rearrange("p a n -> p (a n)")[:, at0 * P:at0 * P + width]
                dve.wait_ge(band_in, 16)
            else:
                start = small[:, j, 0:1]
                table = (inner[:, j, :, :] if at0 is None else edge[:, j, at0:at0 + 8, :]).rearrange("p a n -> p (a n)")
                dve.wait_ge(bias_in, 32)
            dve.tensor_tensor_reduce(masked[:, j, 0:width], scores, table, 1.0, start, ALU.add, ALU.min,
                                     small[:, j, 2:3]).then_inc(min_done, 1)

        def dve_p(dve, ph, i, n, j):
            u = unit(ph, i, n)
            dve.wait_ge(pt0_done, 2 * u + j + 1)
            if not isinstance(u, int) or u > 1:
                dve.wait_ge(pv_done, u - 1)
            dve.tensor_copy(prob_t[n % 2][:, j, 0:4 * P], ps[:, 4, :]).then_inc(pt0_evac, 1)

        def dve_sums(dve, ph, i, n):
            u = unit(ph, i, n)
            terms = 3 if ph == A else 2
            dve.wait_ge(exp_done, 2 * u + 2)
            if not isinstance(u, int) or u > 0:
                dve.wait_ge(dn_step, 2 * u)
            dve.tensor_reduce(dsum[:, :], den[:, n % 2, :, 0:terms], AX_X, ALU.add).then_inc(dn_step, 1)
            dve.wait_ge(dn_step, 2 * u + 1)
            if not isinstance(u, int) or u > 1:
                dve.wait_ge(on_evac, u - 1)
            dve.reciprocal(rden[:, n % 2, :], dsum[:, :]).then_inc(dn_step, 1)

        def dve_o(dve, ph, i, n):
            u = unit(ph, i, n)
            dve.wait_ge(pv_done, u + 1)
            if not isinstance(u, int) or u > 0:
                dve.wait_ge(on_done, u)
            dve.tensor_copy(o_t[:, :], ps[:, 7, 0:P]).then_inc(ot_evac, 1)

        def dve_on(dve, ph, i, n):
            u = unit(ph, i, n)
            dve.wait_ge(on_done, u + 1)
            dve.wait_ge(dn_step, 2 * u + 2)
            dst = q_nat[:, n, ds(AW * ph + P * i, P)].rearrange("p (h d) -> p h d", d=HD)
            dve.tensor_tensor(dst, ps[:, 7, P:2 * P].rearrange("p (h d) -> p h d", d=HD),
                              bcast(rden[:, n % 2, :], 2, HD), ALU.mult).then_inc(on_evac, 1)

        def dve_tables(dve, i):
            for j in range(2):
                if j == 0:
                    dve.wait_ge(bias_in, 32)
                    dve.wait_ge(min_done, 64 + 16 * i)
                h = 2 * i + j
                row = raw_bias[:, ds(h, 1), 0:GRID].squeeze(1)
                windows = bass.AP(row.tensor, row.offset, [list(row.ap[0]), [RB, NE], [1, GRID]])
                dve.scalar_tensor_tensor(out=edge[:, j, :, :], in0=windows, scalar=-1.0, in1=bcast(col_mask[:, :], 1, NE),
                                         op0=ALU.mult, op1=ALU.add).then_inc(tab_done, 1)
            for j in range(2):
                dve.wait_ge(tab_done, 4 * i + 1 + j)
                dve.tensor_tensor(inner[:, j, :, :], edge[:, j, 2:2 + NI, :], bcast(row_mask[:, :], 2, GRID),
                                  ALU.add).then_inc(tab_done, 1)

        def attention_dve(dve):
            for ph in (A, B):
                if ph == B:
                    dve_tables(dve, 0)
                dve_min(dve, ph, 0, 0, 0)
                dve_min(dve, ph, 0, 0, 1)

                def pair(i, first, last):
                    for n in range(NB):
                        ahead, behind = not (last and n + 1 >= NB), not (first and n == 0)
                        if ph == B and n == NB - 1 and ahead:
                            dve_tables(dve, i + 1)
                        dve_p(dve, ph, i, n, 0)
                        if ahead:
                            dve_min(dve, ph, *after(i, n, 1), 0)
                        if behind:
                            dve_o(dve, ph, *before(i, n))
                        dve_p(dve, ph, i, n, 1)
                        if ahead:
                            dve_min(dve, ph, *after(i, n, 1), 1)
                        dve_sums(dve, ph, i, n)
                        if behind:
                            dve_on(dve, ph, *before(i, n))
                each_pair(dve, ph, pair)
                dve_o(dve, ph, PAIRS - 1, NB - 1)
                dve_on(dve, ph, PAIRS - 1, NB - 1)

        def pool_q(pool, ph, i, n):
            u = unit(ph, i, n)
            src = q_nat[:, n, ds(AW * ph + P * i, P)].rearrange("p (h d) -> p h d", d=HD)
            dst = q_split[:, n % 2, :, :, :]
            if not isinstance(u, int) or u >= 2:
                pool.wait_ge(qt_done, 1)
                pool.wait_ge(qt_done, u - 1)
            else:
                pool.wait_ge(roped, ROPED)
                pool.wait_ge(dense_done, D_O)
                pool.wait_ge(hg_done, 10)
            pool.tensor_copy(dst[:, :, 0, 0:HD].bitcast(F32R), src)
            pool.drain()
            pool.tensor_tensor(dst[:, :, 0, HD:P], src, dst[:, :, 0, 0:HD], ALU.subtract)
            pool.tensor_copy(dst[:, :, 1, HD:P], dst[:, :, 0, 0:HD])
            pool.drain()
            pool.tensor_copy(dst[:, :, 1, 0:HD], dst[:, :, 0, HD:P]).then_inc(qs_step, 1)

        def attention_pool(pool):
            for n in range(NB):
                pool_q(pool, A, 0, n)
            with pool.Fori(1, PAIRS) as i:
                for n in range(NB):
                    pool_q(pool, A, i, n)
            with pool.Fori(0, PAIRS) as i:
                for n in range(NB):
                    pool_q(pool, B, i, n)

        def sync_attention(sp):
            sp.wait_ge(ready, 2)
            flat = t["rpb_b"].rearrange("a h r c -> (a h r c)").unsqueeze(0)
            sp.dma_start(rpb_pad[RPAD:RPAD + 8 * RPH].unsqueeze(0), flat).then_inc(pad_done, 16)
            sp.dma_start(rpb_pad[0:RPAD].unsqueeze(0), zero_row[0:1, :]).then_inc(pad_done, 16)
            sp.dma_start(rpb_pad[RPAD + 8 * RPH:].unsqueeze(0), zero_row[0:1, :]).then_inc(pad_done, 16)
            sp.wait_ge(pad_done, 48)
            sp.dma_start(rpb_skew.rearrange("(c n) -> c n", c=GRID)[:, 0:RPL],
                         bass.AP(rpb_pad.tensor, 0, [[0, GRID], [1, RPL]])).then_inc(skewed, 16)
            sp.wait_ge(dense_done, D_O)
            sp.wait_ge(w_lo_done, P_O)
            sp.dma_start(band[:, :, :], t["k_band"]).then_inc(band_in, 16)
            sp.wait_ge(skewed, 16)
            sp.wait_ge(ks_lo, 10)
            for parity in range(2):
                src = bass.AP(rpb_skew.tensor, RPAD + (1 - parity) * RB + RB // 2, [[RPL, GRID], [RPH, 8], [1, RPW]])
                sp.dma_start(raw_bias[GRID * parity:GRID * parity + GRID, :, :], src).then_inc(bias_in, 16)
            sp.wait_ge(modx_stored, 256)
        @block.sync
        def _(sp):
            sp.dma_start(cond[:, 0, :], t["c"][0].rearrange("(p k) -> p k", k=KT)).then_inc(cond_in, 16)
            sp.dma_start(cond[:, 1, :], t["c_ctx"].rearrange("(p k) -> p k", k=KT)).then_inc(cond_in, 16)
            sp.dma_start(ident[:, :], t["k_ident"]).then_inc(pe_consts_in, 16)
            sp.dma_start(pick_x[:, :], t["k_pick"][0]).then_inc(pe_consts_in, 16)
            sp.dma_start(pick_c[:, :], t["k_pick"][1]).then_inc(pe_consts_in, 16)
            for j in range(8):
                w = t["w_mod"][0].rearrange("(p k) n -> p k n", k=KT)[:, :, j * PN:(j + 1) * PN]
                sp.dma_start(mod_w[:, j, :].rearrange("p (k n) -> p k n", k=KT), w).then_inc(modw_in[j], 16)
                if j == 1:
                    for d in range(2):
                        sp.dma_start(mod_1[:, 2 * d:2 * d + 2, :].rearrange("p a b -> p (a b)"),
                                     t["b_mod"][0, 0:2 * D].partition_broadcast(P)).then_inc(mod1_in, 16)
                    sp.dma_start(norm1[:, :], t["norm1_g"][0].partition_broadcast(P)).then_inc(mod1_in, 16)
                if j == 3:
                    sp.dma_start(ctx_in[:, :, :], t["ctx"][0].rearrange("(t p) d -> p t d", p=P)).then_inc(ctx_landed, 16)
            load_weights(sp, 0, panel_of(t["w_in"], CTX_COLS[0]))
            for j in range(NT):
                sp.dma_start(q_nat[:, j, :], t["x"][0, j * P:(j + 1) * P, :]).then_inc(x_in[j], 16)
            sp.dma_start(rope[:, :, :, :], t["k_rope"]).then_inc(consts_in, 16)
            for j, name in enumerate(("qn_a", "kn_a", "qn_b", "kn_b")):
                sp.dma_start(head_gain[:, j, :], t[name][0].partition_broadcast(P)).then_inc(consts_in, 16)
            sp.dma_start(neg_sink[:, :], t["sink_a"][0].partition_broadcast(P)).then_inc(consts_in, 16)
            sp.dma_start(row_mask[:, :], t["k_row_mask"]).then_inc(consts_in, 16)
            sp.dma_start(col_mask[:, :], t["k_col_mask"]).then_inc(consts_in, 16)
            for j in range(1, 5):
                load_weights(sp, j, panel_of(t["w_in"], CTX_COLS[j]))
            for j in range(2):
                load_weights(sp, P_X + j, panel_of(t["w_in"], j * PN))
            sync_x(sp)
            sync_attention(sp)


        @block.gpsimd
        def _(pool):
            pool.memset(neg_half[:, :], -0.5).then_inc(ready, 1)
            pool.memset(zero_row[:, :], 0.0).then_inc(ready, 1)
            norm_pool(pool, NC, T_C, D)
            pool_c(pool)
            norm_pool(pool, NT, T_X, D)
            pool_x(pool)


        @block.tensor
        def _(pe):
            pe.wait_ge(pe_consts_in, 48)
            pe.wait_ge(cond_done, 1)
            pe.wait_ge(banks_clear, 1)
            for j in range(8):
                pe.wait_ge(modw_in[j], 16)
                if j >= 2:
                    pe.wait_ge(part_evac, j - 1)
                w = mod_w[:, j, :].rearrange("p (k n) -> p k n", k=KT)
                for k in range(KT):
                    g = k % 4
                    mm = pe.matmul(ps[32 * g:32 * g + 2, j % 2, 0:PN], cond[:, :, k], w[:, k, :], start=(k < 4), stop=(k >= 4))
                mm.then_inc(part_done, 1)
                pe.wait_ge(part_evac, j + 1)
                if j >= 1:
                    pe.wait_ge(mod_added, 2 * j)
                pe.matmul(ps[:, 2, 0:PN], pick_x[:, :], mod_part[:, j % 2, :], start=True, stop=True).then_inc(mod_done, 1)
                pe.matmul(ps[:, 3, 0:PN], pick_c[:, :], mod_part[:, j % 2, :], start=True, stop=True).then_inc(mod_done, 1)
            turn_pe(pe, NC, T_C)
            for p in range(len(C_PANELS)):
                for _ in rows_pe(pe, p, p % 2, NC, T_C, NC * p, lag=2):
                    pass
            turn_pe(pe, NT, T_X)
            pe.wait_ge(dense_evac, D_X)
            with pe.Fori(0, 4) as i:
                for b in range(2):
                    p = 2 * i + b
                    for j in rows_pe(pe, P_X + p, (P_X + b) % 2, NT, T_X, D_X + NT * p):
                        m = 2 * p + j // 4
                        if j % 4 == 1:
                            modx_pe_part(pe, m, b == 0 and j == 1)
                        if j % 4 == 3:
                            modx_pe_sum(pe, m)
            for _ in rows_pe(pe, P_X + 8, (P_X + 8) % 2, NT, T_X, D_X + NT * 8):
                pass
            keys_pe(pe)
            attention_pe(pe)


        @block.scalar
        def _(act):
            act.wait_ge(cond_in, 32)
            act.activation(cond[:, :, :], cond[:, :, :], ACT.Silu).then_inc(cond_done, 1)
            split_hi(act, 0, 0)
            norm_sums(act, NC, T_C, lambda j: ctx_in[:, j, :], lambda e, j: e.wait_ge(ctx_landed, 16))
            turn_act(act, NC, T_C, None)
            for n, panel in enumerate(C_PANELS):
                heads_act(act, panel, n + 1, NC, NT, NC * n, NC * n)
            norm_sums(act, NT, T_X, lambda j: q_nat[:, j, :], lambda e, j: e.wait_ge(x_in[j], 16))
            turn_act(act, NT, T_X, P_X - 1)
            for n, panel in enumerate(X_PANELS):
                heads_act(act, panel, P_X + n + 1 if n < 8 else None, NT, 0, D_X + NT * n, 6 + NT * n)
            keys_act(act)
            attention_act(act)


        @block.vector
        def _(dve):
            dve.memset(ps[:, 0:2, 0:PN], 0.0).then_inc(banks_clear, 1)
            dve.wait_ge(consts_in, 16 * 8)
            for g in (0, 2):
                dve.tensor_scalar(head_gain[:, g, :], head_gain[:, g, :], -HD ** -0.5, None, ALU.mult).then_inc(neg_done, 1)
            dve.tensor_scalar(neg_sink[:, :], neg_sink[:, :], -1.0, None, ALU.mult).then_inc(neg_done, 1)
            for j in range(8):
                dve.wait_ge(part_done, j + 1)
                if j >= 2:
                    dve.wait_ge(mod_done, 2 * j - 2)
                dve.tensor_copy(mod_part[:, j % 2, :], ps[:, j % 2, 0:PN]).then_inc(part_evac, 1)
                if j == 0:
                    dve.wait_ge(mod1_in, 48)
                dve.wait_ge(mod_done, 2 * j + 2)
                for d in range(2):
                    dst = mod_1[:, 2 * d + j // 4, (j % 4) * PN:(j % 4 + 1) * PN]
                    dve.tensor_tensor(dst, ps[:, 2 + d, 0:PN], dst, ALU.add).then_inc(mod_added, 1)
            for d, g in ((0, gain_c), (1, gain_x)):
                dve.wait_ge(mod_added, 16)
                dve.scalar_tensor_tensor(out=g, in0=g, scalar=1.0, in1=norm1[:, :], op0=ALU.add, op1=ALU.mult).then_inc(mod_added, 1)
            dve.wait_ge(mod_added, 18)
            split_lo(dve, 0, 0)
            turn_dve(dve, NC, T_C, lambda j: row_tile(ctx_in, j, 0, D), gain_c, shift_c, 0)
            last = None
            n = 0
            for q, panel in enumerate(C_PANELS):
                heads_dve(dve, panel, last, q + 1, NC, NT, NC * q, NC * q, n)
                last, n = (panel, n + 1) if panel[0] != "v" else (None, n)
            turn_dve(dve, NT, T_X, lambda j: row_tile(q_nat, j, 0, D), gain_x, shift_x, NC)
            last = None
            for q, panel in enumerate(X_PANELS):
                def mods(j, q=q):
                    m = 2 * q + j // 4
                    (modx_dve_part if j % 4 == 1 else modx_dve_row)(dve, m)
                heads_dve(dve, panel, last, P_X + q + 1 if q < 8 else None, NT, 0, D_X + NT * q, 6 + NT * q, n, mods if q < 8 else None)
                last, n = (panel, n + 1) if panel[0] != "v" else (None, n)
            keys_dve(dve)
            attention_dve(dve)

        done.close()
        mod2_in, on_in, norm2_in = sem("mod2_in"), sem("on_in"), sem("norm2_in")
        gated, merged, gain2_done = sem("gated"), sem("merged"), sem("gain2_done")
        tmp = at("tmp", [2, PN], F32, k_off)
        with nc.Block() as block:

            @block.sync
            def _(sp):
                load_weights(sp, P_O, panel_of(t["w_out"], 0))
                for j, name in enumerate(("on_a", "on_b")):
                    sp.dma_start(on_ab[:, j * AW:(j + 1) * AW], t[name][0].partition_broadcast(P)).then_inc(on_in, 16)
                for j in range(4):
                    sp.dma_start(mod_2[:, j, :], mod_dram[j].partition_broadcast(P)).then_inc(mod2_in, 16)
                sp.dma_start(norm2[:, :], t["norm2_g"][0].partition_broadcast(P)).then_inc(norm2_in, 16)
                load_weights(sp, P_O + 1, panel_of(t["w_out"], PN))
                for j in range(NT):
                    sp.wait_ge(xn_done, T_O + j + 1)
                    sp.dma_start(q_nat[:, j, :], t["x"][0, j * P:(j + 1) * P, :]).then_inc(x_in[j], 16)
                for j in range(2, 4):
                    load_weights(sp, P_O + j, panel_of(t["w_out"], j * PN))
                load_weights(sp, P_F, panel_of(t["w_gate"], 0))

            @block.gpsimd
            def _(pool):
                norm_pool(pool, NT, T_O, AW, 2)

            @block.tensor
            def _(pe):
                turn_pe(pe, NT, T_O)
                for p in range(4):
                    for _ in rows_pe(pe, P_O + p, p % 2, NT, T_O, D_O + NT * p):
                        pass

            @block.scalar
            def _(act):
                for j in range(NT):
                    act.wait_ge(ss_done, T_O + j)
                    if j == 0:
                        act.wait_ge(ms_done, 4)
                    for g in range(2):
                        last = act.activation(junk[:, g * AW:(g + 1) * AW], q_nat[:, j, g * AW:(g + 1) * AW], ACT.Square,
                                              accum_out=sumsq[:, 2 * j + g:2 * j + g + 1])
                    last.then_inc(ss_done, 1)
                split_hi(act, P_O, 0)
                turn_act(act, NT, T_O, None)
                for p in range(1, 4):
                    split_hi(act, P_O + p, p % 2)

            @block.vector
            def _(dve):
                dve.wait_ge(on_in, 32)
                with dve.Fori(0, NT // 2) as i:
                    for b in range(2):
                        j = 2 * i + b
                        dve.wait_ge(rs_done, 2 * STAGE_OF[T_O] + 2)
                        dve.wait_ge(tr_done, T_O + j - 1)
                        for g in range(2):
                            last = dve.scalar_tensor_tensor(
                                out=xn[:, b, g * AW:(g + 1) * AW], in0=row_tile(q_nat, j, g * AW, AW),
                                scalar=rstd[:, ds(2 * j + g, 1)], in1=on_ab[:, g * AW:(g + 1) * AW],
                                op0=ALU.mult, op1=ALU.mult)
                        last.then_inc(xn_done, 1)
                    if True:
                        for b in range(2):
                            j = 2 * i + b
                            dve.wait_ge(th_done, T_O + j + 1)
                            dve.tensor_tensor(ht_lo[:, :, ds(j * P, P)], turned(b),
                                              ht_hi[:, :, ds(j * P, P)].bitcast(F32), ALU.subtract).then_inc(tl_done, 1)
                split_lo(dve, P_O, 0)
                dve.wait_ge(mod2_in, 64)
                dve.wait_ge(norm2_in, 16)
                dve.scalar_tensor_tensor(out=mod_2[:, 2, :], in0=mod_2[:, 2, :], scalar=1.0, in1=norm2[:, :],
                                         op0=ALU.add, op1=ALU.mult).then_inc(gain2_done, 1)
                for p in range(4):
                    if p < 3:
                        split_lo(dve, P_O + p + 1, (p + 1) % 2)
                    cols = slice(p * PN, (p + 1) * PN)
                    for j in range(NT):
                        n = NT * p + j
                        dve.wait_ge(dense_done, D_O + n + 1)
                        if n >= 2:
                            dve.wait_ge(merged, n - 1)
                        dve.tensor_tensor(tmp[:, n % 2, :], ps[:, j % 4, 0:PN], mod_2[:, 0, cols], ALU.mult).then_inc(dense_evac, 1)
                        dve.wait_ge(dense_evac, D_O + n + 1)
                        if p == 0:
                            dve.wait_ge(x_in[j], 32)
                        dve.tensor_tensor(q_nat[:, j, cols], q_nat[:, j, cols], tmp[:, n % 2, :], ALU.add).then_inc(merged, 1)

        def features_pe(pe, p, slot, chunk, bank0, out_done, free):
            pe.wait_ge(w_lo_done, p + 1)
            wh, wl = (w[:, slot, :].rearrange("p (k n) -> p k n", k=KT) for w in (w_hi, w_lo))
            for f in range(2):
                for h in range(2):
                    b = 2 * f + h
                    free(b)
                    bank = ps[:, bank0 + b, :]
                    for k in range(KT):
                        a, c = wh[:, k, f * P:(f + 1) * P], wl[:, k, f * P:(f + 1) * P]
                        x_hi, x_lo = ht_hi[:, k, h * 512:(h + 1) * 512], ht_lo[:, k, h * 512:(h + 1) * 512]
                        pe.matmul(bank, a, x_hi, start=(k == 0), stop=False)
                        pe.matmul(bank, a, x_lo, start=False, stop=False)
                        mm = pe.matmul(bank, c, x_hi, start=False, stop=(k == KT - 1))
                    mm.then_inc(out_done, 1)

        def down_pe(pe, p, slot, chunk, lo_done, out_done, evac):
            pe.wait_ge(w_lo_done, p + 1)
            pe.wait_ge(lo_done, 4 * chunk + 4)
            wh, wl = (w[:, slot, :].rearrange("p (f n) -> p f n", f=2) for w in (w_hi, w_lo))
            for o in range(2 * NT):
                j, h = o // 2, o % 2
                if not isinstance(chunk, int) or 16 * chunk + o >= 4:
                    pe.wait_ge(evac, 16 * chunk + o - 3)
                for f in range(2):
                    a = act_hi[:, f, j * P:(j + 1) * P]
                    c = act_lo[:, f, j * P:(j + 1) * P]
                    x_hi, x_lo = wh[:, f, h * 512:(h + 1) * 512], wl[:, f, h * 512:(h + 1) * 512]
                    pe.matmul(ps[:, 4 + o % 4, :], a, x_hi, start=(f == 0), stop=False)
                    pe.matmul(ps[:, 4 + o % 4, :], a, x_lo, start=False, stop=False)
                    mm = pe.matmul(ps[:, 4 + o % 4, :], c, x_hi, start=False, stop=(f == 1))
                mm.then_inc(out_done, 1)

        def down_dve(dve, chunk, outputs, done_sem, evac, first=False):
            for o in outputs:
                j, h = o // 2, o % 2
                row = q_nat[:, j, h * 512:(h + 1) * 512]
                dve.wait_ge(done_sem, 16 * chunk + o + 1)
                if first:
                    dve.tensor_copy(row, ps[:, 4 + o % 4, :]).then_inc(evac, 1)
                    continue
                if not isinstance(chunk, int) or chunk > 0:
                    dve.wait_ge(evac, 16 * chunk + o - 15)
                dve.tensor_tensor(row, row, ps[:, 4 + o % 4, :], ALU.add).then_inc(evac, 1)

        def quarter(x, b):
            return x[:, b // 2, (b % 2) * 512:(b % 2 + 1) * 512]

        def act_split_hi(act, chunk, src, ready_sem, hi_sem, used):
            for b in range(4):
                act.wait_ge(ready_sem, 4 * chunk + b + 1)
                if b == 0 and (not isinstance(chunk, int) or chunk > 0):
                    act.wait_ge(used, 16 * chunk)
                act.activation(quarter(act_hi, b), quarter(src, b), ACT.Copy).then_inc(hi_sem, 1)

        def act_split_lo(dve, chunk, src, hi_sem, lo_sem):
            for b in range(4):
                dve.wait_ge(hi_sem, 4 * chunk + b + 1)
                dve.tensor_tensor(quarter(act_lo, b), quarter(src, b), quarter(act_hi, b).bitcast(F32), ALU.subtract).then_inc(lo_sem, 1)

        w_scaled = sem("w_scaled")
        gate_done, up_done, down_done = sem("gate_done"), sem("up_done"), sem("down_done")
        silu_done, af_done, ah_done, al_done, down_evac = (sem(x) for x in (
            "silu_done", "af_done", "ah_done", "al_done", "down_evac"))

        def p_gate(c):
            return P_F if isinstance(c, int) and c == 0 else P_F + 3 * c - 1

        def p_down(c):
            return P_F + 3 * c + 3 if not (isinstance(c, int) and c == CH1 - 1) else P_Z - 1

        def p_up(c):
            return P_F + 3 * c + 1

        def down_panel(w, row):
            if isinstance(row, int):
                return w[0, row:row + PN, :].rearrange("(f p) n -> p f n", p=P)
            return w[0, ds(row, PN), :].rearrange("(f p) n -> p f n", p=P)

        def stage_down():
            return stage[:, :].rearrange("p (f n) -> p f n", f=2)

        def used_gate(c):
            return gate_done, 4 * c + 4

        def used_up(c):
            return up_done, 4 * c + 4

        def used_down(c):
            return down_done, 16 * c + 16

        def chunks_in_pairs(eng, chunk):
            for b in range(2):
                chunk(b, b)
            with eng.Fori(1, (CH1 - 1) // 2 - 1) as i:
                for b in range(2):
                    chunk(2 * i + b, b)
            for b in range(2):
                chunk(CH1 - 3 + b, b)

        with nc.Block() as block:

            @block.sync
            def _(sp):
                load_weights(sp, P_F + 1, panel_of(t["w_up"], 0))

                def chunk(c, last=False):
                    if not last:
                        load_weights(sp, p_gate(c + 1), panel_of(t["w_gate"], (c + 1) * PN))
                    load_weights(sp, p_down(c), down_panel(t["w_down"], c * PN), stage_down())
                    if not last:
                        load_weights(sp, p_up(c + 1), panel_of(t["w_up"], (c + 1) * PN))
                with sp.Fori(0, CH1 - 1) as c:
                    chunk(c)
                chunk(CH1 - 1, True)
                load_weights(sp, P_Z, panel_of(t["w_in_2"], 0))

            @block.gpsimd
            def _(pool):
                norm_pool(pool, NT, T_H, D)

                def scale(c, last=False):
                    p = p_down(c)
                    pool.wait_ge(w_landed, 16 * (p + 1))
                    pool.tensor_tensor(stage_down(), stage_down(), bcast(mod_2[:, 3, :], 1, 2), ALU.mult).then_inc(w_scaled, 1)
                with pool.Fori(0, CH1 - 1) as c:
                    scale(c)
                scale(CH1 - 1, True)

            @block.tensor
            def _(pe):
                turn_pe(pe, NT, T_H)
                pe.wait_ge(tl_done, T_H + NT)

                def gate(c, slot):
                    def free(b):
                        if not isinstance(c, int) or c > 0:
                            pe.wait_ge(silu_done, 4 * c + b - 3)
                    features_pe(pe, p_gate(c), slot, c, 0, gate_done, free)

                def up(c, slot):
                    def free(b):
                        if not isinstance(c, int) or c > 0:
                            pe.wait_ge(down_evac, 16 * c + b - 3)
                    features_pe(pe, p_up(c), slot, c, 4, up_done, free)

                gate(0, P_F % 2)
                up(0, (P_F + 1) % 2)

                def chunk(c, b):
                    slot = (P_F + b) % 2
                    gate(c + 1, slot)
                    down_pe(pe, p_down(c), 1 - slot, c, al_done, down_done, down_evac)
                    up(c + 1, slot)

                chunks_in_pairs(pe, chunk)
                down_pe(pe, p_down(CH1 - 1), (P_Z - 1) % 2, CH1 - 1, al_done, down_done, down_evac)

            @block.scalar
            def _(act):
                norm_sums(act, NT, T_H, lambda j: q_nat[:, j, :], lambda e, j: None)
                split_hi(act, P_F, P_F % 2, used=(dense_done, D_O + 3 * NT))
                turn_act(act, NT, T_H, P_F - 1)
                split_hi(act, P_F + 1, (P_F + 1) % 2, used=(dense_done, D_O + 4 * NT))

                def silus(c):
                    for b in range(4):
                        act.wait_ge(gate_done, 4 * c + b + 1)
                        if not isinstance(c, int) or c > 0:
                            act.wait_ge(af_done, 4 * c + b - 3)
                        act.activation(quarter(silu, b), ps[:, b, :], ACT.Silu).then_inc(silu_done, 1)

                silus(0)
                split_hi(act, p_gate(1), P_F % 2, used=used_gate(0))

                def chunk(c, b):
                    slot = (P_F + b) % 2
                    split_hi(act, p_down(c), 1 - slot, used=used_up(c), scaled=c + 1)
                    act_split_hi(act, c, act_f, af_done, ah_done, down_done)
                    silus(c + 1)
                    split_hi(act, p_up(c + 1), slot, used=used_gate(c + 1))
                    if isinstance(c, int) and c == CH1 - 2:
                        split_hi(act, p_down(CH1 - 1), 1 - slot, used=used_down(c), scaled=CH1)
                    else:
                        split_hi(act, p_gate(c + 2), 1 - slot, used=used_down(c))

                chunks_in_pairs(act, chunk)
                act_split_hi(act, CH1 - 1, act_f, af_done, ah_done, down_done)

            @block.vector
            def _(dve):
                turn_dve(dve, NT, T_H, lambda j: row_tile(q_nat, j, 0, D), mod_2[:, 2, :], mod_2[:, 1, :], NC + NT)
                split_lo(dve, P_F, P_F % 2)
                split_lo(dve, P_F + 1, (P_F + 1) % 2)
                split_lo(dve, p_gate(1), P_F % 2)

                def gated_up(c):
                    for b in range(4):
                        dve.wait_ge(silu_done, 4 * c + b + 1)
                        dve.wait_ge(up_done, 4 * c + b + 1)
                        if not isinstance(c, int) or c > 0:
                            dve.wait_ge(al_done, 4 * c + b - 3)
                        dve.tensor_tensor(quarter(act_f, b), quarter(silu, b), ps[:, 4 + b, :], ALU.mult).then_inc(af_done, 1)

                def chunk(c, b):
                    slot = (P_F + b) % 2
                    gated_up(c)
                    split_lo(dve, p_down(c), 1 - slot)
                    act_split_lo(dve, c, act_f, ah_done, al_done)
                    down_dve(dve, c, range(4), down_done, down_evac)
                    split_lo(dve, p_up(c + 1), slot)
                    down_dve(dve, c, range(4, 2 * NT), down_done, down_evac)
                    split_lo(dve, p_gate(c + 2), 1 - slot)

                chunks_in_pairs(dve, chunk)
                gated_up(CH1 - 1)
                act_split_lo(dve, CH1 - 1, act_f, ah_done, al_done)
                down_dve(dve, CH1 - 1, range(2 * NT), down_done, down_evac)
        x2_dram = nc.dram_tensor("x2_dram", [S, D], F32, kind="Internal").ap()
        VW = D // 2
        KW = D // 4
        RANK = 16
        LR = 2 * VW + 2 * KW + 2 * VW
        zu = at("zu", [NT, VW], F32, k_off)
        zv = at("zv", [NT, VW], F32, k_off + 16384)
        zq = at("zq", [NT, KW], F32, k_off + 32768)
        zk = at("zk", [NT, KW], F32, k_off + 40960)
        zvb = at("zvb", [NT, VW], F32, nat)
        zg = at("zg", [NT, VW], F32, nat + 16384)
        w_lr = at("w_lr", [KT, RANK], F32, k_off + 49152)
        w_lr_hi = at("w_lr_hi", [KT, RANK], F32R, k_off + 49152 + 512)
        w_lr_lo = at("w_lr_lo", [KT, RANK], F32R, k_off + 49152 + 1024)
        gain_z = at("gain_z", [D], F32, k_off)
        lr_t = at("lr_t", [S], F32, rope_at)
        vsum = fixed("vsum", [2, NT])
        x2_stored, gz_in, lr_in, lr_ones, lr_split, lr_done, lr_evac, z_done = (sem(x) for x in (
            "x2_stored", "gz_in", "lr_in", "lr_ones", "lr_split", "lr_done", "lr_evac", "z_done"))
        GELU = ACT.Gelu_apprx_tanh
        Z_PANELS = [(zu, 0, GELU), (zu, PN, GELU), (zv, 0, GELU), (zv, PN, GELU), (zq, 0, ACT.Copy), (zk, 0, ACT.Copy),
                    (zvb, 0, ACT.Copy), (zvb, PN, ACT.Copy), (zg, 0, ACT.Silu), (zg, PN, ACT.Silu)]
        D_Z = D_O + 4 * NT
        with nc.Block() as block:

            @block.sync
            def _(sp):
                sp.dma_start(gain_z[:, :], t["pre_mix_g_2"][0].partition_broadcast(P)).then_inc(gz_in, 16)
                for j in range(NT):
                    sp.dma_start(x2_dram[j * P:(j + 1) * P, :], q_nat[:, j, :]).then_inc(x2_stored, 16)
                sp.dma_start(w_lr[:, :, :], t["w_in_2"][0].rearrange("(k p) n -> p k n", p=P)[:, :, LR:LR + RANK]).then_inc(lr_in, 16)
                for p in range(1, 10):
                    load_weights(sp, P_Z + p, panel_of(t["w_in_2"], p * PN))
                load_weights(sp, P_M, panel_of(t["w_out_2"], 0))
                sp.wait_ge(x2_stored, 16 * NT)

            @block.gpsimd
            def _(pool):
                pool.memset(lr_t[0:32, :], 1.0).then_inc(lr_ones, 1)
                norm_pool(pool, NT, T_Z, D)

            @block.tensor
            def _(pe):
                turn_pe(pe, NT, T_Z)
                pe.wait_ge(lr_split, 2)
                pe.wait_ge(tl_done, T_Z + NT)
                for h in range(2):
                    bank = ps[0:RANK, 4 + h, :]
                    for k in range(KT):
                        x_hi, x_lo = ht_hi[:, k, h * 512:(h + 1) * 512], ht_lo[:, k, h * 512:(h + 1) * 512]
                        pe.matmul(bank, w_lr_hi[:, k, :], x_hi, start=(k == 0), stop=False)
                        pe.matmul(bank, w_lr_hi[:, k, :], x_lo, start=False, stop=False)
                        mm = pe.matmul(bank, w_lr_lo[:, k, :], x_hi, start=False, stop=(k == KT - 1))
                    mm.then_inc(lr_done, 1)
                for p in range(10):
                    for _ in rows_pe(pe, P_Z + p, (P_Z + p) % 2, NT, T_Z, D_Z + NT * p):
                        pass

            @block.scalar
            def _(act):
                norm_sums(act, NT, T_Z, lambda j: q_nat[:, j, :], lambda e, j: None)
                split_hi(act, P_Z, P_Z % 2, used=(down_done, 16 * CH1))
                turn_act(act, NT, T_Z, None)
                act.wait_ge(lr_in, 16)
                act.activation(w_lr_hi[:, :, :], w_lr[:, :, :], ACT.Copy).then_inc(lr_split, 1)
                act.wait_ge(lr_ones, 1)
                for h in range(2):
                    act.wait_ge(lr_done, h + 1)
                    act.activation(lr_t[0:RANK, h * 512:(h + 1) * 512], ps[0:RANK, 4 + h, :], ACT.Copy).then_inc(lr_evac, 1)
                for p, (dst, col, fn) in enumerate(Z_PANELS):
                    if p < 9:
                        split_hi(act, P_Z + p + 1, (P_Z + p + 1) % 2, used=(dense_done, D_Z + NT * p))
                    if p == 6:
                        act.wait_ge(x2_stored, 16 * NT)
                    for j in range(NT):
                        act.wait_ge(dense_done, D_Z + NT * p + j + 1)
                        more = {"accum_out": vsum[:, p - 2, j:j + 1]} if dst is zv else {}
                        act.activation(dst[:, j, col:col + PN], ps[:, j % 4, 0:PN], fn, **more).then_inc(dense_evac, 1)

            @block.vector
            def _(dve):
                dve.wait_ge(gz_in, 16)
                turn_dve(dve, NT, T_Z, lambda j: row_tile(q_nat, j, 0, D), gain_z[:, :])
                dve.wait_ge(lr_split, 1)
                dve.tensor_tensor(w_lr_lo[:, :, :], w_lr[:, :, :], w_lr_hi[:, :, :].bitcast(F32), ALU.subtract).then_inc(lr_split, 1)
                for p in range(10):
                    split_lo(dve, P_Z + p, (P_Z + p) % 2)
        GH = 4
        CH = 64
        NCH = S // CH
        MIXC = 4 * P + 2
        qe = at("qe", [NT, KW], F32, ht)
        ke = at("ke", [NT, KW], F32, ht + 8192)
        kd = at("kd", [NT, 2, KW], F32, ht + 16384)
        la = at("la", [NT, KW], F32, ht + 49152)
        states = at("states", [2, NCH, P], F32, ht + 32768)
        mix_gain = at("mix_gain", [4, VW], F32, ring + 8192)
        scores = at("scores", [2, GH, P], F32, ht + 57344)
        ws = at("ws", [GH, P], F32, ht + 61440)
        ws_t = at("ws_t", [GH, P], F32, ht + 63488)
        to_end = at("to_end", [NT, KW], F32, ring + 16384)
        q_pad = at("q_pad", [2, GH, P], F32, ring + 24576)
        k_t = at("k_t", [2, 2, P], F32, ring + 28672)
        gate_wb = at("gate_wb", [KW], F32, xnr + 4096)
        mix_c = at("mix_c", [MIXC], F32, xnr + 5120)
        bs_nat = at("bs_nat", [P], F32, xnr + 7232)
        cum_mat, rev_mat, bound_hi, bound_lo = (mix_c[:, i * P:(i + 1) * P] for i in range(4))
        chunk_mat = mix_c[:, 4 * P:MIXC]
        neg_mean, v_sq, v_ms, v_rs, a_sq, a_ms, a_rs = (fixed(x, [NT]) for x in (
            "neg_mean", "v_sq", "v_ms", "v_rs", "a_sq", "a_ms", "a_rs"))
        o_sq, o_ms, o_rs = (fixed(x, [NT, GH]) for x in ("o_sq", "o_ms", "o_rs"))
        dec = fixed("dec", [2, NCH])
        bs_t = fixed("bs_t", [GH])
        (mix_in, ws_zero, states_zero, gates_done, la_step, la_done, cum_done, rev_done, ecum_done, erev_done, qe_done, ke_done,
         kd_done, dec_done, dec_ready, mean_step, vsq_done, vrs_step, vn_step, wst_done, wst_evac, gm_done, gm_evac, asq_done,
         ars_step, a_done, tq_done, tq_evac, sc_done, sc_step, upd_done, st_done, o_done, o_evac, ors_step, b_step,
         zg_done, kd2_done) = (sem(x) for x in (
             "mix_in", "ws_zero", "states_zero", "gates_done", "la_step", "la_done", "cum_done", "rev_done", "ecum_done",
             "erev_done", "qe_done", "ke_done", "kd_done", "dec_done", "dec_ready", "mean_step", "vsq_done", "vrs_step",
             "vn_step", "wst_done", "wst_evac", "gm_done", "gm_evac", "asq_done", "ars_step", "a_done", "tq_done", "tq_evac",
             "sc_done", "sc_step", "upd_done", "st_done", "o_done", "o_evac", "ors_step", "b_step", "zg_done", "kd2_done"))

        def two(x, g):
            return x[:, 2 * g:2 * g + 2, :].rearrange("p t n -> p (t n)")

        with nc.Block() as block:

            @block.sync
            def _(sp):
                sp.dma_start(gate_wb[0:RANK, :], t["gla_gate_w_2"][0]).then_inc(mix_in, 16)
                sp.dma_start(gate_wb[RANK:RANK + 1, :], t["gla_gate_b_2"][0:1, :]).then_inc(mix_in, 16)
                sp.dma_start(mix_c[:, :], t["k_mix"]).then_inc(mix_in, 16)
                sp.dma_start(ws[:, :, :], t["gmlp_ws_2"][0].rearrange("h i j -> i h j")).then_inc(mix_in, 16)
                sp.dma_start(bs_nat[0:GH, :], t["gmlp_bs_2"][0]).then_inc(mix_in, 16)
                for j, name in enumerate(("gmlp_ln_g_2", "gmlp_ln_b_2", "gmlp_out_g_2", "gla_out_g_2")):
                    sp.dma_start(mix_gain[:, j, :], t[name][0].partition_broadcast(P)).then_inc(mix_in, 16)

            @block.gpsimd
            def _(pool):
                pool.tensor_tensor(neg_mean[:, :], vsum[:, 0, :], vsum[:, 1, :], ALU.add).then_inc(mean_step, 1)
                pool.wait_ge(mean_step, 1)
                pool.tensor_scalar(neg_mean[:, :], neg_mean[:, :], -1.0 / VW, None, ALU.mult).then_inc(mean_step, 1)

                def roots(total, n_done, done_sem, step, ms, rs, width, calls=0):
                    pool.wait_ge(done_sem, n_done)
                    n = ms.shape[1]
                    pool.tensor_scalar(ms, total, 1.0 / width, EPS, ALU.mult, ALU.add).then_inc(step, 1)
                    pool.wait_ge(step, calls + 1)
                    pool.tensor_tensor(rs, ms, neg_half[:, 0:n], ALU.pow).then_inc(step, 1)

                roots(v_sq[:, :], NT, vsq_done, vrs_step, v_ms[:, :], v_rs[:, :], VW)
                for g in range(4):
                    pool.wait_ge(erev_done, g + 1)
                    part = slice(2 * g, 2 * g + 2)
                    pool.tensor_tensor(kd[0:CH, part, 0, :], to_end[0:CH, part, :], zk[0:CH, part, :], ALU.mult).then_inc(kd_done, 1)
                for j in range(NT):
                    if j == 0:
                        pool.wait_ge(mix_in, 144)
                    pool.tensor_tensor(zg[:, j, :], zg[:, j, :], mix_gain[:, 3, :], ALU.mult).then_inc(zg_done, 1)
                roots(a_sq[:, :], NT, asq_done, ars_step, a_ms[:, :], a_rs[:, :], VW)
                for g in range(2):
                    part = slice(4 * g, 4 * g + 4)
                    flat = [x[:, part, :].rearrange("p t h -> p (t h)") for x in (o_sq, o_ms, o_rs)]
                    roots(flat[0], 4 * g + 4, o_evac, ors_step, flat[1], flat[2], P, 2 * g)

            @block.tensor
            def _(pe):
                pe.wait_ge(mix_in, 144)
                pe.wait_ge(lr_evac, 2)
                for j in range(NT):
                    mm = pe.matmul(ps[:, j // 2, (j % 2) * KW:(j % 2 + 1) * KW], lr_t[0:RANK + 1, j * P:(j + 1) * P],
                                   gate_wb[0:RANK + 1, :], start=True, stop=True)
                    if j % 2:
                        mm.then_inc(gates_done, 1)
                pe.wait_ge(ws_zero, 1)
                for h in range(GH):
                    pe.transpose(ps[:, 4, h * P:(h + 1) * P], ws[:, h, :], ident[:, :])
                pe.transpose(ps[:, 5, 0:GH], bs_nat[0:GH, :], ident[0:GH, 0:GH]).then_inc(wst_done, 1)
                pe.wait_ge(wst_evac, 2)
                for mat, bank0, done_sem in ((cum_mat, 4, cum_done), (rev_mat, 0, rev_done)):
                    for g in range(4):
                        pe.wait_ge(la_done, g + 1)
                        pe.matmul(ps[:, bank0 + g, :], mat, two(la, g), start=True, stop=True).then_inc(done_sem, 1)
                pe.wait_ge(ecum_done, 2)
                for j in range(NT):
                    for q in range(2):
                        mm = pe.matmul(ps[:, 4, q * NCH + 2 * j:q * NCH + 2 * j + 2], la[:, j, q * P:(q + 1) * P], chunk_mat,
                                       start=True, stop=True)
                mm.then_inc(dec_done, 1)
                for n in range(2 * GH):
                    h, g = n % GH, n // GH
                    pe.wait_ge(erev_done, 4)
                    pe.wait_ge(vn_step, 8 * g + 8)
                    if n >= 4:
                        pe.wait_ge(gm_evac, n - 3)
                    pe.matmul(ps[:, n % 4, :].rearrange("p (t n) -> p t n", n=P), ws_t[:, h, :],
                              zv[:, 4 * g:4 * g + 4, h * P:(h + 1) * P], start=True, stop=True).then_inc(gm_done, 1)

                def prepare(j):
                    s = j % 2
                    if j == 0:
                        pe.wait_ge(qe_done, 4)
                        pe.wait_ge(ke_done, 4)
                        pe.wait_ge(kd_done, 4)
                        pe.wait_ge(kd2_done, 4)
                        pe.wait_ge(states_zero, 1)
                        pe.wait_ge(gm_evac, 8)
                        pe.wait_ge(dec_ready, 1)
                        pe.wait_ge(ecum_done, 8)
                    if j >= 2:
                        pe.wait_ge(tq_evac, j - 1)
                    for q in range(4):
                        mm = pe.transpose(ps[:, s, q * P:(q + 1) * P], (qe if q < 2 else ke)[:, j, (q % 2) * P:(q % 2 + 1) * P], ident[:, :])
                    mm.then_inc(tq_done, 1)
                    if j >= 2:
                        pe.wait_ge(st_done, 4 * (j - 1))
                    for c in range(2):
                        for h in range(GH):
                            dst = ps[CH * (h % 2):CH * (h % 2) + CH, 4 + s, (2 * c + h // 2) * P:(2 * c + h // 2 + 1) * P]
                            mm = pe.matmul(dst, kd[:, j, c, h * CH:(h + 1) * CH], zvb[:, j, h * P:(h + 1) * P], start=True, stop=True)
                    mm.then_inc(upd_done, 1)
                    pe.wait_ge(tq_evac, j + 1)
                    if j >= 2:
                        pe.wait_ge(sc_step, 2 * (j - 2) + 1)
                    for h in range(GH):
                        mm = pe.matmul(ps[:, 2 + s, h * P:(h + 1) * P], k_t[:, s, h // 2, :], q_pad[:, s, h, :],
                                       start=True, stop=True)
                    mm.then_inc(sc_done, 1)

                prepare(0)
                for j in range(NT):
                    s = j % 2
                    if j + 1 < NT:
                        prepare(j + 1)
                    pe.wait_ge(sc_step, 2 * j + 2)
                    pe.wait_ge(st_done, min(4 * j + 2, 30))
                    pe.wait_ge(states_zero, 1)
                    if j >= 2:
                        pe.wait_ge(o_evac, j - 1)
                    for h in range(GH):
                        dst = ps[:, 6 + s, h * P:(h + 1) * P]
                        pe.matmul(dst, scores[:, s, h, :], zvb[:, j, h * P:(h + 1) * P], start=True, stop=False)
                        for c in range(2):
                            dst = ps[CH * c:CH * c + CH, 6 + s, h * P:(h + 1) * P]
                            mm = pe.matmul(dst, q_pad[:, s, h, CH * c:CH * c + CH], states[:, h // 2, 2 * j + c, :],
                                           start=False, stop=True)
                    mm.then_inc(o_done, 1)

            @block.scalar
            def _(act):
                for step, fn, more in ((0, ACT.Abs, {}), (1, ACT.Exp, {"scale": -1.0}), (2, ACT.Ln, {"bias": 1.0})):
                    for g in range(4):
                        if step == 0:
                            act.wait_ge(gates_done, g + 1)
                        else:
                            act.wait_ge(la_step, 4 * step + g - 3)
                        src = ps[:, g, :] if step == 0 else two(la, g)
                        act.activation(two(la, g), src, fn, **more).then_inc(la_step, 1)
                act.wait_ge(wst_done, 1)
                act.activation(ws_t[:, :, :].rearrange("p h n -> p (h n)"), ps[:, 4, :], ACT.Copy).then_inc(wst_evac, 1)
                act.activation(bs_t[:, :], ps[:, 5, 0:GH], ACT.Copy).then_inc(wst_evac, 1)
                act.wait_ge(mean_step, 2)
                for j in range(NT):
                    if j:
                        act.wait_ge(vsq_done, j)
                    act.activation(junk[:, 0:VW], zv[:, j, :], ACT.Square, bias=neg_mean[:, j:j + 1],
                                   accum_out=v_sq[:, j:j + 1]).then_inc(vsq_done, 1)
                for g in range(4):
                    act.wait_ge(cum_done, g + 1)
                    act.activation(two(qe, g), ps[:, 4 + g, :], ACT.Exp).then_inc(ecum_done, 1)
                    act.activation(two(ke, g), ps[:, 4 + g, :], ACT.Exp, scale=-1.0).then_inc(ecum_done, 1)
                for g in range(4):
                    act.wait_ge(rev_done, g + 1)
                    act.activation(two(to_end, g), ps[:, g, :], ACT.Exp).then_inc(erev_done, 1)
                act.wait_ge(dec_done, 1)
                act.activation(dec[:, :, :].rearrange("p q c -> p (q c)"), ps[:, 4, 0:2 * NCH], ACT.Exp).then_inc(dec_ready, 1)

                def turned_qk(j):
                    act.wait_ge(tq_done, j + 1)
                    if j >= 2:
                        act.wait_ge(o_done, j - 1)
                    if j < 2:
                        act.wait_ge(states_zero, 1)
                    act.activation(k_t[:, j % 2, :, :].rearrange("p q n -> p (q n)"), ps[:, j % 2, 2 * P:4 * P], ACT.Copy)
                    for c in range(2):
                        rows = slice(CH * c, CH * c + CH)
                        last = act.activation(q_pad[rows, j % 2, c:GH:2, :], ps[rows, j % 2, 0:2 * P].rearrange("p (q n) -> p q n", n=P), ACT.Copy)
                    last.then_inc(tq_evac, 1)

                def gated_square(j):
                    act.wait_ge(gm_evac, 8)
                    act.wait_ge(asq_done, j) if j else act.wait_ge(vsq_done, NT)
                    act.activation(junk[:, 0:VW], zu[:, j, :], ACT.Square, accum_out=a_sq[:, j:j + 1]).then_inc(asq_done, 1)

                turned_qk(0)
                gated_square(0)
                for j in range(NT):
                    if j + 1 < NT:
                        turned_qk(j + 1)
                        gated_square(j + 1)
                    act.wait_ge(o_done, j + 1)
                    act.activation(zvb[:, j, :], ps[:, 6 + j % 2, :], ACT.Copy)
                    if j:
                        act.wait_ge(o_evac, j)
                    for h in range(GH):
                        last = act.activation(junk[:, VW + h * P:VW + (h + 1) * P], ps[:, 6 + j % 2, h * P:(h + 1) * P], ACT.Square,
                                              accum_out=o_sq[:, j, h:h + 1])
                    last.then_inc(o_evac, 1)

            @block.vector
            def _(dve):
                dve.wait_ge(mix_in, 144)
                dve.memset(ws[0:CH, :, CH:P], 0.0).then_inc(ws_zero, 1)
                dve.memset(states[:, :, 0, :], 0.0)
                for c in range(2):
                    rest = slice(CH * (1 - c), CH * (1 - c) + CH)
                    dve.memset(kd[rest, :, c, :], 0.0)
                    last = dve.memset(q_pad[rest, :, c:GH:2, :], 0.0)
                last.then_inc(states_zero, 1)
                for g in range(4):
                    dve.wait_ge(la_step, 8 + g + 1)
                    dve.scalar_tensor_tensor(out=two(la, g), in0=ps[:, g, :], scalar=0.0, in1=two(la, g),
                                             op0=ALU.min, op1=ALU.subtract).then_inc(la_done, 1)
                dve.wait_ge(vrs_step, 2)
                for j in range(NT):
                    dve.scalar_tensor_tensor(out=zv[:, j, :], in0=zv[:, j, :], scalar=neg_mean[:, j:j + 1], in1=mix_gain[:, 0, :],
                                             op0=ALU.add, op1=ALU.mult).then_inc(vn_step, 1)
                    dve.wait_ge(vn_step, 2 * j + 1)
                    dve.scalar_tensor_tensor(out=zv[:, j, :], in0=zv[:, j, :], scalar=v_rs[:, j:j + 1], in1=mix_gain[:, 1, :],
                                             op0=ALU.mult, op1=ALU.add).then_inc(vn_step, 1)
                for g in range(4):
                    dve.wait_ge(ecum_done, 2 * g + 2)
                    dve.scalar_tensor_tensor(out=two(qe, g), in0=two(zq, g), scalar=CH ** -0.5, in1=two(qe, g),
                                             op0=ALU.mult, op1=ALU.mult).then_inc(qe_done, 1)
                    dve.tensor_tensor(two(ke, g), two(ke, g), two(zk, g), ALU.mult).then_inc(ke_done, 1)
                for g in range(4):
                    dve.wait_ge(erev_done, g + 1)
                    part = slice(2 * g, 2 * g + 2)
                    dve.tensor_tensor(kd[CH:P, part, 1, :], to_end[CH:P, part, :], zk[CH:P, part, :], ALU.mult).then_inc(kd2_done, 1)
                for n in range(2 * GH):
                    h, g = n % GH, n // GH
                    u = zu[:, 4 * g:4 * g + 4, h * P:(h + 1) * P]
                    dve.wait_ge(gm_done, n + 1)
                    dve.wait_ge(wst_evac, 2)
                    dve.scalar_tensor_tensor(out=u, in0=ps[:, n % 4, :].rearrange("p (t n) -> p t n", n=P), scalar=bs_t[:, h:h + 1],
                                             in1=u, op0=ALU.add, op1=ALU.mult).then_inc(gm_evac, 1)

                def mask(j):
                    s = j % 2
                    dve.wait_ge(sc_done, j + 1)
                    if j >= 2:
                        dve.wait_ge(o_done, j - 1)
                    rows = ps[:, 2 + s, :].rearrange("p (h n) -> p h n", n=P)
                    dve.tensor_tensor(scores[:, s, :, :], rows, bcast(bound_hi, 1, GH), ALU.min).then_inc(sc_step, 1)
                    dve.wait_ge(sc_step, 2 * j + 1)
                    dve.tensor_tensor(scores[:, s, :, :], scores[:, s, :, :], bcast(bound_lo, 1, GH), ALU.max).then_inc(sc_step, 1)

                def advance(j):
                    for c in range(2):
                        n = 2 * j + c
                        if n == NCH - 1:
                            break
                        for q in range(2):
                            if n == 0 and q == 0:
                                dve.wait_ge(dec_ready, 1)
                                dve.wait_ge(states_zero, 1)
                            if c == 0 and q == 0:
                                dve.wait_ge(upd_done, j + 1)
                            if n:
                                dve.wait_ge(st_done, 2 * n - 1 + q)
                            dve.scalar_tensor_tensor(out=states[:, q, n + 1, :], in0=states[:, q, n, :], scalar=dec[:, q, n:n + 1],
                                                     in1=ps[:, 4 + j % 2, (2 * c + q) * P:(2 * c + q + 1) * P],
                                                     op0=ALU.mult, op1=ALU.add).then_inc(st_done, 1)

                for j in range(NT):
                    advance(j)
                    mask(j)
                dve.wait_ge(ars_step, 2)
                for j in range(NT):
                    dve.scalar_tensor_tensor(out=zu[:, j, :], in0=zu[:, j, :], scalar=a_rs[:, j:j + 1], in1=mix_gain[:, 2, :],
                                             op0=ALU.mult, op1=ALU.mult).then_inc(a_done, 1)
                dve.wait_ge(zg_done, NT)
                for j in range(NT):
                    dve.wait_ge(ors_step, 2 if j < 4 else 4)
                    row = zvb[:, j, :].rearrange("p (h n) -> p h n", n=P)
                    dve.tensor_tensor(row, row, bcast(o_rs[:, j, :], 2, P), ALU.mult).then_inc(b_step, 1)
                    dve.wait_ge(b_step, 2 * j + 1)
                    dve.tensor_tensor(zvb[:, j, :], zvb[:, j, :], zg[:, j, :], ALU.mult).then_inc(b_step, 1)
        x_res = at("x_res", [NT, D], F32, k_off)
        gain_m = at("gain_m", [D], F32, rope_at)
        gm_in, added = sem("gm_in"), sem("added")
        D_M = D_Z + 10 * NT
        with nc.Block() as block:

            @block.sync
            def _(sp):
                load_weights(sp, P_M + 1, panel_of(t["w_out_2"], PN))
                sp.dma_start(gain_m[:, :], t["post_mix_g_2"][0].partition_broadcast(P)).then_inc(gm_in, 16)
                sp.wait_ge(tr_done, T_M + NT)
                for j in range(NT):
                    sp.dma_start(x_res[:, j, :], x2_dram[j * P:(j + 1) * P, :]).then_inc(x_in[j], 16)
                for p in range(2, 4):
                    load_weights(sp, P_M + p, panel_of(t["w_out_2"], p * PN))
                load_weights(sp, P_G, panel_of(t["w_ff1_2"], 0))

            @block.gpsimd
            def _(pool):
                norm_pool(pool, NT, T_M, D)

            @block.tensor
            def _(pe):
                for j in range(NT):
                    pe.wait_ge(tl_done, T_M + j - 1)
                    for k in range(KT):
                        src = (zu if k < 4 else zvb)[:, j, (k % 4) * P:(k % 4 + 1) * P]
                        mm = pe.transpose(ps[:, 4 + 2 * (j % 2) + k // 4, (k % 4) * P:(k % 4 + 1) * P], src, ident[:, :])
                    mm.then_inc(tr_done, 1)
                for p in range(4):
                    for _ in rows_pe(pe, P_M + p, (P_M + p) % 2, NT, T_M, D_M + NT * p):
                        pass

            @block.scalar
            def _(act):
                split_hi(act, P_M, P_M % 2, used=(dense_done, D_M))
                turn_act(act, NT, T_M, None)
                for p in range(4):
                    if p < 3:
                        split_hi(act, P_M + p + 1, (P_M + p + 1) % 2, used=(dense_done, D_M + NT * p))
                    for j in range(NT):
                        act.wait_ge(dense_done, D_M + NT * p + j + 1)
                        act.activation(q_nat[:, j, p * PN:(p + 1) * PN], ps[:, j % 4, 0:PN], ACT.Copy).then_inc(dense_evac, 1)
                        if p == 3:
                            act.wait_ge(dense_evac, D_M + NT * p + j + 1)
                            act.wait_ge(ss_done, T_M + j)
                            act.wait_ge(ms_done, 2 * STAGE_OF[T_M])
                            act.activation(junk[:, :], q_nat[:, j, :], ACT.Square, accum_out=sumsq[:, j:j + 1]).then_inc(ss_done, 1)

            @block.vector
            def _(dve):
                split_lo(dve, P_M, P_M % 2)
                for j in range(NT):
                    dve.wait_ge(th_done, T_M + j + 1)
                    dve.tensor_tensor(ht_lo[:, :, j * P:(j + 1) * P], turned(j % 2),
                                      ht_hi[:, :, j * P:(j + 1) * P].bitcast(F32), ALU.subtract).then_inc(tl_done, 1)
                for p in range(1, 4):
                    split_lo(dve, P_M + p, (P_M + p) % 2)
                dve.wait_ge(gm_in, 16)
                for j in range(NT):
                    dve.wait_ge(rs_done, 2 * STAGE_OF[T_M] + 1 + j // 4)
                    dve.scalar_tensor_tensor(out=q_nat[:, j, :], in0=q_nat[:, j, :], scalar=rstd[:, j:j + 1], in1=gain_m[:, :],
                                             op0=ALU.mult, op1=ALU.mult).then_inc(xn_done, 1)
                    dve.wait_ge(xn_done, T_M + j + 1)
                    dve.wait_ge(x_in[j], 48)
                    dve.tensor_tensor(x_res[:, j, :], x_res[:, j, :], q_nat[:, j, :], ALU.add).then_inc(added, 1)
        gain_g = at("gain_g", [D], F32, k_off + 32768)
        gain_e = at("gain_e", [D], F32, rope_at)
        relu = at("relu", [2, S], F32, xnr)
        gg_in = sem("gg_in")
        hid_done, relu_done, sq_done, rh_done, rl_done, ff_done, ff_evac = (sem(x) for x in (
            "hid_done", "relu_done", "sq_done", "rh_done", "rl_done", "ff_done", "ff_evac"))
        e_done, out_stored = sem("e_done"), sem("out_stored")

        def p_hid(c):
            return P_G if isinstance(c, int) and c == 0 else P_G + 2 * c - 1

        def p_ff(c):
            return P_G + 2 * c + 2 if not (isinstance(c, int) and c == CH2 - 1) else P_END - 1

        S_DOWN = (P_G + 2) % 2

        def steps(eng, step):
            step(0)
            with eng.Fori(1, CH2 - 2) as c:
                step(c)
            step(CH2 - 2)

        with nc.Block() as block:

            @block.sync
            def _(sp):
                sp.dma_start(gain_g[:, :], t["pre_ff_g_2"][0].partition_broadcast(P)).then_inc(gg_in, 16)
                sp.dma_start(gain_e[:, :], t["post_ff_g_2"][0].partition_broadcast(P)).then_inc(gg_in, 16)
                load_weights(sp, P_G + 1, panel_of(t["w_ff1_2"], PN))

                def step(c, more=True):
                    load_weights(sp, p_ff(c), down_panel(t["w_ff2_2"], c * PN), stage_down())
                    if more:
                        load_weights(sp, p_hid(c + 2), panel_of(t["w_ff1_2"], (c + 2) * PN))
                with sp.Fori(0, CH2 - 2) as c:
                    step(c)
                step(CH2 - 2, False)
                step(CH2 - 1, False)
                for j in range(NT):
                    sp.wait_ge(e_done, 2 * j + 2)
                    sp.dma_start(out[0, j * P:(j + 1) * P, :], q_nat[:, j, :]).then_inc(out_stored, 16)
                sp.wait_ge(out_stored, 16 * NT)

            @block.gpsimd
            def _(pool):
                norm_pool(pool, NT, T_G, D)
                norm_pool(pool, NT, T_E, D)

            @block.tensor
            def _(pe):
                turn_pe(pe, NT, T_G)
                pe.wait_ge(tl_done, T_G + NT)

                def hidden(c, slot):
                    def free(b):
                        if not isinstance(c, int) or c > 0:
                            pe.wait_ge(relu_done, 4 * c + b - 3)
                    features_pe(pe, p_hid(c), slot, c, 0, hid_done, free)

                hidden(0, P_G % 2)

                def step(c):
                    hidden(c + 1, 1 - S_DOWN)
                    down_pe(pe, p_ff(c), S_DOWN, c, rl_done, ff_done, ff_evac)
                steps(pe, step)
                down_pe(pe, P_END - 1, 1 - S_DOWN, CH2 - 1, rl_done, ff_done, ff_evac)

            @block.scalar
            def _(act):
                norm_sums(act, NT, T_G, lambda j: x_res[:, j, :], lambda e, j: None)
                split_hi(act, P_G, P_G % 2, used=(dense_done, D_M + 3 * NT))
                turn_act(act, NT, T_G, None)
                split_hi(act, P_G + 1, (P_G + 1) % 2, used=(dense_done, D_M + 4 * NT))

                def relus(c):
                    for b in range(4):
                        act.wait_ge(hid_done, 4 * c + b + 1)
                        if not isinstance(c, int) or c > 0:
                            act.wait_ge(rl_done, 4 * c + b - 3)
                        elif b == 0:
                            act.wait_ge(tr_done, T_G + NT)
                        act.activation(quarter(relu, b), ps[:, b, :], ACT.Relu).then_inc(relu_done, 1)

                relus(0)

                def step(c):
                    used = (ff_done, 16 * c) if not isinstance(c, int) or c > 0 else (hid_done, 4)
                    split_hi(act, p_ff(c), S_DOWN, used=used)
                    act_split_hi(act, c, relu, sq_done, rh_done, ff_done)
                    relus(c + 1)
                    split_hi(act, P_G + 2 * c + 3, 1 - S_DOWN, used=(hid_done, 4 * c + 8))
                steps(act, step)
                act_split_hi(act, CH2 - 1, relu, sq_done, rh_done, ff_done)
                norm_sums(act, NT, T_E, lambda j: q_nat[:, j, :], lambda e, j: e.wait_ge(ff_evac, 16 * (CH2 - 1) + 2 * j + 2))

            @block.vector
            def _(dve):
                dve.wait_ge(gg_in, 32)
                turn_dve(dve, NT, T_G, lambda j: row_tile(x_res, j, 0, D), gain_g[:, :])
                split_lo(dve, P_G, P_G % 2)
                split_lo(dve, P_G + 1, (P_G + 1) % 2)

                def squares(c):
                    for b in range(4):
                        dve.wait_ge(relu_done, 4 * c + b + 1)
                        dve.tensor_tensor(quarter(relu, b), quarter(relu, b), quarter(relu, b), ALU.mult).then_inc(sq_done, 1)

                def step(c):
                    squares(c)
                    split_lo(dve, p_ff(c), S_DOWN)
                    act_split_lo(dve, c, relu, rh_done, rl_done)
                    first = isinstance(c, int) and c == 0
                    down_dve(dve, c, range(4), ff_done, ff_evac, first)
                    split_lo(dve, P_G + 2 * c + 3, 1 - S_DOWN)
                    down_dve(dve, c, range(4, 2 * NT), ff_done, ff_evac, first)
                steps(dve, step)
                squares(CH2 - 1)
                act_split_lo(dve, CH2 - 1, relu, rh_done, rl_done)
                down_dve(dve, CH2 - 1, range(2 * NT), ff_done, ff_evac)
                dve.wait_ge(gg_in, 32)
                for j in range(NT):
                    dve.wait_ge(rs_done, 2 * STAGE_OF[T_E] + 1 + j // 4)
                    dve.scalar_tensor_tensor(out=q_nat[:, j, :], in0=q_nat[:, j, :], scalar=rstd[:, j:j + 1], in1=gain_e[:, :],
                                             op0=ALU.mult, op1=ALU.mult).then_inc(e_done, 1)
                    dve.wait_ge(e_done, 2 * j + 1)
                    dve.tensor_tensor(q_nat[:, j, :], q_nat[:, j, :], x_res[:, j, :], ALU.add).then_inc(e_done, 1)


def constants():
    P=128
    pick=np.zeros((2,P,P),np.float32)
    for g in range(4):
        pick[0,32*g,:]=1; pick[1,32*g+1,:]=1
    tok=np.arange(1024)
    q=np.arange(16,dtype=np.float32)
    inv=(1.0/(np.float32(10000.0)**(q/np.float32(16)))).astype(np.float32)
    rope=np.zeros((P,2,8,64),np.float32)
    for half,pos in enumerate((tok//64,tok%64)):
        ang=pos.astype(np.float32)[:,None]*inv[None]
        c=np.cos(ang).astype(np.float32); s=np.sin(ang).astype(np.float32)
        c=c.reshape(8,P,16).transpose(1,0,2); s=s.reshape(8,P,16).transpose(1,0,2)
        for p2 in range(2):
            rope[:,0,:,half*32+p2*16:half*32+p2*16+16]=c
            rope[:,1,:,half*32+p2*16:half*32+p2*16+16]=s if p2 else -s
    BIG=np.float32(1e30)
    rm=np.zeros((P,9),np.float32); rm[:64,8]=BIG; rm[64:,0]=BIG
    qc=np.arange(P)%64; kc=np.arange(64); cs=np.clip(qc-8,0,48)
    cm=np.where((kc[None]>=cs[:,None])&(kc[None]<cs[:,None]+16),0,BIG).astype(np.float32)
    i=np.arange(P)[:,None]; j=np.arange(P)[None]
    band=np.zeros((P,3,P),np.float32); band[:,0]=np.where(j>=i,0,BIG); band[:,2]=np.where(j<=i,0,BIG)
    same=(i//64)==(j//64)
    mix=np.zeros((P,4*P+2),np.float32)
    mix[:,0:P]=np.where(same&(i<=j),1/16,0); mix[:,P:2*P]=np.where(same&(i>j),1/16,0)
    keep=same&(i<=j); FM=np.finfo(np.float32).max
    mix[:,2*P:3*P]=np.where(keep,FM,0); mix[:,3*P:4*P]=np.where(keep,-FM,0)
    mix[:64,4*P]=1/16; mix[64:,4*P+1]=1/16
    return {"k_mix":mix,"k_ident":np.eye(P,dtype=np.float32),"k_pick":pick,"k_rope":rope,"k_row_mask":rm,"k_col_mask":cm,"k_band":band}


NAMES = ["x", "c", "ctx", "c_ctx", "w_mod", "b_mod", "norm1_g", "w_in", "qn_a", "kn_a", "sink_a", "qn_b", "kn_b", "rpb_b",
         "on_a", "on_b", "w_out", "norm2_g", "w_gate", "w_up", "w_down", "pre_mix_g_2", "w_in_2", "gmlp_ln_g_2", "gmlp_ln_b_2",
         "gmlp_ws_2", "gmlp_bs_2", "gmlp_out_g_2", "gla_gate_w_2", "gla_gate_b_2", "gla_out_g_2", "w_out_2", "post_mix_g_2",
         "pre_ff_g_2", "w_ff1_2", "w_ff2_2", "post_ff_g_2"]


def kernel(**inputs):
    import concourse.bacc as bacc
    from concourse.bass_utils import run_bass_kernel_spmd

    nc = bacc.Bacc("TRN2", target_bir_lowering=False, num_devices=1)
    arrays = {name: np.ascontiguousarray(inputs[name]) for name in NAMES}
    arrays.update(constants())
    t = {name: nc.dram_tensor(name, a.shape, F32, kind="ExternalInput").ap() for name, a in arrays.items()}
    out = nc.dram_tensor("out", (1, S, D), F32, kind="ExternalOutput").ap()
    program(nc, t, out)
    r = run_bass_kernel_spmd(nc, [arrays], core_ids=[0])
    return r.results[0]["out"]
```

```python
from contextlib import ExitStack

import numpy as np

import concourse.bass as bass
from concourse import mybir

F32 = mybir.dt.float32
F32R = mybir.dt.float32r
ALU = mybir.AluOpType
ACT = mybir.ActivationFunctionType
AX_X = mybir.AxisListType.X
ds = bass.ds

P = 128
D = 1024
S = 1024
CTX = 256
NT = S // P
NC = CTX // P
KT = D // P
HD = 64
A_KV = 128
AW = 512
KVW = A_KV + AW
GRID = 64
PN = 256
F1 = 2816
F2 = 4096
CH1, CH2 = F1 // PN, F2 // PN
EPS = 1e-6
BIG = 1e30
PAIRS = 4
RB = 31
NE = 14
NI = 9
RPW = (NE - 1) * RB + GRID
RPH = 15 * RB
RPAD = 64


def bcast(ap, axis, n):
    shape = list(ap.shape)
    return ap.unsqueeze(axis).broadcast_to(shape[:axis] + [n] + shape[axis:])


def program(nc, t, out):
    BASE, TOP = 16512, 229344
    place = [BASE]

    def at(name, shape, dt, offset):
        return nc.alloc_sbuf_tensor_at(name, [P] + shape, dt, offset=offset)

    def region(size):
        offset = place[0]
        place[0] += (size + 31) // 32 * 32
        assert place[0] <= TOP, (place[0], TOP)
        return offset

    def fixed(name, shape, dt=F32):
        n = 4
        for x in shape:
            n *= x
        return at(name, shape, dt, region(n))

    ident = fixed("ident", [P])
    pick_x = fixed("pick_x", [P])
    pick_c = fixed("pick_c", [P])
    head_gain = fixed("head_gain", [4, HD])
    neg_sink = fixed("neg_sink", [8])
    row_mask = fixed("row_mask", [NI])
    col_mask = fixed("col_mask", [GRID])
    neg_half = fixed("neg_half", [40])
    cond = fixed("cond", [2, KT])
    sumsq = fixed("sumsq", [16])
    msq = fixed("msq", [16])
    rstd = fixed("rstd", [16])
    junk = at("junk", [D], mybir.dt.bfloat16, region(2 * D))
    hsum = fixed("hsum", [10, 4])
    hms = fixed("hms", [10, 4])
    hrs = fixed("hrs", [10, 4])
    rope_at = place[0]
    rope = fixed("rope", [2, NT, HD])
    mod_b = fixed("mod_b", [PN])
    zero_row = fixed("zero_row", [RPAD])
    ring = region(40 * 1024)
    ht = region(64 * 1024)
    nat = region(4 * (NT * D + 2 * 10 * KVW))
    xnr = region(2 * D * 4)

    stage = at("stage", [2048], F32, ring)
    w_hi = at("w_hi", [2, 2048], F32R, ring + 8192)
    w_lo = at("w_lo", [2, 2048], F32R, ring + 8192 * 3)
    ht_hi = at("ht_hi", [KT, S], F32R, ht)
    ht_lo = at("ht_lo", [KT, S], F32R, ht + 32768)
    mod_w = at("mod_w", [8, 2048], F32, ht)
    xn = at("xn", [2, D], F32, xnr)
    rot = at("rot", [4, PN], F32, xnr)
    hsq = fixed("hsq", [2, PN])
    mod_q = at("mod_q", [PN], F32, xnr + 6144)
    mod_row = at("mod_row", [PN], F32, xnr + 7168)
    mod_part = at("mod_part", [2, PN], F32, xnr)
    q_nat = at("q_nat", [NT, D], F32, nat)
    k_off = nat + NT * D * 4
    v_off = k_off + 10 * KVW * 4
    k_nat = at("k_nat", [10, KVW], F32, k_off)
    v_nat = at("v_nat", [10, KVW], F32, v_off)
    mod_1 = at("mod_1", [4, D], F32, k_off)
    norm1 = at("norm1", [D], F32, v_off)
    ctx_in = at("ctx_in", [NC, D], F32, v_off + 4096)
    shift_x, gain_x, shift_c, gain_c = (mod_1[:, j, :] for j in range(4))
    kt = at("kt", [10, S + CTX], F32R, ht)
    probs = at("probs", [2, CTX + NI * GRID], F32, ring)
    prob_t = [at("prob_t0", [2, 7 * P], F32, ring + 6656), at("prob_t1", [2, 7 * P], F32, xnr)]
    masked = at("masked", [2, CTX + NI * GRID], F32, ring + 13824)
    edge = at("edge", [2, NE, GRID], F32, ring + 20480)
    inner = at("inner", [2, CTX + NI * GRID], F32, ring + 27648)
    o_t = at("o_t", [P], F32, ring + 34304)
    small = at("small", [2, 8], F32, ring + 34816)
    v_pair = at("v_pair", [10, P], F32, ring + 34880)
    den = at("den", [2, 2, 4], F32, ring + 40000)
    dsum = at("dsum", [2], F32, ring + 40064)
    rden = at("rden", [2, 2], F32, ring + 40096)
    band = at("band", [9, P], F32, ht + 59392)
    q_split = at("q_split", [2, 2, 2, P], F32, ht + 51200)
    q_t = at("q_t", [2, 2, 2, P], F32R, ht + 55296)
    k_split = at("k_split", [2, 10, P], F32, ring)
    raw_bias = at("raw_bias", [8, RPW], F32, k_off)
    x_again = at("x_again", [2, NT, PN], F32, k_off)
    mod_2 = at("mod_2", [4, D], F32, k_off + 16384)
    on_ab = at("on_ab", [D], F32, k_off + 32768)
    norm2 = at("norm2", [D], F32, k_off + 36864)
    silu = at("silu", [2, S], F32, k_off)
    act_f = at("act_f", [2, S], F32, k_off + 8192)
    act_hi = at("act_hi", [2, S], F32R, k_off + 32768)
    act_lo = at("act_lo", [2, S], F32R, k_off + 32768 + 8192)

    rpb_pad = nc.dram_tensor("rpb_pad", [RPAD + 8 * RPH + RPAD], F32, kind="Internal").ap()
    RPL = RPAD + 8 * RPH + RPAD
    rpb_skew = nc.dram_tensor("rpb_skew", [GRID * (RPL + 1)], F32, kind="Internal").ap()
    mod_dram = nc.dram_tensor("mod_dram", [4, D], F32, kind="Internal").ap()

    ctx = ExitStack()
    with ctx:
        ps = ctx.enter_context(nc.psum_tensor("ps", [P, 8, 512], F32))

        def sem(name):
            return ctx.enter_context(nc.semaphore(name))

        consts_in = sem("consts_in")
        mod1_in = sem("mod1_in")
        modw_in = [sem(f"modw_in{j}") for j in range(8)]
        ctx_landed = sem("ctx_landed")
        x_in = [sem(f"x_in{j}") for j in range(NT)]
        cond_in, pe_consts_in = sem("cond_in"), sem("pe_consts_in")
        banks_clear = sem("banks_clear")
        ready = sem("ready")
        cond_done = sem("cond_done")
        part_done, part_evac, mod_done, mod_added = sem("part_done"), sem("part_evac"), sem("mod_done"), sem("mod_added")
        w_landed, w_hi_done, w_lo_done = sem("w_landed"), sem("w_hi_done"), sem("w_lo_done")
        ss_done, ms_done, rs_done = sem("ss_done"), sem("ms_done"), sem("rs_done")
        xs_done = sem("xs_done")
        xn_done, tr_done, th_done, tl_done = sem("xn_done"), sem("tr_done"), sem("th_done"), sem("tl_done")
        dense_done, dense_evac = sem("dense_done"), sem("dense_evac")
        hsum_done, hms_done, hrs_done = sem("hsum_done"), sem("hms_done"), sem("hrs_done")
        modb_in, neg_done = sem("modb_in"), sem("neg_done")
        hn_done, hg_done, roped = sem("hn_done"), sem("hg_done"), sem("roped")
        skewed, pad_done, bias_in = sem("skewed"), sem("pad_done"), sem("bias_in")
        mod2_landed, modx_part, modx_q, modx_row, modx_b, modx_out, modx_stored = (
            sem(x) for x in ("mod2_landed", "modx_part", "modx_q", "modx_row", "modx_b", "modx_out", "modx_stored"))
        ks_hi, ks_lo, kt_tr, kt_a, kt_v = sem("ks_hi"), sem("ks_lo"), sem("kt_tr"), sem("kt_a"), sem("kt_v")
        band_in = sem("band_in")
        (qs_step, qt_done, qt_ready, s_done, min_done, exp_done, pt0_done, pt1_done, pt0_evac, pt1_evac, vp_ready,
         pv_done, ot_evac, on_done, on_evac, dn_step, tab_done) = (sem(x) for x in (
             "qs_step", "qt_done", "qt_ready", "s_done", "min_done", "exp_done", "pt0_done", "pt1_done",
             "pt0_evac", "pt1_evac", "vp_ready", "pv_done", "ot_evac", "on_done", "on_evac", "dn_step", "tab_done"))

        P_C, P_X, P_O = 0, 5, 14
        P_F = 18
        P_Z = P_F + 3 * CH1
        P_M = P_Z + 10
        P_G = P_M + 4
        P_END = P_G + 2 * CH2
        T_C, T_X, T_O, T_H, T_Z, T_M, T_G, T_E = 0, 2, 10, 18, 26, 34, 42, 50

        def panel_of(w, col):
            return w[0].rearrange("(k p) n -> p k n", p=P)[:, :, col:col + PN] if isinstance(col, int) else \
                w[0].rearrange("(k p) n -> p k n", p=P)[:, :, ds(col, PN)]

        def stage_up():
            return stage[:, :].rearrange("p (k n) -> p k n", k=KT)

        CTX_COLS = [512, 1280, 1536, 1792, 2048]

        done = ExitStack()
        block = done.enter_context(nc.Block())

        def load_weights(sp, p, source, dst=None):
            if not isinstance(p, int) or p > 0:
                sp.wait_ge(w_lo_done, p)
            sp.dma_start(stage_up() if dst is None else dst, source).then_inc(w_landed, 16)

        def mod_panel(m):
            return t["w_mod"][0].rearrange("(p k) n -> p k n", k=KT)[:, :, 2 * D + m * PN:2 * D + (m + 1) * PN]

        def mod_flat(m):
            return mod_dram.rearrange("a b -> (a b)")[m * PN:(m + 1) * PN].unsqueeze(0)

        def sync_x(sp):
            for p in range(8):
                for m in (2 * p, 2 * p + 1):
                    if m == 2 * p:
                        sp.wait_ge(w_lo_done, P_X + p + 2)
                    else:
                        sp.wait_ge(modx_part, m)
                    sp.dma_start(stage_up(), mod_panel(m)).then_inc(mod2_landed, 16)
                    if m:
                        sp.wait_ge(modx_row, m)
                        sp.dma_start(mod_flat(m - 1), mod_row[0:1, :]).then_inc(modx_stored, 16)
                    sp.dma_start(mod_b[0:1, :], t["b_mod"][0:1, 2 * D + m * PN:2 * D + (m + 1) * PN]).then_inc(modb_in, 16)
                if p < 7:
                    sp.wait_ge(modx_part, 2 * p + 2)
                    sp.dma_start(stage_up(), panel_of(t["w_in"], (p + 2) * PN)).then_inc(w_landed, 16)
            sp.wait_ge(modx_row, 16)
            sp.dma_start(mod_flat(15), mod_row[0:1, :]).then_inc(modx_stored, 16)


        def normed(before):
            return before - NT if before >= T_G else before

        def norm_tile(pool, j, before, width, groups=1):
            before = normed(before)
            cols = slice(groups * j, groups * j + groups)
            pool.wait_ge(ss_done, before + j + 1)
            if before + j == 0:
                pool.wait_ge(ready, 1)
            pool.tensor_scalar(msq[:, cols], sumsq[:, cols], 1.0 / width, EPS, ALU.mult, ALU.add).then_inc(ms_done, 1)
            pool.wait_ge(ms_done, before + j + 1)
            if before:
                pool.wait_ge(xn_done, before)
            pool.tensor_tensor(rstd[:, cols], msq[:, cols], neg_half[:, cols], ALU.pow).then_inc(rs_done, 1)

        def sum_tile(act, j, before, source):
            before = normed(before)
            if before + j:
                act.wait_ge(ss_done, before + j)
            if j == 0 and before:
                act.wait_ge(ms_done, before)
            act.activation(junk[:, :], source, ACT.Square, accum_out=sumsq[:, j:j + 1]).then_inc(ss_done, 1)

        def scale_tile(dve, j, b, before, source, gain, shifted):
            dve.wait_ge(rs_done, normed(before) + j + 1)
            if before:
                dve.wait_ge(tr_done, before + j - 1)
            dve.scalar_tensor_tensor(out=xn[:, b, :], in0=source, scalar=rstd[:, j:j + 1] if isinstance(j, int) else rstd[:, ds(j, 1)],
                                     in1=gain, op0=ALU.mult, op1=ALU.mult).then_inc(xs_done if shifted else xn_done, 1)

        def shift_tile(pool, j, shifts, shift):
            pool.wait_ge(xs_done, shifts + j + 1)
            pool.tensor_tensor(xn[:, j % 2, :], xn[:, j % 2, :], shift, ALU.add).then_inc(xn_done, 1)

        def turned(b, bank0=4):
            return ps[:, bank0 + 2 * b:bank0 + 2 * b + 2, :].rearrange("p a (k n) -> p (a k) n", n=P)

        def turn_tile(pe, j, b, before, bank0=4):
            pe.wait_ge(xn_done, normed(before) + j + 1)
            if before:
                pe.wait_ge(tl_done, before + j - 1)
            for k in range(KT):
                mm = pe.transpose(ps[:, bank0 + 2 * b + k // 4, (k % 4) * P:(k % 4 + 1) * P],
                                  xn[:, b, k * P:(k + 1) * P], ident[:, :])
            mm.then_inc(tr_done, 1)

        def tile_cols(x, j):
            return x[:, :, j * P:(j + 1) * P] if isinstance(j, int) else x[:, :, ds(j * P, P)]

        def turned_hi(act, j, b, before, bank0=4, at=0):
            act.wait_ge(tr_done, before + 1)
            act.wait_ge(tr_done, before + j + 1)
            act.activation(tile_cols(ht_hi, j + at), turned(b, bank0), ACT.Copy).then_inc(th_done, 1)

        def turned_lo(dve, j, b, before, bank0=4, at=0):
            dve.wait_ge(th_done, before + j + 1)
            dve.tensor_tensor(tile_cols(ht_lo, j + at), turned(b, bank0), tile_cols(ht_hi, j + at).bitcast(F32), ALU.subtract).then_inc(tl_done, 1)

        def norms_pool(pool, n, before, width, groups=1, shift=None, shifts=0):
            for j in range(n + 1):
                if j < n:
                    norm_tile(pool, j, before, width, groups)
                if j and shift is not None:
                    shift_tile(pool, j - 1, shifts, shift)

        def turn_pe(pe, n, before):
            if before == 0:
                pe.wait_ge(mod_added, 16)
            with pe.Fori(0, n // 2) as i:
                for b in range(2):
                    turn_tile(pe, 2 * i + b, b, before)

        def turn_act(act, n, before, used, at=0):
            if used is not None:
                act.wait_ge(*panel_used(used))
            with act.Fori(0, n // 2) as i:
                for b in range(2):
                    turned_hi(act, 2 * i + b, b, before, at=at)

        def turn_dve(dve, n, before, source, gain, shifted=False, at=0):
            for b in range(2):
                scale_tile(dve, b, b, before, source(b), gain, shifted)
            if n > 2:
                with dve.Fori(1, n // 2) as i:
                    for b in range(2):
                        j = 2 * i + b
                        turned_lo(dve, j - 2, b, before)
                        scale_tile(dve, j, b, before, source(j), gain, shifted)
            for b in range(2):
                turned_lo(dve, n - 2 + b, b, before, at=at)

        def panel_used(p):
            if p < P_X:
                return dense_done, NC * (p + 1)
            if p < P_O:
                return dense_done, D_X + NT * (p - P_X + 1)
            if p < P_F:
                return dense_done, D_O + NT * (p - P_O + 1)
            return later_used(p)

        def split_hi(act, p, slot, used=None, scaled=None):
            act.wait_ge(w_landed, 16 * (p + 1))
            if used is None and p >= 2:
                used = panel_used(p - 2)
            if used is not None:
                act.wait_ge(*used)
            if scaled is not None:
                act.wait_ge(w_scaled, scaled)
            act.activation(w_hi[:, slot, :], stage[:, :], ACT.Copy).then_inc(w_hi_done, 1)

        def split_lo(dve, p, slot):
            dve.wait_ge(w_hi_done, p + 1)
            dve.tensor_tensor(w_lo[:, slot, :], stage[:, :], w_hi[:, slot, :].bitcast(F32), ALU.subtract).then_inc(w_lo_done, 1)

        def rows_pe(pe, p, slot, tiles, tiles_before, d0, lag=4, at=0):
            pe.wait_ge(w_lo_done, p + 1)
            wh, wl = (w[:, slot, :].rearrange("p (k n) -> p k n", k=KT) for w in (w_hi, w_lo))
            for j in range(tiles):
                pe.wait_ge(tl_done, tiles_before + j + 1)
                if not isinstance(d0, int) or d0 + j >= lag:
                    pe.wait_ge(dense_evac, d0 + j + 1 - lag)
                bank = bank_of(j)
                for k in range(KT):
                    a, b = (x[:, k, (at + j) * P:(at + j + 1) * P] for x in (ht_hi, ht_lo))
                    pe.matmul(bank, a, wh[:, k, :], start=(k == 0), stop=False)
                    pe.matmul(bank, a, wl[:, k, :], start=False, stop=False)
                    mm = pe.matmul(bank, b, wh[:, k, :], start=False, stop=(k == KT - 1))
                mm.then_inc(dense_done, 1)
                yield j

        def bank_of(j):
            return ps[:, j % 4, 0:PN]

        X_PANELS = [("q", 0, PN, 0, True), ("q", PN, PN, 0, True), ("k", 0, A_KV, 1, True),
                    ("q", AW, PN, 2, False), ("q", AW + PN, PN, 2, False),
                    ("k", A_KV, PN, 3, False), ("k", A_KV + PN, PN, 3, False),
                    ("v", A_KV, PN, None, False), ("v", A_KV + PN, PN, None, False)]
        C_PANELS = [("k", 0, A_KV, 1, False), ("k", A_KV, PN, 3, False), ("k", A_KV + PN, PN, 3, False),
                    ("v", A_KV, PN, None, False), ("v", A_KV + PN, PN, None, False)]
        D_X = NC * len(C_PANELS)
        D_O = D_X + NT * len(X_PANELS)

        def each_tile(eng, tiles):
            if tiles < 4:
                for j in range(tiles):
                    yield j, j
            else:
                with eng.Fori(0, tiles // 4) as i:
                    for b in range(4):
                        yield 4 * i + b, b

        def heads_act(act, panel, p_next, tiles, t0, d0, sq0):
            kind, col, width, gain, _ = panel
            if p_next is not None:
                split_hi(act, p_next, p_next % 2)
            for j, b in each_tile(act, tiles):
                act.wait_ge(dense_done, d0 + 1)
                act.wait_ge(dense_done, d0 + j + 1)
                bank = ps[:, b, 0:PN]
                if kind == "v":
                    act.activation(row_tile(v_nat, t0 + j, col, PN), bank, ACT.Copy).then_inc(dense_evac, 1)
                    continue
                if width < PN:
                    act.activation(row_tile(v_nat, t0 + j, 0, A_KV), ps[:, b, A_KV:PN], ACT.Copy)
                act.activation(row_tile(q_nat if kind == "q" else k_nat, t0 + j, col, width), ps[:, b, 0:width], ACT.Copy)
                if not (isinstance(j, int) and sq0 + j < 2):
                    act.wait_ge(hsum_done, sq0 + j - 1)
                act.activation(hsq[:, b % 2, 0:width], ps[:, b, 0:width], ACT.Square).then_inc(dense_evac, 1)

        def row_tile(nat, j, col, width):
            if isinstance(j, int):
                return nat[:, j, col:col + width]
            return nat[:, ds(j, 1), col:col + width].squeeze(1)

        def head_rows(panel, tiles, t0):
            kind, col, width, _, _ = panel
            return (q_nat if kind == "q" else k_nat)[:, t0:t0 + tiles, col:col + width].rearrange("p t (h d) -> p t h d", d=HD)

        def heads_scale(dve, panel, tiles, t0, n):
            rows = head_rows(panel, tiles, t0)
            dve.wait_ge(hrs_done, n + 1)
            dve.tensor_tensor(rows, rows, bcast(hrs[:, 0:tiles, 0:panel[2] // HD], 3, HD), ALU.mult).then_inc(hn_done, 1)

        def heads_dve(dve, panel, before, p_next, tiles, t0, d0, sq0, n, mods=None):
            if p_next is not None:
                split_lo(dve, p_next, p_next % 2)
            if before is not None:
                heads_scale(dve, before, tiles, t0, n - 1)
            kind, col, width, gain, _ = panel
            for j in range(tiles):
                if kind != "v":
                    dve.wait_ge(dense_evac, d0 + j + 1)
                    if j == 0 and n:
                        dve.wait_ge(hms_done, n)
                    dve.tensor_reduce(hsum[:, j, 0:width // HD],
                                      hsq[:, j % 2, 0:width].rearrange("p (h d) -> p h d", d=HD),
                                      AX_X, ALU.add).then_inc(hsum_done, 1)
                if mods is not None and j >= 4:
                    mods(j)

        pool_steps = [0]

        def pool_heads(pool, panel, tiles, t0, n, sums):
            pool_roots(pool, panel, tiles, n, sums)
            pool_gains(pool, panel, tiles, t0, n)

        def pool_roots(pool, panel, tiles, n, sums):
            H = panel[2] // HD
            pool.wait_ge(hsum_done, sums)
            if n:
                pool.wait_ge(hrs_done, n)
            pool.tensor_scalar(hms[:, 0:tiles, 0:H], hsum[:, 0:tiles, 0:H], 1.0 / HD, EPS, ALU.mult, ALU.add).then_inc(hms_done, 1)
            pool.wait_ge(hms_done, n + 1)
            if n:
                pool.wait_ge(hn_done, n)
            half = neg_half[:, 0:tiles * H].rearrange("p (t h) -> p t h", h=H)
            pool.tensor_tensor(hrs[:, 0:tiles, 0:H], hms[:, 0:tiles, 0:H], half, ALU.pow).then_inc(hrs_done, 1)

        def pool_gains(pool, panel, tiles, t0, n):
            kind, col, width, gain, turn = panel
            H = width // HD
            rows = head_rows(panel, tiles, t0)
            pool.wait_ge(hn_done, n + 1)
            if n == 0:
                pool.wait_ge(neg_done, 3)
            pool.tensor_tensor(rows, rows, bcast(bcast(head_gain[:, gain, :], 1, tiles), 2, H), ALU.mult).then_inc(hg_done, 1)
            if not turn:
                return
            for g in range(0, tiles, 4):
                if g == 0:
                    pool.wait_ge(hg_done, n + 1)
                    pool.wait_ge(tl_done, T_O)
                if pool_steps[0]:
                    pool.wait_ge(roped, pool_steps[0])
                part = rows[:, g:g + 4]
                out4 = rot[:, :, 0:width].rearrange("p t (h d) -> p t h d", d=HD)
                for half in range(2):
                    for pos in range(2):
                        a, b = half * 32 + pos * 16, half * 32 + (1 - pos) * 16
                        pool.tensor_tensor(out4[:, :, :, a:a + 16], part[:, :, :, b:b + 16],
                                           bcast(rope[:, 1, g:g + 4, a:a + 16], 2, H), ALU.mult).then_inc(roped, 1)
                pool.wait_ge(roped, pool_steps[0] + 4)
                pool.tensor_tensor(part, part, bcast(rope[:, 0, g:g + 4, :], 2, H), ALU.mult).then_inc(roped, 1)
                pool.wait_ge(roped, pool_steps[0] + 5)
                pool.tensor_tensor(part, part, out4, ALU.add).then_inc(roped, 1)
                pool_steps[0] += 6

        ROPED = 6 * 2 * 3

        def modx_pe_part(pe, m, first):
            pe.wait_ge(mod2_landed, 16 * (m + 1))
            if first:
                pe.wait_ge(tl_done, T_O)
            w = stage_up()
            for k in range(KT):
                g = k % 4
                mm = pe.matmul(ps[32 * g:32 * g + 2, 4, 0:PN], cond[:, :, k], w[:, k, :], start=(k < 4), stop=(k >= 4))
            mm.then_inc(modx_part, 1)

        def modx_pe_sum(pe, m):
            pe.wait_ge(modx_q, m + 1)
            pe.matmul(ps[0:1, 5, 0:PN], pick_x[:, 0:1], mod_q[:, :], start=True, stop=True).then_inc(modx_b, 1)

        def modx_dve_part(dve, m):
            dve.wait_ge(modx_part, m + 1)
            if m == 0:
                dve.wait_ge(tl_done, T_O)
            else:
                dve.wait_ge(modx_b, m)
            dve.tensor_copy(mod_q[:, :], ps[:, 4, 0:PN]).then_inc(modx_q, 1)

        def modx_dve_row(dve, m):
            dve.wait_ge(modx_b, m + 1)
            dve.wait_ge(modb_in, 16 * (m + 1))
            if m:
                dve.wait_ge(modx_stored, 16 * m)
            dve.tensor_tensor(mod_row[0:1, :], ps[0:1, 5, 0:PN], mod_b[0:1, :], ALU.add).then_inc(modx_row, 1)

        def keys_pe(pe):
            def tile(j, b, late):
                pe.wait_ge(ks_lo, j + 1)
                if late:
                    pe.wait_ge(kt_a, j - 1)
                    pe.wait_ge(kt_v, j - 1)
                else:
                    pe.wait_ge(dense_evac, D_O)
                for h in range(10):
                    mm = pe.transpose(ps[:, 3 * b + h // 4, (h % 4) * P:(h % 4 + 1) * P], k_split[:, b, h, :], ident[:, :])
                mm.then_inc(kt_tr, 1)
            tile(0, 0, False)
            tile(1, 1, False)
            with pe.Fori(1, 5) as i:
                for b in range(2):
                    tile(2 * i + b, b, True)

        def keys_act(act):
            def hi(j, b, late):
                if late:
                    act.wait_ge(kt_tr, 1)
                    act.wait_ge(kt_tr, j - 1)
                act.activation(k_split[:, b, :, 0:HD].bitcast(F32R),
                               row_tile(k_nat, j, 0, KVW).rearrange("p (h d) -> p h d", d=HD), ACT.Copy).then_inc(ks_hi, 1)

            def out(j, b):
                act.wait_ge(kt_tr, 1)
                act.wait_ge(kt_tr, j + 1)
                act.activation(kt[:, 0:4, ds(j * P, P)], ps[:, 3 * b, :].rearrange("p (h n) -> p h n", n=P), ACT.Copy).then_inc(kt_a, 1)

            act.wait_ge(*panel_used(P_O - 1))
            act.wait_ge(hg_done, 10)
            act.wait_ge(roped, ROPED)
            hi(0, 0, False)
            hi(1, 1, False)
            out(0, 0)
            out(1, 1)
            with act.Fori(1, 5) as i:
                for b in range(2):
                    hi(2 * i + b, b, True)
                for b in range(2):
                    out(2 * i + b, b)

        def keys_dve(dve):
            def lo(j, b):
                dve.wait_ge(ks_hi, j + 1)
                dve.tensor_tensor(k_split[:, b, :, HD:P], row_tile(k_nat, j, 0, KVW).rearrange("p (h d) -> p h d", d=HD),
                                  k_split[:, b, :, 0:HD], ALU.subtract).then_inc(ks_lo, 1)

            def out(j, b):
                dve.wait_ge(kt_tr, j + 1)
                dve.tensor_copy(kt[:, 4:8, ds(j * P, P)], ps[:, 3 * b + 1, :].rearrange("p (h n) -> p h n", n=P))
                dve.tensor_copy(kt[:, 8:10, ds(j * P, P)], ps[:, 3 * b + 2, 0:2 * P].rearrange("p (h n) -> p h n", n=P)).then_inc(kt_v, 1)

            dve.wait_ge(hg_done, 10)
            dve.wait_ge(roped, ROPED)
            with dve.Fori(0, 5) as i:
                for b in range(2):
                    lo(2 * i + b, b)
                for b in range(2):
                    out(2 * i + b, b)

        def pool_x(pool):
            for q, panel in enumerate(X_PANELS[:7]):
                pool_heads(pool, panel, NT, 0, 3 + q, 6 + NT * (q + 1))
            attention_pool(pool)

        C_AT = NT - NC
        TILE_OF = 2

        def pool_c(pool):
            def x_tile(j):
                if j < NT:
                    norm_tile(pool, j, T_X, D)
                if 1 <= j <= NT:
                    shift_tile(pool, j - 1, NC, shift_x)

            for j in range(2):
                x_tile(j)
            for s in range(NT):
                if s < 3:
                    pool_roots(pool, C_PANELS[s], NC, s, NC * (s + 1))
                if 1 <= s < 4:
                    pool_gains(pool, C_PANELS[s - 1], NC, NT, s - 1)
                x_tile(s + 2)

        def pe_c(pe):
            for s in range(NT):
                if s < len(C_PANELS):
                    for _ in rows_pe(pe, s, s % 2, NC, T_C, NC * s, lag=2, at=C_AT):
                        pass
                turn_tile(pe, s, s % 2, T_X)

        def act_c(act):
            def x_sum(j):
                if j < NT:
                    act.wait_ge(x_in[j], 16)
                    sum_tile(act, j, T_X, q_nat[:, j, :])

            for j in range(2):
                x_sum(j)
            for s in range(NT):
                if s < len(C_PANELS):
                    heads_act(act, C_PANELS[s], s + 1, NC, NT, NC * s, NC * s)
                x_sum(s + 2)
                if s == C_AT:
                    act.wait_ge(dense_done, D_X)
                turned_hi(act, s, s % 2, T_X)

        def dve_c(dve):
            def x_scaled(j):
                if j < NT:
                    scale_tile(dve, j, j % 2, T_X, q_nat[:, j, :], gain_x, True)

            x_scaled(0)
            last, n = None, 0
            for s in range(NT):
                if s < len(C_PANELS):
                    heads_dve(dve, C_PANELS[s], last, s + 1, NC, NT, NC * s, NC * s, n)
                    last, n = (C_PANELS[s], n + 1) if C_PANELS[s][0] != "v" else (None, n)
                x_scaled(s + 1)
                turned_lo(dve, s, s % 2, T_X)

        A, B = 0, 1
        NB = NT

        def unit(ph, i, n):
            return 32 * ph + NB * i + n

        def local(ph, n):
            if ph == A:
                first, last = max(n - 1, 0), min(n + 1, NT - 1)
                return first, P * (last - first + 1), first - (n - 1)
            if n < 2:
                return 0, 8 * GRID, 7 - 2 * n - 1
            if n >= 6:
                return 4, 8 * GRID, 8 - 2 * n + 7 - 1
            return n - 2, NI * GRID, None

        def chunks(ph, n):
            first, width, _ = local(ph, n)
            return [(NT, P), (NT + 1, P)] + [(first + c, min(P, width - c * P)) for c in range((width + P - 1) // P)]

        def late_groups(ph, i, n, j=0):
            if ph == A:
                return 12 * i + 2 * max(0, min(n, 7) - 1) + (j if 1 <= n <= 6 else 0)
            return 48 + 16 * i + 2 * n + j

        def joined(ph, n):
            return ph == A or 2 <= n < 6

        def late(ph, n):
            return len(chunks(ph, n)) > 4

        def after(i, n, k):
            return (i, n + k) if n + k < NB else (i + 1, n + k - NB)

        def before(i, n):
            return (i, n - 1) if n else (i - 1, NB - 1)

        def keys_of(ph, i, j, a, width):
            if ph == A:
                h = i // 2
            else:
                h = 2 + 2 * i + j
            if isinstance(h, int):
                return kt[:, h, a:a + width]
            return kt[:, ds(h, 1), a:a + width].squeeze(1)

        def pe_turn_q(pe, ph, i, n):
            u = unit(ph, i, n)
            pe.wait_ge(qs_step, u + 1)
            if not isinstance(u, int) or u > 0:
                pe.wait_ge(qt_ready, u)
            for j in range(2):
                for o in range(2):
                    mm = pe.transpose(ps[:, 6, (2 * j + o) * P:(2 * j + o + 1) * P], q_split[:, n % 2, j, o, :], ident[:, :])
            mm.then_inc(qt_done, 1)

        def pe_scores(pe, ph, i, n, j):
            u = unit(ph, i, n)
            first, width, _ = local(ph, n)
            pe.wait_ge(qt_ready, u + 1)
            if isinstance(u, int) and u == 0:
                pe.wait_ge(kt_a, 10)
                pe.wait_ge(kt_v, 10)
            else:
                pe.wait_ge(exp_done, 2 * u - 1 + j)
            parts = [(ps[:, 2 * j, 0:CTX], S, CTX)]
            if ph == A:
                parts = [(ps[:, 2 * j, CTX:2 * CTX], S, CTX)]
                parts.append((ps[:, 2 * j + 1, 0:width], first * P, width))
            else:
                parts.append((ps[:, 2 * j, CTX:2 * CTX], first * P, 256))
                parts.append((ps[:, 2 * j + 1, 0:width - 256], first * P + 256, width - 256))
            for dst, a, w in parts:
                for o in range(2):
                    mm = pe.matmul(dst, q_t[:, n % 2, j, o, :], keys_of(ph, i, j, a, w), start=(o == 0), stop=(o == 1))
            mm.then_inc(s_done, 1)

        def pe_turn_p(pe, ph, i, n, j):
            u = unit(ph, i, n)
            every = chunks(ph, n)
            pe.wait_ge(exp_done, 2 * u + j + 1)
            if not isinstance(u, int) or 2 * u + j > 0:
                pe.wait_ge(pt0_evac, 2 * u + j)
            for c, (_, rows) in enumerate(every[:4]):
                mm = pe.transpose(ps[0:rows, 4, c * P:(c + 1) * P], probs[:, j, c * P:c * P + rows], ident[:, :])
            mm.then_inc(pt0_done, 1)
            if late(ph, n):
                g = late_groups(ph, i, n, j)
                if not isinstance(g, int) or g > 0:
                    pe.wait_ge(pt1_evac, g)
                for c, (_, rows) in enumerate(every[4:]):
                    mm = pe.transpose(ps[0:rows, 5, c * P:(c + 1) * P], probs[:, j, (4 + c) * P:(4 + c) * P + rows], ident[:, :])
                mm.then_inc(pt1_done, 1)

        def pe_values(pe, ph, i, n):
            u = unit(ph, i, n)
            pe.wait_ge(pt0_evac, 2 * u + 2)
            if late(ph, n):
                pe.wait_ge(pt1_evac, late_groups(ph, i, n) + 2)
            pe.wait_ge(vp_ready, 4 * ph + i + 1)
            if not isinstance(u, int) or u > 0:
                pe.wait_ge(on_evac, u)
            every = chunks(ph, n)
            for c, (tile, rows) in enumerate(every):
                for j in range(2):
                    mm = pe.matmul(ps[HD * j:HD * j + HD, 7, 0:P], v_pair[0:rows, tile, HD * j:HD * j + HD],
                                   prob_t[n % 2][0:rows, j, c * P:(c + 1) * P], start=(c == 0), stop=(c == len(every) - 1))
            mm.then_inc(pv_done, 1)

        def pe_turn_o(pe, ph, i, n):
            pe.wait_ge(ot_evac, unit(ph, i, n) + 1)
            pe.transpose(ps[:, 7, P:2 * P], o_t[:, :], ident[:, :]).then_inc(on_done, 1)

        def attention_pe(pe):
            for ph in (A, B):
                pe_turn_q(pe, ph, 0, 0)
                pe_turn_q(pe, ph, 0, 1)
                pe_scores(pe, ph, 0, 0, 0)
                pe_scores(pe, ph, 0, 0, 1)

                def pair(i, first, last):
                    for n in range(NB):
                        ahead, behind = not (last and n + 1 >= NB), not (first and n == 0)
                        pe_turn_p(pe, ph, i, n, 0)
                        if ahead:
                            pe_scores(pe, ph, *after(i, n, 1), 0)
                        if behind:
                            pe_values(pe, ph, *before(i, n))
                        if not (last and n + 2 >= NB):
                            pe_turn_q(pe, ph, *after(i, n, 2))
                        pe_turn_p(pe, ph, i, n, 1)
                        if ahead:
                            pe_scores(pe, ph, *after(i, n, 1), 1)
                        if behind:
                            pe_turn_o(pe, ph, *before(i, n))
                each_pair(pe, ph, pair)
                pe_values(pe, ph, PAIRS - 1, NB - 1)
                pe_turn_o(pe, ph, PAIRS - 1, NB - 1)

        def each_pair(eng, ph, pair):
            pair(0, True, False)
            with eng.Fori(1, PAIRS - 1) as i:
                pair(i, False, False)
            pair(PAIRS - 1, False, True)

        def act_q(act, ph, i, n):
            u = unit(ph, i, n)
            act.wait_ge(qt_done, u + 1)
            if not isinstance(u, int) or u >= 2:
                act.wait_ge(s_done, 2 * u - 2)
            act.activation(q_t[:, n % 2, :, :, :].rearrange("p a b n -> p (a b n)"), ps[:, 6, :], ACT.Copy).then_inc(qt_ready, 1)

        def act_exp(act, ph, i, n, j):
            u = unit(ph, i, n)
            _, width, _ = local(ph, n)
            act.wait_ge(min_done, 2 * u + j + 1)
            if not isinstance(u, int) or u > 0:
                pi, pn = (i, n - 1) if n else (i - 1, NB - 1)
                pp = ph
                if n == 0 and isinstance(i, int) and i == 0:
                    pp, pi = A, PAIRS - 1
                if late(pp, pn):
                    act.wait_ge(pt1_done, late_groups(pp, pi, pn, j) + 1)
                else:
                    act.wait_ge(pt0_done, 2 * u - 1 + j)
            low = small[:, j, 2:3]
            if joined(ph, n):
                last = act.activation(probs[:, j, 0:CTX + width], masked[:, j, 0:CTX + width], ACT.Exp, bias=low, scale=-1.0,
                                      accum_out=den[:, n % 2, j, 0:1])
                if ph == A:
                    h = 2 * i + j
                    last = act.activation(den[:, n % 2, j, 1:2], neg_sink[:, ds(h, 1)], ACT.Exp, bias=low, scale=-1.0)
                last.then_inc(exp_done, 1)
                return
            act.activation(probs[:, j, 0:CTX], ps[:, 2 * j, 0:CTX], ACT.Exp, bias=low, scale=-1.0,
                           accum_out=den[:, n % 2, j, 0:1])
            act.activation(probs[:, j, CTX:CTX + width], masked[:, j, 0:width], ACT.Exp, bias=low, scale=-1.0,
                           accum_out=den[:, n % 2, j, 1:2]).then_inc(exp_done, 1)

        def act_p(act, ph, i, n, j):
            if not late(ph, n):
                return
            u = unit(ph, i, n)
            act.wait_ge(pt1_done, late_groups(ph, i, n, j) + 1)
            if not isinstance(u, int) or u > 1:
                act.wait_ge(pv_done, u - 1)
            cols = P * (len(chunks(ph, n)) - 4)
            act.activation(prob_t[n % 2][:, j, 4 * P:4 * P + cols], ps[:, 5, 0:cols], ACT.Copy).then_inc(pt1_evac, 1)

        def act_v(act, ph, i):
            if ph == B or not isinstance(i, int) or i > 0:
                act.wait_ge(pv_done, NB)
                act.wait_ge(pv_done, 32 * ph + NB * i)
            if ph == A:
                col = (i // 2) * HD
                for j in range(2):
                    ins = act.activation(v_pair[:, :, HD * j:HD * j + HD], v_nat[:, :, ds(col, HD)], ACT.Copy)
            else:
                ins = act.activation(v_pair[:, :, :], v_nat[:, :, ds(A_KV + P * i, P)], ACT.Copy)
            ins.then_inc(vp_ready, 1)

        def attention_act(act):
            for ph in (A, B):
                act_q(act, ph, 0, 0)
                act_q(act, ph, 0, 1)
                act_exp(act, ph, 0, 0, 0)
                act_exp(act, ph, 0, 0, 1)

                def pair(i, first, last):
                    for n in range(NB):
                        for j in range(2):
                            act_p(act, ph, i, n, j)
                            if not (last and n + 1 >= NB):
                                act_exp(act, ph, *after(i, n, 1), j)
                            if j == 0 and not (last and n + 2 >= NB):
                                act_q(act, ph, *after(i, n, 2))
                        if n == 0:
                            act_v(act, ph, i)
                each_pair(act, ph, pair)

        def dve_min(dve, ph, i, n, j):
            u = unit(ph, i, n)
            first, width, at0 = local(ph, n)
            if ph == A and n == 0 and j == 0:
                dve.drain()
                dve.tensor_copy(small[:, :, 3:4], neg_sink[:, ds(2 * i, 2)].unsqueeze(2))
                dve.drain()
            both = ps[:, 2 * j:2 * j + 2, :].rearrange("p a n -> p (a n)")
            if joined(ph, n):
                dve.wait_ge(s_done, 2 * u + j + 1)
                if ph == B:
                    dve.wait_ge(tab_done, 4 * (i + 1))
                if not isinstance(i, int):
                    dve.memset(small[:, j, 5:6], 0.0)
                dve.wait_ge(band_in, 16) if ph == A else dve.wait_ge(bias_in, 32)
                if ph == A:
                    scores, start = both[:, CTX:2 * CTX + width], small[:, j, 3:4]
                    at0 = 5 * P if n == 0 else 0
                    table = band[:, :, :].rearrange("p a n -> p (a n)")[:, at0:at0 + CTX + width]
                else:
                    scores, start, table = both[:, 0:CTX + width], BIG, inner[:, j, :]
                out = masked[:, j, 0:CTX + width]
            else:
                dve.wait_ge(s_done, 2 * u + j + 1)
                dve.wait_ge(tab_done, 4 * (i + 1))
                dve.tensor_reduce(small[:, j, 0:1], ps[:, 2 * j, 0:CTX], AX_X, ALU.min)
                dve.drain()
                dve.wait_ge(bias_in, 32)
                scores, start, out = both[:, CTX:CTX + width], small[:, j, 0:1], masked[:, j, 0:width]
                table = edge[:, j, at0:at0 + 8, :].rearrange("p a n -> p (a n)")
            dve.tensor_tensor_reduce(out, scores, table, 1.0, start, ALU.add, ALU.min, small[:, j, 2:3]).then_inc(min_done, 1)

        def dve_p(dve, ph, i, n, j):
            u = unit(ph, i, n)
            dve.wait_ge(pt0_done, 2 * u + j + 1)
            if not isinstance(u, int) or u > 1:
                dve.wait_ge(pv_done, u - 1)
            dve.tensor_copy(prob_t[n % 2][:, j, 0:4 * P], ps[:, 4, :]).then_inc(pt0_evac, 1)

        def dve_sums(dve, ph, i, n):
            u = unit(ph, i, n)
            terms = 1 if ph == B and joined(ph, n) else 2
            dve.wait_ge(exp_done, 2 * u + 2)
            if not isinstance(u, int) or u > 0:
                dve.wait_ge(dn_step, 2 * u)
            dve.tensor_reduce(dsum[:, :], den[:, n % 2, :, 0:terms], AX_X, ALU.add).then_inc(dn_step, 1)
            dve.wait_ge(dn_step, 2 * u + 1)
            if not isinstance(u, int) or u > 1:
                dve.wait_ge(on_evac, u - 1)
            dve.reciprocal(rden[:, n % 2, :], dsum[:, :]).then_inc(dn_step, 1)

        def dve_o(dve, ph, i, n):
            u = unit(ph, i, n)
            dve.wait_ge(pv_done, u + 1)
            if not isinstance(u, int) or u > 0:
                dve.wait_ge(on_done, u)
            dve.tensor_copy(o_t[:, :], ps[:, 7, 0:P]).then_inc(ot_evac, 1)

        def dve_on(dve, ph, i, n):
            u = unit(ph, i, n)
            dve.wait_ge(on_done, u + 1)
            dve.wait_ge(dn_step, 2 * u + 2)
            dst = q_nat[:, n, ds(AW * ph + P * i, P)].rearrange("p (h d) -> p h d", d=HD)
            dve.tensor_tensor(dst, ps[:, 7, P:2 * P].rearrange("p (h d) -> p h d", d=HD),
                              bcast(rden[:, n % 2, :], 2, HD), ALU.mult).then_inc(on_evac, 1)

        def dve_tables(dve, i):
            for j in range(2):
                if j == 0:
                    dve.wait_ge(bias_in, 32)
                    dve.wait_ge(min_done, 64 + 16 * i)
                h = 2 * i + j
                row = raw_bias[:, ds(h, 1), 0:GRID].squeeze(1)
                windows = bass.AP(row.tensor, row.offset, [list(row.ap[0]), [RB, NE], [1, GRID]])
                dve.scalar_tensor_tensor(out=edge[:, j, :, :], in0=windows, scalar=-1.0, in1=bcast(col_mask[:, :], 1, NE),
                                         op0=ALU.mult, op1=ALU.add).then_inc(tab_done, 1)
            for j in range(2):
                dve.wait_ge(tab_done, 4 * i + 1 + j)
                dve.tensor_tensor(inner[:, j, CTX:].rearrange("p (r c) -> p r c", c=GRID), edge[:, j, 2:2 + NI, :], bcast(row_mask[:, :], 2, GRID),
                                  ALU.add).then_inc(tab_done, 1)

        def attention_dve(dve):
            for ph in (A, B):
                if ph == B:
                    dve.memset(inner[:, :, 0:CTX], 0.0)
                    dve_tables(dve, 0)
                dve_min(dve, ph, 0, 0, 0)
                dve_min(dve, ph, 0, 0, 1)

                def pair(i, first, last):
                    for n in range(NB):
                        ahead, behind = not (last and n + 1 >= NB), not (first and n == 0)
                        if ph == B and n == NB - 1 and ahead:
                            dve_tables(dve, i + 1)
                        dve_p(dve, ph, i, n, 0)
                        if ahead:
                            dve_min(dve, ph, *after(i, n, 1), 0)
                        if behind:
                            dve_o(dve, ph, *before(i, n))
                        dve_p(dve, ph, i, n, 1)
                        if ahead:
                            dve_min(dve, ph, *after(i, n, 1), 1)
                        dve_sums(dve, ph, i, n)
                        if behind:
                            dve_on(dve, ph, *before(i, n))
                each_pair(dve, ph, pair)
                dve_o(dve, ph, PAIRS - 1, NB - 1)
                dve_on(dve, ph, PAIRS - 1, NB - 1)

        def pool_q(pool, ph, i, n):
            u = unit(ph, i, n)
            src = q_nat[:, n, ds(AW * ph + P * i, P)].rearrange("p (h d) -> p h d", d=HD)
            dst = q_split[:, n % 2, :, :, :]
            if not isinstance(u, int) or u >= 2:
                pool.wait_ge(qt_done, 1)
                pool.wait_ge(qt_done, u - 1)
            else:
                pool.wait_ge(roped, ROPED)
                pool.wait_ge(dense_done, D_O)
                pool.wait_ge(hg_done, 10)
            pool.tensor_copy(dst[:, :, 0, 0:HD].bitcast(F32R), src)
            pool.drain()
            pool.tensor_tensor(dst[:, :, 0, HD:P], src, dst[:, :, 0, 0:HD], ALU.subtract)
            pool.tensor_copy(dst[:, :, 1, HD:P], dst[:, :, 0, 0:HD])
            pool.drain()
            pool.tensor_copy(dst[:, :, 1, 0:HD], dst[:, :, 0, HD:P]).then_inc(qs_step, 1)

        def attention_pool(pool):
            for n in range(NB):
                pool_q(pool, A, 0, n)
            with pool.Fori(1, PAIRS) as i:
                for n in range(NB):
                    pool_q(pool, A, i, n)
            with pool.Fori(0, PAIRS) as i:
                for n in range(NB):
                    pool_q(pool, B, i, n)

        def sync_attention(sp):
            sp.wait_ge(ready, 2)
            flat = t["rpb_b"].rearrange("a h r c -> (a h r c)").unsqueeze(0)
            sp.dma_start(rpb_pad[RPAD:RPAD + 8 * RPH].unsqueeze(0), flat).then_inc(pad_done, 16)
            sp.dma_start(rpb_pad[0:RPAD].unsqueeze(0), zero_row[0:1, :]).then_inc(pad_done, 16)
            sp.dma_start(rpb_pad[RPAD + 8 * RPH:].unsqueeze(0), zero_row[0:1, :]).then_inc(pad_done, 16)
            sp.wait_ge(pad_done, 48)
            sp.dma_start(rpb_skew.rearrange("(c n) -> c n", c=GRID)[:, 0:RPL],
                         bass.AP(rpb_pad.tensor, 0, [[0, GRID], [1, RPL]])).then_inc(skewed, 16)
            sp.wait_ge(dense_done, D_O)
            sp.wait_ge(w_lo_done, P_O)
            sp.dma_start(band[:, :, :], t["k_band"]).then_inc(band_in, 16)
            sp.wait_ge(skewed, 16)
            sp.wait_ge(ks_lo, 10)
            for parity in range(2):
                src = bass.AP(rpb_skew.tensor, RPAD + (1 - parity) * RB + RB // 2, [[RPL, GRID], [RPH, 8], [1, RPW]])
                sp.dma_start(raw_bias[GRID * parity:GRID * parity + GRID, :, :], src).then_inc(bias_in, 16)
            sp.wait_ge(modx_stored, 256)
        @block.sync
        def _(sp):
            sp.dma_start(cond[:, 0, :], t["c"][0].rearrange("(p k) -> p k", k=KT)).then_inc(cond_in, 16)
            sp.dma_start(cond[:, 1, :], t["c_ctx"].rearrange("(p k) -> p k", k=KT)).then_inc(cond_in, 16)
            sp.dma_start(ident[:, :], t["k_ident"]).then_inc(pe_consts_in, 16)
            sp.dma_start(pick_x[:, :], t["k_pick"][0]).then_inc(pe_consts_in, 16)
            sp.dma_start(pick_c[:, :], t["k_pick"][1]).then_inc(pe_consts_in, 16)
            for j in range(8):
                w = t["w_mod"][0].rearrange("(p k) n -> p k n", k=KT)[:, :, j * PN:(j + 1) * PN]
                sp.dma_start(mod_w[:, j, :].rearrange("p (k n) -> p k n", k=KT), w).then_inc(modw_in[j], 16)
                if j == 1:
                    for d in range(2):
                        sp.dma_start(mod_1[:, 2 * d:2 * d + 2, :].rearrange("p a b -> p (a b)"),
                                     t["b_mod"][0, 0:2 * D].partition_broadcast(P)).then_inc(mod1_in, 16)
                    sp.dma_start(norm1[:, :], t["norm1_g"][0].partition_broadcast(P)).then_inc(mod1_in, 16)
                if j == 3:
                    sp.dma_start(ctx_in[:, :, :], t["ctx"][0].rearrange("(t p) d -> p t d", p=P)).then_inc(ctx_landed, 16)
            load_weights(sp, 0, panel_of(t["w_in"], CTX_COLS[0]))
            for j in range(NT):
                sp.dma_start(q_nat[:, j, :], t["x"][0, j * P:(j + 1) * P, :]).then_inc(x_in[j], 16)
            sp.dma_start(rope[:, :, :, :], t["k_rope"]).then_inc(consts_in, 16)
            for j, name in enumerate(("qn_a", "kn_a", "qn_b", "kn_b")):
                sp.dma_start(head_gain[:, j, :], t[name][0].partition_broadcast(P)).then_inc(consts_in, 16)
            sp.dma_start(neg_sink[:, :], t["sink_a"][0].partition_broadcast(P)).then_inc(consts_in, 16)
            sp.dma_start(row_mask[:, :], t["k_row_mask"]).then_inc(consts_in, 16)
            sp.dma_start(col_mask[:, :], t["k_col_mask"]).then_inc(consts_in, 16)
            for j in range(1, 5):
                load_weights(sp, j, panel_of(t["w_in"], CTX_COLS[j]))
            for j in range(2):
                load_weights(sp, P_X + j, panel_of(t["w_in"], j * PN))
            sync_x(sp)
            sync_attention(sp)


        @block.gpsimd
        def _(pool):
            pool.memset(neg_half[:, :], -0.5).then_inc(ready, 1)
            pool.memset(zero_row[:, :], 0.0).then_inc(ready, 1)
            norms_pool(pool, NC, T_C, D, shift=shift_c)
            pool_c(pool)
            pool_x(pool)


        @block.tensor
        def _(pe):
            pe.wait_ge(pe_consts_in, 48)
            pe.wait_ge(cond_done, 1)
            pe.wait_ge(banks_clear, 1)
            for j in range(8):
                pe.wait_ge(modw_in[j], 16)
                if j >= 2:
                    pe.wait_ge(part_evac, j - 1)
                w = mod_w[:, j, :].rearrange("p (k n) -> p k n", k=KT)
                for k in range(KT):
                    g = k % 4
                    mm = pe.matmul(ps[32 * g:32 * g + 2, j % 2, 0:PN], cond[:, :, k], w[:, k, :], start=(k < 4), stop=(k >= 4))
                mm.then_inc(part_done, 1)
                pe.wait_ge(part_evac, j + 1)
                if j >= 1:
                    pe.wait_ge(mod_added, 2 * j)
                pe.matmul(ps[:, 2, 0:PN], pick_x[:, :], mod_part[:, j % 2, :], start=True, stop=True).then_inc(mod_done, 1)
                pe.matmul(ps[:, 3, 0:PN], pick_c[:, :], mod_part[:, j % 2, :], start=True, stop=True).then_inc(mod_done, 1)
            turn_pe(pe, NC, T_C)
            pe_c(pe)
            pe.wait_ge(dense_evac, D_X)
            with pe.Fori(0, 4) as i:
                for b in range(2):
                    p = 2 * i + b
                    for j in rows_pe(pe, P_X + p, (P_X + b) % 2, NT, T_X, D_X + NT * p):
                        m = 2 * p + (j - 4) // 2
                        if j in (4, 6):
                            modx_pe_part(pe, m, b == 0 and j == 4)
                        if j in (5, 7):
                            modx_pe_sum(pe, m)
            for _ in rows_pe(pe, P_X + 8, (P_X + 8) % 2, NT, T_X, D_X + NT * 8):
                pass
            keys_pe(pe)
            attention_pe(pe)


        @block.scalar
        def _(act):
            act.wait_ge(cond_in, 32)
            act.activation(cond[:, :, :], cond[:, :, :], ACT.Silu).then_inc(cond_done, 1)
            act.wait_ge(ctx_landed, 16)
            for j in range(NC):
                sum_tile(act, j, T_C, ctx_in[:, j, :])
            split_hi(act, 0, 0)
            turn_act(act, NC, T_C, None, at=C_AT)
            act_c(act)
            for n, panel in enumerate(X_PANELS):
                heads_act(act, panel, P_X + n + 1 if n < 8 else None, NT, 0, D_X + NT * n, 6 + NT * n)
            keys_act(act)
            attention_act(act)


        @block.vector
        def _(dve):
            dve.memset(ps[:, 0:2, 0:PN], 0.0).then_inc(banks_clear, 1)
            for j in range(8):
                dve.wait_ge(part_done, j + 1)
                if j >= 2:
                    dve.wait_ge(mod_done, 2 * j - 2)
                dve.tensor_copy(mod_part[:, j % 2, :], ps[:, j % 2, 0:PN]).then_inc(part_evac, 1)
                if j == 0:
                    dve.wait_ge(mod1_in, 48)
                dve.wait_ge(mod_done, 2 * j + 2)
                for d in range(2):
                    dst = mod_1[:, 2 * d + j // 4, (j % 4) * PN:(j % 4 + 1) * PN]
                    dve.tensor_tensor(dst, ps[:, 2 + d, 0:PN], dst, ALU.add).then_inc(mod_added, 1)
            for d, g in ((0, gain_c), (1, gain_x)):
                dve.wait_ge(mod_added, 16)
                dve.scalar_tensor_tensor(out=g, in0=g, scalar=1.0, in1=norm1[:, :], op0=ALU.add, op1=ALU.mult).then_inc(mod_added, 1)
            dve.wait_ge(mod_added, 18)
            turn_dve(dve, NC, T_C, lambda j: row_tile(ctx_in, j, 0, D), gain_c, True, at=C_AT)
            split_lo(dve, 0, 0)
            dve.wait_ge(consts_in, 16 * 8)
            for g in (0, 2):
                dve.tensor_scalar(head_gain[:, g, :], head_gain[:, g, :], -HD ** -0.5, None, ALU.mult).then_inc(neg_done, 1)
            dve.tensor_scalar(neg_sink[:, :], neg_sink[:, :], -1.0, None, ALU.mult).then_inc(neg_done, 1)
            dve_c(dve)
            n = 3
            last = None
            for q, panel in enumerate(X_PANELS):
                def mods(j, q=q):
                    m = 2 * q + (j - 4) // 2
                    (modx_dve_part if j in (4, 6) else modx_dve_row)(dve, m)
                heads_dve(dve, panel, last, P_X + q + 1 if q < 8 else None, NT, 0, D_X + NT * q, 6 + NT * q, n, mods if q < 8 else None)
                last, n = (panel, n + 1) if panel[0] != "v" else (None, n)
            keys_dve(dve)
            attention_dve(dve)

        done.close()
        mod2_in, on_in, norm2_in = sem("mod2_in"), sem("on_in"), sem("norm2_in")
        merged, gain2_done = sem("merged"), sem("gain2_done")
        tmp = at("tmp", [2, PN], F32, k_off)
        LAG = 3

        def merge_sp(sp):
            load_weights(sp, P_O, panel_of(t["w_out"], 0))
            for j, name in enumerate(("on_a", "on_b")):
                sp.dma_start(on_ab[:, j * AW:(j + 1) * AW], t[name][0].partition_broadcast(P)).then_inc(on_in, 16)
            for j in range(4):
                sp.dma_start(mod_2[:, j, :], mod_dram[j].partition_broadcast(P)).then_inc(mod2_in, 16)
            sp.dma_start(norm2[:, :], t["norm2_g"][0].partition_broadcast(P)).then_inc(norm2_in, 16)
            load_weights(sp, P_O + 1, panel_of(t["w_out"], PN))
            for j in range(NT):
                sp.wait_ge(xn_done, T_O + j + 1)
                sp.dma_start(q_nat[:, j, :], t["x"][0, j * P:(j + 1) * P, :]).then_inc(x_in[j], 16)
            for j in range(2, 4):
                load_weights(sp, P_O + j, panel_of(t["w_out"], j * PN))
            load_weights(sp, P_F, panel_of(t["w_gate"], 0))

        def merge_pool(pool):
            norms_pool(pool, NT, T_O, AW, 2)
            pool.wait_ge(mod2_in, 64)
            norms_pool(pool, NT, T_H, D, shift=mod_2[:, 1, :], shifts=NC + NT)

        def merge_pe(pe):
            turn_pe(pe, NT, T_O)
            for p in range(4):
                for j in rows_pe(pe, P_O + p, p % 2, NT, T_O, D_O + NT * p):
                    if p == 3 and j >= LAG:
                        turn_tile(pe, j - LAG, (j - LAG) % 2, T_H)
            for j in range(NT - LAG, NT):
                turn_tile(pe, j, j % 2, T_H)

        def merge_act(act):
            for j in range(NT):
                act.wait_ge(ss_done, T_O + j)
                if j == 0:
                    act.wait_ge(ms_done, T_O)
                for g in range(2):
                    last = act.activation(junk[:, g * AW:(g + 1) * AW], q_nat[:, j, g * AW:(g + 1) * AW], ACT.Square,
                                          accum_out=sumsq[:, 2 * j + g:2 * j + g + 1])
                last.then_inc(ss_done, 1)
            split_hi(act, P_O, 0)
            turn_act(act, NT, T_O, None)
            for p in range(1, 4):
                split_hi(act, P_O + p, p % 2)
            split_hi(act, P_F, P_F % 2, used=(dense_done, D_O + 3 * NT))
            for j in range(NT + LAG):
                if j < NT:
                    act.wait_ge(merged, 3 * NT + j + 1)
                    sum_tile(act, j, T_H, q_nat[:, j, :])
                if j >= LAG:
                    act.wait_ge(dense_done, D_O + 3 * NT + j - LAG + 1)
                    turned_hi(act, j - LAG, (j - LAG) % 2, T_H)

        def merge_dve(dve):
            dve.wait_ge(on_in, 32)

            def scale_halves(j, b):
                dve.wait_ge(rs_done, T_O + j + 1)
                dve.wait_ge(tr_done, T_O + j - 1)
                for g in range(2):
                    root = rstd[:, 2 * j + g:2 * j + g + 1] if isinstance(j, int) else rstd[:, ds(2 * j + g, 1)]
                    last = dve.scalar_tensor_tensor(out=xn[:, b, g * AW:(g + 1) * AW], in0=row_tile(q_nat, j, g * AW, AW),
                                                    scalar=root, in1=on_ab[:, g * AW:(g + 1) * AW], op0=ALU.mult, op1=ALU.mult)
                last.then_inc(xn_done, 1)

            for b in range(2):
                scale_halves(b, b)
            with dve.Fori(1, NT // 2) as i:
                for b in range(2):
                    turned_lo(dve, 2 * i + b - 2, b, T_O)
                    scale_halves(2 * i + b, b)
            split_lo(dve, P_O, 0)
            for b in range(2):
                turned_lo(dve, NT - 2 + b, b, T_O)
            dve.wait_ge(mod2_in, 64)
            dve.wait_ge(norm2_in, 16)
            dve.scalar_tensor_tensor(out=mod_2[:, 2, :], in0=mod_2[:, 2, :], scalar=1.0, in1=norm2[:, :],
                                     op0=ALU.add, op1=ALU.mult).then_inc(gain2_done, 1)
            for p in range(4):
                split_lo(dve, P_O + p + 1, (p + 1) % 2)
                cols = slice(p * PN, (p + 1) * PN)
                for j in range(NT + (LAG if p == 3 else 0)):
                    if j < NT:
                        n = NT * p + j
                        dve.wait_ge(dense_done, D_O + n + 1)
                        if n >= 2:
                            dve.wait_ge(merged, n - 1)
                        dve.tensor_tensor(tmp[:, n % 2, :], ps[:, j % 4, 0:PN], mod_2[:, 0, cols], ALU.mult).then_inc(dense_evac, 1)
                        dve.wait_ge(dense_evac, D_O + n + 1)
                        if p == 0:
                            dve.wait_ge(x_in[j], 32)
                        dve.tensor_tensor(q_nat[:, j, cols], q_nat[:, j, cols], tmp[:, n % 2, :], ALU.add).then_inc(merged, 1)
                    if p == 3:
                        if j == 1:
                            dve.wait_ge(gain2_done, 1)
                        if 1 <= j <= NT:
                            scale_tile(dve, j - 1, (j - 1) % 2, T_H, q_nat[:, j - 1, :], mod_2[:, 2, :], True)
                        if j >= LAG:
                            turned_lo(dve, j - LAG, (j - LAG) % 2, T_H)


        def features_pe(pe, p, slot, chunk, bank0, out_done, free):
            pe.wait_ge(w_lo_done, p + 1)
            wh, wl = (w[:, slot, :].rearrange("p (k n) -> p k n", k=KT) for w in (w_hi, w_lo))
            for f in range(2):
                for h in range(2):
                    b = 2 * f + h
                    free(b)
                    bank = ps[:, bank0 + b, :]
                    for k in range(KT):
                        a, c = wh[:, k, f * P:(f + 1) * P], wl[:, k, f * P:(f + 1) * P]
                        x_hi, x_lo = ht_hi[:, k, h * 512:(h + 1) * 512], ht_lo[:, k, h * 512:(h + 1) * 512]
                        pe.matmul(bank, a, x_hi, start=(k == 0), stop=False)
                        pe.matmul(bank, a, x_lo, start=False, stop=False)
                        mm = pe.matmul(bank, c, x_hi, start=False, stop=(k == KT - 1))
                    mm.then_inc(out_done, 1)

        def down_pe(pe, *args):
            for _ in down_tiles(pe, *args):
                pass

        def down_tiles(pe, p, slot, chunk, lo_done, out_done, evac):
            pe.wait_ge(w_lo_done, p + 1)
            pe.wait_ge(lo_done, 4 * chunk + 4)
            wh, wl = (w[:, slot, :].rearrange("p (f n) -> p f n", f=2) for w in (w_hi, w_lo))
            for o in range(2 * NT):
                j, h = o // 2, o % 2
                if not isinstance(chunk, int) or 16 * chunk + o >= 4:
                    pe.wait_ge(evac, 16 * chunk + o - 3)
                for f in range(2):
                    a = act_hi[:, f, j * P:(j + 1) * P]
                    c = act_lo[:, f, j * P:(j + 1) * P]
                    x_hi, x_lo = wh[:, f, h * 512:(h + 1) * 512], wl[:, f, h * 512:(h + 1) * 512]
                    pe.matmul(ps[:, 4 + o % 4, :], a, x_hi, start=(f == 0), stop=False)
                    pe.matmul(ps[:, 4 + o % 4, :], a, x_lo, start=False, stop=False)
                    mm = pe.matmul(ps[:, 4 + o % 4, :], c, x_hi, start=False, stop=(f == 1))
                mm.then_inc(out_done, 1)
                if h:
                    yield j

        def down_dve(dve, chunk, outputs, done_sem, evac, first=False):
            for o in outputs:
                j, h = o // 2, o % 2
                row = q_nat[:, j, h * 512:(h + 1) * 512]
                dve.wait_ge(done_sem, 16 * chunk + o + 1)
                if first:
                    dve.tensor_copy(row, ps[:, 4 + o % 4, :]).then_inc(evac, 1)
                    continue
                if not isinstance(chunk, int) or chunk > 0:
                    dve.wait_ge(evac, 16 * chunk + o - 15)
                dve.tensor_tensor(row, row, ps[:, 4 + o % 4, :], ALU.add).then_inc(evac, 1)

        def quarter(x, b):
            return x[:, b // 2, (b % 2) * 512:(b % 2 + 1) * 512]

        def act_split_hi(act, chunk, src, ready_sem, hi_sem, used):
            for b in range(4):
                act.wait_ge(ready_sem, 4 * chunk + b + 1)
                if b == 0 and (not isinstance(chunk, int) or chunk > 0):
                    act.wait_ge(used, 16 * chunk)
                act.activation(quarter(act_hi, b), quarter(src, b), ACT.Copy).then_inc(hi_sem, 1)

        def act_split_lo(dve, chunk, src, hi_sem, lo_sem):
            for b in range(4):
                dve.wait_ge(hi_sem, 4 * chunk + b + 1)
                dve.tensor_tensor(quarter(act_lo, b), quarter(src, b), quarter(act_hi, b).bitcast(F32), ALU.subtract).then_inc(lo_sem, 1)

        w_scaled = sem("w_scaled")
        hidden_done, up_done, down_done = sem("hidden_done"), sem("up_done"), sem("down_done")
        function_done, act_done, act_hi_done, act_lo_done, down_evac = (sem(x) for x in (
            "function_done", "act_done", "act_hi_done", "act_lo_done", "down_evac"))

        def p_gate(c):
            return P_F if isinstance(c, int) and c == 0 else P_F + 3 * c - 1

        def p_down(c):
            return P_F + 3 * c + 3 if not (isinstance(c, int) and c == CH1 - 1) else P_Z - 1

        def p_up(c):
            return P_F + 3 * c + 1

        def down_panel(w, row):
            if isinstance(row, int):
                return w[0, row:row + PN, :].rearrange("(f p) n -> p f n", p=P)
            return w[0, ds(row, PN), :].rearrange("(f p) n -> p f n", p=P)

        def stage_down():
            return stage[:, :].rearrange("p (f n) -> p f n", f=2)

        def used_gate(c):
            return hidden_done, 4 * c + 4

        def used_up(c):
            return up_done, 4 * c + 4

        def used_down(c):
            return down_done, 16 * c + 16

        def chunks_in_pairs(eng, chunk):
            for b in range(2):
                chunk(b, b)
            with eng.Fori(1, (CH1 - 1) // 2 - 1) as i:
                for b in range(2):
                    chunk(2 * i + b, b)
            for b in range(2):
                chunk(CH1 - 3 + b, b)

        def swiglu_sp(sp):
            load_weights(sp, P_F + 1, panel_of(t["w_up"], 0))

            def chunk(c, last=False):
                if not last:
                    load_weights(sp, p_gate(c + 1), panel_of(t["w_gate"], (c + 1) * PN))
                load_weights(sp, p_down(c), down_panel(t["w_down"], c * PN), stage_down())
                if not last:
                    load_weights(sp, p_up(c + 1), panel_of(t["w_up"], (c + 1) * PN))
            with sp.Fori(0, CH1 - 1) as c:
                chunk(c)
            chunk(CH1 - 1, True)
            load_weights(sp, P_Z, panel_of(t["w_in_2"], Z_FROM[0] * PN))

        def swiglu_pool(pool):
            def scale(c, last=False):
                p = p_down(c)
                pool.wait_ge(w_landed, 16 * (p + 1))
                pool.tensor_tensor(stage_down(), stage_down(), bcast(mod_2[:, 3, :], 1, 2), ALU.mult).then_inc(w_scaled, 1)
            with pool.Fori(0, CH1 - 1) as c:
                scale(c)
            scale(CH1 - 1, True)

        def swiglu_pe(pe):
            pe.wait_ge(tl_done, T_H + NT)

            def gate(c, slot):
                def free(b):
                    if not isinstance(c, int) or c > 0:
                        pe.wait_ge(function_done, 4 * c + b - 3)
                features_pe(pe, p_gate(c), slot, c, 0, hidden_done, free)

            def up(c, slot):
                def free(b):
                    if not isinstance(c, int) or c > 0:
                        pe.wait_ge(down_evac, 16 * c + b - 3)
                features_pe(pe, p_up(c), slot, c, 4, up_done, free)

            gate(0, P_F % 2)
            up(0, (P_F + 1) % 2)

            def chunk(c, b):
                slot = (P_F + b) % 2
                gate(c + 1, slot)
                down_pe(pe, p_down(c), 1 - slot, c, act_lo_done, down_done, down_evac)
                up(c + 1, slot)

            chunks_in_pairs(pe, chunk)
            pe.wait_ge(function_done, 4 * CH1)
            for j in down_tiles(pe, p_down(CH1 - 1), (P_Z - 1) % 2, CH1 - 1, act_lo_done, down_done, down_evac):
                if j >= LAG:
                    turn_tile(pe, j - LAG, (j - LAG) % 2, T_Z, 0)
            for j in range(NT - LAG, NT):
                turn_tile(pe, j, j % 2, T_Z, 0)

        def swiglu_act(act):
            split_hi(act, P_F + 1, (P_F + 1) % 2, used=(dense_done, D_O + 4 * NT))

            def silus(c):
                for b in range(4):
                    act.wait_ge(hidden_done, 4 * c + b + 1)
                    if not isinstance(c, int) or c > 0:
                        act.wait_ge(act_done, 4 * c + b - 3)
                    act.activation(quarter(silu, b), ps[:, b, :], ACT.Silu).then_inc(function_done, 1)

            silus(0)
            split_hi(act, p_gate(1), P_F % 2, used=used_gate(0))

            def chunk(c, b):
                slot = (P_F + b) % 2
                split_hi(act, p_down(c), 1 - slot, used=used_up(c), scaled=c + 1)
                act_split_hi(act, c, act_f, act_done, act_hi_done, down_done)
                silus(c + 1)
                split_hi(act, p_up(c + 1), slot, used=used_gate(c + 1))
                if isinstance(c, int) and c == CH1 - 2:
                    split_hi(act, p_down(CH1 - 1), 1 - slot, used=used_down(c), scaled=CH1)
                else:
                    split_hi(act, p_gate(c + 2), 1 - slot, used=used_down(c))

            chunks_in_pairs(act, chunk)
            act_split_hi(act, CH1 - 1, act_f, act_done, act_hi_done, down_done)
            split_hi(act, P_Z, P_Z % 2, used=used_up(CH1 - 1))
            for j in range(NT + LAG):
                if j < NT:
                    act.wait_ge(down_evac, 16 * (CH1 - 1) + 2 * j + 2)
                    sum_tile(act, j, T_Z, q_nat[:, j, :])
                if j >= LAG:
                    turned_hi(act, j - LAG, (j - LAG) % 2, T_Z, 0)

        def swiglu_dve(dve):
            split_lo(dve, P_F + 1, (P_F + 1) % 2)
            split_lo(dve, p_gate(1), P_F % 2)

            def gated_up(c):
                for b in range(4):
                    dve.wait_ge(function_done, 4 * c + b + 1)
                    dve.wait_ge(up_done, 4 * c + b + 1)
                    if not isinstance(c, int) or c > 0:
                        dve.wait_ge(act_lo_done, 4 * c + b - 3)
                    dve.tensor_tensor(quarter(act_f, b), quarter(silu, b), ps[:, 4 + b, :], ALU.mult).then_inc(act_done, 1)

            def chunk(c, b):
                slot = (P_F + b) % 2
                gated_up(c)
                split_lo(dve, p_down(c), 1 - slot)
                act_split_lo(dve, c, act_f, act_hi_done, act_lo_done)
                down_dve(dve, c, range(4), down_done, down_evac)
                split_lo(dve, p_up(c + 1), slot)
                down_dve(dve, c, range(4, 2 * NT), down_done, down_evac)
                split_lo(dve, p_gate(c + 2), 1 - slot)

            chunks_in_pairs(dve, chunk)
            gated_up(CH1 - 1)
            act_split_lo(dve, CH1 - 1, act_f, act_hi_done, act_lo_done)
            split_lo(dve, P_Z, P_Z % 2)
            dve.wait_ge(gz_in, 16)
            for j in range(NT + LAG):
                if j < NT:
                    down_dve(dve, CH1 - 1, range(2 * j, 2 * j + 2), down_done, down_evac)
                if 1 <= j <= NT:
                    dve.wait_ge(down_evac, 16 * (CH1 - 1) + 2 * j)
                    scale_tile(dve, j - 1, (j - 1) % 2, T_Z, q_nat[:, j - 1, :], gain_z[:, :], False)
                if j >= LAG:
                    turned_lo(dve, j - LAG, (j - LAG) % 2, T_Z, 0)
        x2_dram = nc.dram_tensor("x2_dram", [S, D], F32, kind="Internal").ap()
        VW = D // 2
        KW = D // 4
        RANK = 16
        LR = 2 * VW + 2 * KW + 2 * VW
        zu = at("zu", [NT, VW], F32, k_off)
        zv = at("zv", [NT, VW], F32, k_off + 16384)
        zq = at("zq", [NT, KW], F32, k_off + 32768)
        zk = at("zk", [NT, KW], F32, k_off + 40960)
        zvb = at("zvb", [NT, VW], F32, nat)
        zg = at("zg", [NT, VW], F32, nat + 16384)
        w_lr = at("w_lr", [KT, RANK], F32, k_off + 49152)
        w_lr_hi = at("w_lr_hi", [KT, RANK], F32R, k_off + 49152 + 512)
        w_lr_lo = at("w_lr_lo", [KT, RANK], F32R, k_off + 49152 + 1024)
        gain_z = at("gain_z", [D], F32, k_off)
        lr_t = at("lr_t", [S], F32, rope_at)
        vsum = fixed("vsum", [2, NT])
        x2_stored, gz_in, lr_in, lr_ones, lr_split, lr_done, lr_evac, z_done = (sem(x) for x in (
            "x2_stored", "gz_in", "lr_in", "lr_ones", "lr_split", "lr_done", "lr_evac", "z_done"))
        GELU = ACT.Gelu_apprx_tanh
        Z_PANELS = [(zv, 0, GELU), (zv, PN, GELU), (zu, 0, GELU), (zu, PN, GELU), (zq, 0, ACT.Copy), (zk, 0, ACT.Copy),
                    (zvb, 0, ACT.Copy), (zvb, PN, ACT.Copy), (zg, 0, ACT.Silu), (zg, PN, ACT.Silu)]
        Z_FROM = [2, 3, 0, 1] + list(range(4, 10))
        D_Z = D_O + 4 * NT
        D_M = D_Z + 10 * NT
        MIXC = 4 * P + 2
        ln_gain = at("ln_gain", [2, VW], F32, xnr)
        gate_wb = at("gate_wb", [KW], F32, xnr + 4096)
        mix_c = at("mix_c", [MIXC], F32, xnr + 5120)
        bs_nat = at("bs_nat", [P], F32, xnr + 7232)
        neg_mean, v_sq, v_ms, v_rs, a_sq, a_ms, a_rs = (fixed(x, [NT]) for x in (
            "neg_mean", "v_sq", "v_ms", "v_rs", "a_sq", "a_ms", "a_rs"))
        early_in, ln_in, mean_step, vsq_done, vrs_step, vn_step = (sem(x) for x in (
            "early_in", "ln_in", "mean_step", "vsq_done", "vrs_step", "vn_step"))
        def project_sp(sp):
            sp.wait_ge(act_done, 4 * CH1)
            sp.dma_start(gain_z[:, :], t["pre_mix_g_2"][0].partition_broadcast(P)).then_inc(gz_in, 16)
            for j in range(NT):
                sp.wait_ge(down_evac, 16 * (CH1 - 1) + 2 * j + 2)
                sp.dma_start(x2_dram[j * P:(j + 1) * P, :], q_nat[:, j, :]).then_inc(x2_stored, 16)
            sp.dma_start(w_lr[:, :, :], t["w_in_2"][0].rearrange("(k p) n -> p k n", p=P)[:, :, LR:LR + RANK]).then_inc(lr_in, 16)
            load_weights(sp, P_Z + 1, panel_of(t["w_in_2"], Z_FROM[1] * PN))
            sp.wait_ge(tr_done, T_Z + NT)
            for j, name in enumerate(("gmlp_ln_g_2", "gmlp_ln_b_2")):
                sp.dma_start(ln_gain[:, j, :], t[name][0].partition_broadcast(P)).then_inc(ln_in, 16)
            sp.dma_start(gate_wb[0:RANK, :], t["gla_gate_w_2"][0]).then_inc(early_in, 16)
            sp.dma_start(gate_wb[RANK:RANK + 1, :], t["gla_gate_b_2"][0:1, :]).then_inc(early_in, 16)
            sp.dma_start(mix_c[:, :], t["k_mix"]).then_inc(early_in, 16)
            sp.dma_start(bs_nat[0:4, :], t["gmlp_bs_2"][0]).then_inc(early_in, 16)
            for p in range(2, 10):
                load_weights(sp, P_Z + p, panel_of(t["w_in_2"], Z_FROM[p] * PN))
            load_weights(sp, P_M, panel_of(t["w_out_2"], 0))
            sp.wait_ge(x2_stored, 16 * NT)

        def project_pool(pool):
            pool.memset(lr_t[0:32, :], 1.0).then_inc(lr_ones, 1)
            norms_pool(pool, NT, T_Z, D)
            pool.wait_ge(dense_evac, D_Z + 2 * NT)
            pool.tensor_tensor(neg_mean[:, :], vsum[:, 0, :], vsum[:, 1, :], ALU.add).then_inc(mean_step, 1)
            pool.wait_ge(mean_step, 1)
            pool.tensor_scalar(neg_mean[:, :], neg_mean[:, :], -1.0 / VW, None, ALU.mult).then_inc(mean_step, 1)
            roots(pool, v_sq[:, :], NT, vsq_done, vrs_step, v_ms[:, :], v_rs[:, :], VW)

        def roots(pool, total, n_done, done_sem, step, ms, rs, width, calls=0):
            pool.wait_ge(done_sem, n_done)
            n = ms.shape[1]
            pool.tensor_scalar(ms, total, 1.0 / width, EPS, ALU.mult, ALU.add).then_inc(step, 1)
            pool.wait_ge(step, calls + 1)
            pool.tensor_tensor(rs, ms, neg_half[:, 0:n], ALU.pow).then_inc(step, 1)

        def project_pe(pe):
            pe.wait_ge(lr_split, 2)
            pe.wait_ge(tl_done, T_Z + NT)
            pe.wait_ge(down_evac, 16 * CH1)
            for h in range(2):
                bank = ps[0:RANK, 4 + h, :]
                for k in range(KT):
                    x_hi, x_lo = ht_hi[:, k, h * 512:(h + 1) * 512], ht_lo[:, k, h * 512:(h + 1) * 512]
                    pe.matmul(bank, w_lr_hi[:, k, :], x_hi, start=(k == 0), stop=False)
                    pe.matmul(bank, w_lr_hi[:, k, :], x_lo, start=False, stop=False)
                    mm = pe.matmul(bank, w_lr_lo[:, k, :], x_hi, start=False, stop=(k == KT - 1))
                mm.then_inc(lr_done, 1)
            for p in range(10):
                for _ in rows_pe(pe, P_Z + p, (P_Z + p) % 2, NT, T_Z, D_Z + NT * p):
                    pass

        def project_act(act):
            act.wait_ge(lr_in, 16)
            act.activation(w_lr_hi[:, :, :], w_lr[:, :, :], ACT.Copy).then_inc(lr_split, 1)
            act.wait_ge(lr_ones, 1)
            for h in range(2):
                act.wait_ge(lr_done, h + 1)
                act.activation(lr_t[0:RANK, h * 512:(h + 1) * 512], ps[0:RANK, 4 + h, :], ACT.Copy).then_inc(lr_evac, 1)
            for p, (dst, col, fn) in enumerate(Z_PANELS):
                if p < 9:
                    split_hi(act, P_Z + p + 1, (P_Z + p + 1) % 2, used=(dense_done, D_Z + NT * p))
                if p == 6:
                    act.wait_ge(x2_stored, 16 * NT)
                for j in range(NT):
                    act.wait_ge(dense_done, D_Z + NT * p + j + 1)
                    more = {"accum_out": vsum[:, p, j:j + 1]} if dst is zv else {}
                    act.activation(dst[:, j, col:col + PN], ps[:, j % 4, 0:PN], fn, **more).then_inc(dense_evac, 1)
                    if p == 2:
                        act.wait_ge(mean_step, 2)
                        if j:
                            act.wait_ge(vsq_done, j)
                        act.activation(junk[:, 0:VW], zv[:, j, :], ACT.Square, bias=neg_mean[:, j:j + 1],
                                       accum_out=v_sq[:, j:j + 1]).then_inc(vsq_done, 1)

        def project_dve(dve):
            dve.wait_ge(lr_split, 1)
            dve.tensor_tensor(w_lr_lo[:, :, :], w_lr[:, :, :], w_lr_hi[:, :, :].bitcast(F32), ALU.subtract).then_inc(lr_split, 1)
            for p in range(1, 10):
                split_lo(dve, P_Z + p, (P_Z + p) % 2)
                if p == 4:
                    normalise_v(dve)

        def normalise_v(dve):
            dve.wait_ge(ln_in, 32)
            dve.wait_ge(vrs_step, 2)
            for j in range(NT):
                dve.scalar_tensor_tensor(out=zv[:, j, :], in0=zv[:, j, :], scalar=neg_mean[:, j:j + 1], in1=ln_gain[:, 0, :],
                                         op0=ALU.add, op1=ALU.mult).then_inc(vn_step, 1)
                dve.wait_ge(vn_step, 2 * j + 1)
                dve.scalar_tensor_tensor(out=zv[:, j, :], in0=zv[:, j, :], scalar=v_rs[:, j:j + 1], in1=ln_gain[:, 1, :],
                                         op0=ALU.mult, op1=ALU.add).then_inc(vn_step, 1)

        with nc.Block() as block:

            @block.sync
            def _(sp):
                merge_sp(sp)
                swiglu_sp(sp)
                project_sp(sp)

            @block.gpsimd
            def _(pool):
                merge_pool(pool)
                swiglu_pool(pool)
                project_pool(pool)

            @block.tensor
            def _(pe):
                merge_pe(pe)
                swiglu_pe(pe)
                project_pe(pe)

            @block.scalar
            def _(act):
                merge_act(act)
                swiglu_act(act)
                project_act(act)

            @block.vector
            def _(dve):
                merge_dve(dve)
                swiglu_dve(dve)
                project_dve(dve)
        GH = 4
        CH = 64
        NCH = S // CH
        qe = at("qe", [NT, KW], F32, ht)
        ke = at("ke", [NT, KW], F32, ht + 8192)
        kd = at("kd", [NT, 2, KW], F32, ht + 16384)
        la = at("la", [NT, KW], F32, ht + 49152)
        states = at("states", [2, NCH, P], F32, ht + 32768)
        scores = at("scores", [2, GH, P], F32, ht + 57344)
        ws = at("ws", [GH, P], F32, ht + 61440)
        ws_t = at("ws_t", [GH, P], F32, ht + 63488)
        mix_gain = at("mix_gain", [2, VW], F32, ring + 8192)
        to_end = at("to_end", [NT, KW], F32, ring + 16384)
        q_pad = at("q_pad", [2, GH, P], F32, ring + 24576)
        k_t = at("k_t", [2, 2, P], F32, ring + 28672)
        cum_mat, rev_mat, bound_hi, bound_lo = (mix_c[:, i * P:(i + 1) * P] for i in range(4))
        chunk_mat = mix_c[:, 4 * P:MIXC]
        o_sq, o_ms, o_rs = (fixed(x, [NT, GH]) for x in ("o_sq", "o_ms", "o_rs"))
        dec = fixed("dec", [2, NCH])
        bs_t = fixed("bs_t", [GH])
        (mix_in, ws_zero, states_zero, gates_done, la_step, la_done, cum_done, rev_done, ecum_done, erev_done, qe_done, ke_done,
         kd_done, dec_done, dec_ready, wst_done, wst_evac, gm_done, gm_evac, asq_done,
         ars_step, a_done, tq_done, tq_evac, sc_done, sc_step, upd_done, st_done, o_done, o_evac, ors_step, b_step,
         zg_done, kd2_done) = (sem(x) for x in (
             "mix_in", "ws_zero", "states_zero", "gates_done", "la_step", "la_done", "cum_done", "rev_done", "ecum_done",
             "erev_done", "qe_done", "ke_done", "kd_done", "dec_done", "dec_ready",
             "wst_done", "wst_evac", "gm_done", "gm_evac", "asq_done", "ars_step", "a_done", "tq_done", "tq_evac",
             "sc_done", "sc_step", "upd_done", "st_done", "o_done", "o_evac", "ors_step", "b_step", "zg_done", "kd2_done"))

        def two(x, g):
            return x[:, 2 * g:2 * g + 2, :].rearrange("p t n -> p (t n)")

        def mix_sp(sp):
            sp.dma_start(ws[:, :, :], t["gmlp_ws_2"][0].rearrange("h i j -> i h j")).then_inc(mix_in, 16)
            for j, name in enumerate(("gmlp_out_g_2", "gla_out_g_2")):
                sp.dma_start(mix_gain[:, j, :], t[name][0].partition_broadcast(P)).then_inc(mix_in, 16)

        def mix_pool(pool):
            for g in range(4):
                pool.wait_ge(erev_done, g + 1)
                part = slice(2 * g, 2 * g + 2)
                pool.tensor_tensor(kd[0:CH, part, 0, :], to_end[0:CH, part, :], zk[0:CH, part, :], ALU.mult).then_inc(kd_done, 1)
            for j in range(NT):
                if j == 0:
                    pool.wait_ge(mix_in, 48)
                pool.tensor_tensor(zg[:, j, :], zg[:, j, :], mix_gain[:, 1, :], ALU.mult).then_inc(zg_done, 1)
            for j in range(NT):
                one = slice(j, j + 1)
                roots(pool, a_sq[:, one], j + 1, asq_done, ars_step, a_ms[:, one], a_rs[:, one], VW, 2 * j)
                roots(pool, o_sq[:, j, :], j + 1, o_evac, ors_step, o_ms[:, j, :], o_rs[:, j, :], P, 2 * j)

        def mix_pe(pe):
            pe.wait_ge(early_in, 64)
            pe.wait_ge(lr_evac, 2)
            for j in range(NT):
                mm = pe.matmul(ps[:, j // 2, (j % 2) * KW:(j % 2 + 1) * KW], lr_t[0:RANK + 1, j * P:(j + 1) * P],
                               gate_wb[0:RANK + 1, :], start=True, stop=True)
                if j % 2:
                    mm.then_inc(gates_done, 1)
            pe.wait_ge(ws_zero, 1)
            for h in range(GH):
                pe.transpose(ps[:, 4, h * P:(h + 1) * P], ws[:, h, :], ident[:, :])
            pe.transpose(ps[:, 5, 0:GH], bs_nat[0:GH, :], ident[0:GH, 0:GH]).then_inc(wst_done, 1)
            pe.wait_ge(wst_evac, 2)
            for n in range(2 * GH):
                h, g = n % GH, n // GH
                pe.wait_ge(vn_step, 8 * g + 8)
                if n >= 4:
                    pe.wait_ge(gm_evac, n - 3)
                pe.matmul(ps[:, 4 + n % 4, :].rearrange("p (t n) -> p t n", n=P), ws_t[:, h, :],
                          zv[:, 4 * g:4 * g + 4, h * P:(h + 1) * P], start=True, stop=True).then_inc(gm_done, 1)
            for mat, bank0, done_sem in ((cum_mat, 4, cum_done), (rev_mat, 0, rev_done)):
                for g in range(4):
                    pe.wait_ge(la_done, g + 1)
                    pe.wait_ge(gm_evac, 8)
                    pe.matmul(ps[:, bank0 + g, :], mat, two(la, g), start=True, stop=True).then_inc(done_sem, 1)
            pe.wait_ge(ecum_done, 2)
            for j in range(NT):
                for q in range(2):
                    mm = pe.matmul(ps[:, 4, q * NCH + 2 * j:q * NCH + 2 * j + 2], la[:, j, q * P:(q + 1) * P], chunk_mat,
                                   start=True, stop=True)
            mm.then_inc(dec_done, 1)

            def turn_qk(j):
                if j == 0:
                    pe.wait_ge(erev_done, 4)
                pe.wait_ge(qe_done, j // 2 + 1)
                pe.wait_ge(ke_done, j // 2 + 1)
                if j >= 2:
                    pe.wait_ge(tq_evac, j - 1)
                for q in range(4):
                    mm = pe.transpose(ps[:, j % 2, q * P:(q + 1) * P], (qe if q < 2 else ke)[:, j, (q % 2) * P:(q % 2 + 1) * P], ident[:, :])
                mm.then_inc(tq_done, 1)

            def updates(j):
                if j == 0:
                    pe.wait_ge(dec_ready, 1)
                    pe.wait_ge(ecum_done, 8)
                    pe.wait_ge(states_zero, 1)
                pe.wait_ge(kd_done, j // 2 + 1)
                pe.wait_ge(kd2_done, j // 2 + 1)
                if j >= 2:
                    pe.wait_ge(st_done, 4 * (j - 1))
                for c in range(2):
                    for h in range(GH):
                        dst = ps[CH * (h % 2):CH * (h % 2) + CH, 4 + j % 2, (2 * c + h // 2) * P:(2 * c + h // 2 + 1) * P]
                        mm = pe.matmul(dst, kd[:, j, c, h * CH:(h + 1) * CH], zvb[:, j, h * P:(h + 1) * P], start=True, stop=True)
                mm.then_inc(upd_done, 1)

            def scores_of(j):
                pe.wait_ge(tq_evac, j + 1)
                if j >= 2:
                    pe.wait_ge(sc_step, 2 * (j - 2) + 1)
                for h in range(GH):
                    mm = pe.matmul(ps[:, 2 + j % 2, h * P:(h + 1) * P], k_t[:, j % 2, h // 2, :], q_pad[:, j % 2, h, :],
                                   start=True, stop=True)
                mm.then_inc(sc_done, 1)

            turn_qk(0)
            turn_qk(1)
            updates(0)
            scores_of(0)
            for j in range(NT):
                s = j % 2
                if j + 2 < NT:
                    turn_qk(j + 2)
                if j + 1 < NT:
                    updates(j + 1)
                    scores_of(j + 1)
                pe.wait_ge(sc_step, 2 * j + 2)
                pe.wait_ge(st_done, min(4 * j + 2, 30))
                if j >= 2:
                    pe.wait_ge(o_evac, j - 1)
                for h in range(GH):
                    dst = ps[:, 6 + s, h * P:(h + 1) * P]
                    pe.matmul(dst, scores[:, s, h, :], zvb[:, j, h * P:(h + 1) * P], start=True, stop=False)
                    for c in range(2):
                        dst = ps[CH * c:CH * c + CH, 6 + s, h * P:(h + 1) * P]
                        mm = pe.matmul(dst, q_pad[:, s, h, CH * c:CH * c + CH], states[:, h // 2, 2 * j + c, :],
                                       start=False, stop=True)
                mm.then_inc(o_done, 1)

        def mix_act(act):
            for step, fn, more in ((0, ACT.Abs, {}), (1, ACT.Exp, {"scale": -1.0}), (2, ACT.Ln, {"bias": 1.0})):
                for g in range(4):
                    if step == 0:
                        act.wait_ge(gates_done, g + 1)
                    else:
                        act.wait_ge(la_step, 4 * step + g - 3)
                    src = ps[:, g, :] if step == 0 else two(la, g)
                    act.activation(two(la, g), src, fn, **more).then_inc(la_step, 1)
                if step == 0:
                    act.wait_ge(wst_done, 1)
                    act.activation(ws_t[:, :, :].rearrange("p h n -> p (h n)"), ps[:, 4, :], ACT.Copy).then_inc(wst_evac, 1)
                    act.activation(bs_t[:, :], ps[:, 5, 0:GH], ACT.Copy).then_inc(wst_evac, 1)
            for g in range(4):
                act.wait_ge(cum_done, g + 1)
                act.activation(two(qe, g), ps[:, 4 + g, :], ACT.Exp).then_inc(ecum_done, 1)
                act.activation(two(ke, g), ps[:, 4 + g, :], ACT.Exp, scale=-1.0).then_inc(ecum_done, 1)
                act.wait_ge(rev_done, g + 1)
                act.activation(two(to_end, g), ps[:, g, :], ACT.Exp).then_inc(erev_done, 1)
            act.wait_ge(dec_done, 1)
            act.activation(dec[:, :, :].rearrange("p q c -> p (q c)"), ps[:, 4, 0:2 * NCH], ACT.Exp).then_inc(dec_ready, 1)

            def turned_qk(j):
                act.wait_ge(tq_done, j + 1)
                if j < 2:
                    act.wait_ge(states_zero, 1)
                else:
                    act.wait_ge(o_done, j - 1)
                act.activation(k_t[:, j % 2, :, :].rearrange("p q n -> p (q n)"), ps[:, j % 2, 2 * P:4 * P], ACT.Copy)
                for c in range(2):
                    rows = slice(CH * c, CH * c + CH)
                    last = act.activation(q_pad[rows, j % 2, c:GH:2, :], ps[rows, j % 2, 0:2 * P].rearrange("p (q n) -> p q n", n=P), ACT.Copy)
                last.then_inc(tq_evac, 1)

            def gated_square(j):
                act.wait_ge(gm_evac, 8)
                act.wait_ge(asq_done, j) if j else act.wait_ge(vsq_done, NT)
                act.activation(junk[:, 0:VW], zu[:, j, :], ACT.Square, accum_out=a_sq[:, j:j + 1]).then_inc(asq_done, 1)

            turned_qk(0)
            turned_qk(1)
            for j in range(NT):
                gated_square(j)
                act.wait_ge(o_done, j + 1)
                if j + 2 < NT:
                    turned_qk(j + 2)
                act.activation(zvb[:, j, :], ps[:, 6 + j % 2, :], ACT.Copy)
                if j:
                    act.wait_ge(o_evac, j)
                for h in range(GH):
                    last = act.activation(junk[:, VW + h * P:VW + (h + 1) * P], ps[:, 6 + j % 2, h * P:(h + 1) * P], ACT.Square,
                                          accum_out=o_sq[:, j, h:h + 1])
                last.then_inc(o_evac, 1)

        def mix_dve(dve):
            dve.wait_ge(dense_done, D_M)
            dve.memset(states[:, :, 0, :], 0.0)
            for c in range(2):
                rest = slice(CH * (1 - c), CH * (1 - c) + CH)
                last = dve.memset(q_pad[rest, :, c:GH:2, :], 0.0)
            dve.wait_ge(mix_in, 48)
            dve.memset(ws[0:CH, :, CH:P], 0.0).then_inc(ws_zero, 1)
            for c in range(2):
                rest = slice(CH * (1 - c), CH * (1 - c) + CH)
                last = dve.memset(kd[rest, :, c, :], 0.0)
            last.then_inc(states_zero, 1)
            for n in range(2 * GH):
                h, g = n % GH, n // GH
                u = zu[:, 4 * g:4 * g + 4, h * P:(h + 1) * P]
                dve.wait_ge(gm_done, n + 1)
                dve.wait_ge(wst_evac, 2)
                dve.scalar_tensor_tensor(out=u, in0=ps[:, 4 + n % 4, :].rearrange("p (t n) -> p t n", n=P), scalar=bs_t[:, h:h + 1],
                                         in1=u, op0=ALU.add, op1=ALU.mult).then_inc(gm_evac, 1)
            for g in range(4):
                dve.wait_ge(la_step, 8 + g + 1)
                dve.scalar_tensor_tensor(out=two(la, g), in0=ps[:, g, :], scalar=0.0, in1=two(la, g),
                                         op0=ALU.min, op1=ALU.subtract).then_inc(la_done, 1)
            for g in range(4):
                dve.wait_ge(ecum_done, 2 * g + 2)
                dve.scalar_tensor_tensor(out=two(qe, g), in0=two(zq, g), scalar=CH ** -0.5, in1=two(qe, g),
                                         op0=ALU.mult, op1=ALU.mult).then_inc(qe_done, 1)
                dve.tensor_tensor(two(ke, g), two(ke, g), two(zk, g), ALU.mult).then_inc(ke_done, 1)
                dve.wait_ge(erev_done, g + 1)
                part = slice(2 * g, 2 * g + 2)
                dve.tensor_tensor(kd[CH:P, part, 1, :], to_end[CH:P, part, :], zk[CH:P, part, :], ALU.mult).then_inc(kd2_done, 1)

            def mask(j):
                s = j % 2
                dve.wait_ge(sc_done, j + 1)
                if j >= 2:
                    dve.wait_ge(o_done, j - 1)
                rows = ps[:, 2 + s, :].rearrange("p (h n) -> p h n", n=P)
                dve.tensor_tensor(scores[:, s, :, :], rows, bcast(bound_hi, 1, GH), ALU.min).then_inc(sc_step, 1)
                dve.wait_ge(sc_step, 2 * j + 1)
                dve.tensor_tensor(scores[:, s, :, :], scores[:, s, :, :], bcast(bound_lo, 1, GH), ALU.max).then_inc(sc_step, 1)

            def advance(j):
                for c in range(2):
                    n = 2 * j + c
                    if n == NCH - 1:
                        break
                    for q in range(2):
                        if n == 0 and q == 0:
                            dve.wait_ge(dec_ready, 1)
                            dve.wait_ge(states_zero, 1)
                        if c == 0 and q == 0:
                            dve.wait_ge(upd_done, j + 1)
                        if n:
                            dve.wait_ge(st_done, 2 * n - 1 + q)
                        dve.scalar_tensor_tensor(out=states[:, q, n + 1, :], in0=states[:, q, n, :], scalar=dec[:, q, n:n + 1],
                                                 in1=ps[:, 4 + j % 2, (2 * c + q) * P:(2 * c + q + 1) * P],
                                                 op0=ALU.mult, op1=ALU.add).then_inc(st_done, 1)

            def finish_a(j):
                dve.wait_ge(ars_step, 2 * j + 2)
                dve.scalar_tensor_tensor(out=zu[:, j, :], in0=zu[:, j, :], scalar=a_rs[:, j:j + 1], in1=mix_gain[:, 0, :],
                                         op0=ALU.mult, op1=ALU.mult).then_inc(a_done, 1)

            def finish_b(j):
                dve.wait_ge(zg_done, NT)
                dve.wait_ge(ors_step, 2 * j + 2)
                row = zvb[:, j, :].rearrange("p (h n) -> p h n", n=P)
                dve.tensor_tensor(row, row, bcast(o_rs[:, j, :], 2, P), ALU.mult).then_inc(b_step, 1)
                dve.wait_ge(b_step, 2 * j + 1)
                dve.tensor_tensor(zvb[:, j, :], zvb[:, j, :], zg[:, j, :], ALU.mult).then_inc(b_step, 1)

            for j in range(NT + 2):
                if j < NT:
                    advance(j)
                    mask(j)
                if j >= 2:
                    finish_a(j - 2)
                    finish_b(j - 2)

        x_res = at("x_res", [NT, D], F32, k_off)
        gain_m = at("gain_m", [D], F32, rope_at)
        gm_in, added = sem("gm_in"), sem("added")
        m_sq, m_ms, m_rs, m_scaled = sem("m_sq"), sem("m_ms"), sem("m_rs"), sem("m_scaled")
        LAG_M = 5
        def leave_sp(sp):
            load_weights(sp, P_M + 1, panel_of(t["w_out_2"], PN))
            sp.wait_ge(gates_done, 4)
            sp.wait_ge(qe_done, 4)
            sp.dma_start(gain_m[:, :], t["post_mix_g_2"][0].partition_broadcast(P)).then_inc(gm_in, 16)
            sp.dma_start(gain_g[:, :], t["pre_ff_g_2"][0].partition_broadcast(P)).then_inc(gg_in, 16)
            sp.wait_ge(tr_done, T_M + NT)
            for j in range(NT):
                sp.dma_start(x_res[:, j, :], x2_dram[j * P:(j + 1) * P, :]).then_inc(x_in[j], 16)
            for p in range(2, 4):
                load_weights(sp, P_M + p, panel_of(t["w_out_2"], p * PN))
            load_weights(sp, P_G, panel_of(t["w_ff1_2"], 0))

        def leave_pool(pool):
            for j in range(NT + 2):
                if j < NT:
                    pool.wait_ge(m_sq, j + 1)
                    pool.tensor_scalar(msq[:, 8 + j:9 + j], sumsq[:, 8 + j:9 + j], 1.0 / D, EPS, ALU.mult, ALU.add).then_inc(m_ms, 1)
                    pool.wait_ge(m_ms, j + 1)
                    pool.tensor_tensor(rstd[:, 8 + j:9 + j], msq[:, 8 + j:9 + j], neg_half[:, 8 + j:9 + j], ALU.pow).then_inc(m_rs, 1)
                if j >= 2:
                    norm_tile(pool, j - 2, T_G, D)

        def leave_pe(pe):
            for j in range(NT):
                pe.wait_ge(a_done, j + 1)
                pe.wait_ge(b_step, 2 * j + 2)
                if j == 0:
                    pe.wait_ge(st_done, 30)
                    pe.wait_ge(o_evac, NT)
                pe.wait_ge(tl_done, T_M + j - 1)
                for k in range(KT):
                    src = (zu if k < 4 else zvb)[:, j, (k % 4) * P:(k % 4 + 1) * P]
                    mm = pe.transpose(ps[:, 4 + 2 * (j % 2) + k // 4, (k % 4) * P:(k % 4 + 1) * P], src, ident[:, :])
                mm.then_inc(tr_done, 1)
            for p in range(4):
                for j in rows_pe(pe, P_M + p, (P_M + p) % 2, NT, T_M, D_M + NT * p):
                    if p == 3 and j >= LAG_M:
                        turn_tile(pe, j - LAG_M, (j - LAG_M) % 2, T_G)
            for j in range(NT - LAG_M, NT):
                turn_tile(pe, j, j % 2, T_G)

        def leave_act(act):
            act.wait_ge(kd_done, 4)
            act.wait_ge(kd2_done, 4)
            split_hi(act, P_M, P_M % 2, used=(o_done, NT))
            turn_act(act, NT, T_M, None)
            for p in range(4):
                split_hi(act, P_M + p + 1, (P_M + p + 1) % 2, used=(dense_done, D_M + NT * p))
                for j in range(NT + (LAG_M if p == 3 else 0)):
                    if j < NT:
                        act.wait_ge(dense_done, D_M + NT * p + j + 1)
                        act.activation(q_nat[:, j, p * PN:(p + 1) * PN], ps[:, j % 4, 0:PN], ACT.Copy).then_inc(dense_evac, 1)
                    if p == 3 and j < NT:
                        act.wait_ge(dense_evac, D_M + NT * p + j + 1)
                        act.wait_ge(m_sq, j) if j else act.wait_ge(ss_done, T_M)
                        act.activation(junk[:, :], q_nat[:, j, :], ACT.Square, accum_out=sumsq[:, 8 + j:9 + j]).then_inc(m_sq, 1)
                    if p == 3 and 2 <= j < NT + 2:
                        act.wait_ge(added, j - 1)
                        act.wait_ge(m_sq, min(j + 1, NT))
                        sum_tile(act, j - 2, T_G, x_res[:, j - 2, :])
                    if p == 3 and j >= LAG_M:
                        turned_hi(act, j - LAG_M, (j - LAG_M) % 2, T_G)

        def leave_dve(dve):
            split_lo(dve, P_M, P_M % 2)
            for j in range(NT):
                dve.wait_ge(th_done, T_M + j + 1)
                dve.tensor_tensor(ht_lo[:, :, j * P:(j + 1) * P], turned(j % 2),
                                  ht_hi[:, :, j * P:(j + 1) * P].bitcast(F32), ALU.subtract).then_inc(tl_done, 1)
            for p in range(1, 5):
                split_lo(dve, P_M + p, (P_M + p) % 2)
            dve.wait_ge(gm_in, 16)
            dve.wait_ge(gg_in, 16)
            for j in range(1, NT + LAG_M):
                if j <= NT:
                    k = j - 1
                    dve.wait_ge(m_rs, k + 1)
                    dve.scalar_tensor_tensor(out=q_nat[:, k, :], in0=q_nat[:, k, :], scalar=rstd[:, 8 + k:9 + k], in1=gain_m[:, :],
                                             op0=ALU.mult, op1=ALU.mult).then_inc(m_scaled, 1)
                    dve.wait_ge(m_scaled, k + 1)
                    dve.wait_ge(x_in[k], 48)
                    dve.tensor_tensor(x_res[:, k, :], x_res[:, k, :], q_nat[:, k, :], ALU.add).then_inc(added, 1)
                if 3 <= j < NT + 3:
                    scale_tile(dve, j - 3, (j - 3) % 2, T_G, x_res[:, j - 3, :], gain_g[:, :], False)
                if j >= LAG_M:
                    turned_lo(dve, j - LAG_M, (j - LAG_M) % 2, T_G)
        gain_g = at("gain_g", [D], F32, k_off + 32768)
        gain_e = at("gain_e", [D], F32, rope_at)
        relu = at("relu", [2, S], F32, xnr)
        gg_in, ge_in = sem("gg_in"), sem("ge_in")
        def chunk_no(c):
            return CH1 + c

        e_scaled, e_done, e_last, out_stored = sem("e_scaled"), sem("e_done"), sem("e_last"), sem("out_stored")
        POOLED = 6

        def p_hid(c):
            return P_G if isinstance(c, int) and c == 0 else P_G + 2 * c - 1

        def p_ff(c):
            return P_G + 2 * c + 2 if not (isinstance(c, int) and c == CH2 - 1) else P_END - 1

        S_DOWN = (P_G + 2) % 2

        def steps(eng, step):
            step(0)
            with eng.Fori(1, CH2 - 2) as c:
                step(c)
            step(CH2 - 2)

        def ffn_sp(sp):
            sp.wait_ge(m_scaled, NT)
            sp.dma_start(gain_e[:, :], t["post_ff_g_2"][0].partition_broadcast(P)).then_inc(ge_in, 16)
            load_weights(sp, P_G + 1, panel_of(t["w_ff1_2"], PN))

            def step(c, more=True):
                load_weights(sp, p_ff(c), down_panel(t["w_ff2_2"], c * PN), stage_down())
                if more:
                    load_weights(sp, p_hid(c + 2), panel_of(t["w_ff1_2"], (c + 2) * PN))
            with sp.Fori(0, CH2 - 2) as c:
                step(c)
            step(CH2 - 2, False)
            step(CH2 - 1, False)
            for j in range(NT):
                if j < POOLED:
                    sp.wait_ge(e_done, j + 1)
                else:
                    sp.wait_ge(e_last, j - POOLED + 1)
                sp.dma_start(out[0, j * P:(j + 1) * P, :], q_nat[:, j, :]).then_inc(out_stored, 16)
            sp.wait_ge(out_stored, 16 * NT)

        def ffn_pool(pool):
            for j in range(NT):
                norm_tile(pool, j, T_E, D)
                if 1 <= j <= POOLED:
                    pool.wait_ge(e_scaled, j)
                    pool.tensor_tensor(q_nat[:, j - 1, :], q_nat[:, j - 1, :], x_res[:, j - 1, :], ALU.add).then_inc(e_done, 1)

        def ffn_pe(pe):
            pe.wait_ge(tl_done, T_G + NT)

            def hidden(c, slot):
                def free(b):
                    if not isinstance(c, int) or c > 0:
                        pe.wait_ge(function_done, 4 * chunk_no(c) + b - 3)
                features_pe(pe, p_hid(c), slot, c, 0, hidden_done, free)

            hidden(0, P_G % 2)

            def step(c):
                hidden(c + 1, 1 - S_DOWN)
                down_pe(pe, p_ff(c), S_DOWN, chunk_no(c), act_lo_done, down_done, down_evac)
            steps(pe, step)
            down_pe(pe, P_END - 1, 1 - S_DOWN, chunk_no(CH2 - 1), act_lo_done, down_done, down_evac)

        def ffn_act(act):
            split_hi(act, P_G + 1, (P_G + 1) % 2, used=(dense_done, D_M + 4 * NT))

            def relus(c):
                for b in range(4):
                    act.wait_ge(hidden_done, 4 * chunk_no(c) + b + 1)
                    if not isinstance(c, int) or c > 0:
                        act.wait_ge(act_lo_done, 4 * chunk_no(c) + b - 3)
                    elif b == 0:
                        act.wait_ge(tr_done, T_G + NT)
                    act.activation(quarter(relu, b), ps[:, b, :], ACT.Relu).then_inc(function_done, 1)

            relus(0)

            def step(c):
                used = (down_done, 16 * chunk_no(c)) if not isinstance(c, int) or c > 0 else (hidden_done, 4 * chunk_no(0) + 4)
                split_hi(act, p_ff(c), S_DOWN, used=used)
                act_split_hi(act, chunk_no(c), relu, act_done, act_hi_done, down_done)
                relus(c + 1)
                split_hi(act, P_G + 2 * c + 3, 1 - S_DOWN, used=(hidden_done, 4 * chunk_no(c) + 8))
            steps(act, step)
            act_split_hi(act, chunk_no(CH2 - 1), relu, act_done, act_hi_done, down_done)
            for j in range(NT):
                act.wait_ge(down_evac, 16 * chunk_no(CH2 - 1) + 2 * j + 2)
                sum_tile(act, j, T_E, q_nat[:, j, :])

        def ffn_dve(dve):
            split_lo(dve, P_G + 1, (P_G + 1) % 2)

            def squares(c):
                for b in range(4):
                    dve.wait_ge(function_done, 4 * chunk_no(c) + b + 1)
                    dve.tensor_tensor(quarter(relu, b), quarter(relu, b), quarter(relu, b), ALU.mult).then_inc(act_done, 1)

            def step(c):
                squares(c)
                split_lo(dve, p_ff(c), S_DOWN)
                act_split_lo(dve, chunk_no(c), relu, act_hi_done, act_lo_done)
                first = isinstance(c, int) and c == 0
                down_dve(dve, chunk_no(c), range(4), down_done, down_evac, first)
                split_lo(dve, P_G + 2 * c + 3, 1 - S_DOWN)
                down_dve(dve, chunk_no(c), range(4, 2 * NT), down_done, down_evac, first)
            steps(dve, step)
            squares(CH2 - 1)
            act_split_lo(dve, chunk_no(CH2 - 1), relu, act_hi_done, act_lo_done)
            dve.wait_ge(ge_in, 16)
            for j in range(NT + 1):
                if j < NT:
                    down_dve(dve, chunk_no(CH2 - 1), range(2 * j, 2 * j + 2), down_done, down_evac)
                if j:
                    k = j - 1
                    dve.wait_ge(rs_done, normed(T_E) + k + 1)
                    dve.wait_ge(down_evac, 16 * chunk_no(CH2 - 1) + 2 * k + 2)
                    dve.scalar_tensor_tensor(out=q_nat[:, k, :], in0=q_nat[:, k, :], scalar=rstd[:, k:k + 1], in1=gain_e[:, :],
                                             op0=ALU.mult, op1=ALU.mult).then_inc(e_scaled, 1)
                    if k >= POOLED:
                        dve.wait_ge(e_scaled, k + 1)
                        dve.tensor_tensor(q_nat[:, k, :], q_nat[:, k, :], x_res[:, k, :], ALU.add).then_inc(e_last, 1)

        with nc.Block() as block:

            @block.sync
            def _(sp):
                mix_sp(sp)
                leave_sp(sp)
                ffn_sp(sp)

            @block.gpsimd
            def _(pool):
                mix_pool(pool)
                leave_pool(pool)
                ffn_pool(pool)

            @block.tensor
            def _(pe):
                mix_pe(pe)
                leave_pe(pe)
                ffn_pe(pe)

            @block.scalar
            def _(act):
                mix_act(act)
                leave_act(act)
                ffn_act(act)

            @block.vector
            def _(dve):
                mix_dve(dve)
                leave_dve(dve)
                ffn_dve(dve)


def constants():
    P=128
    pick=np.zeros((2,P,P),np.float32)
    for g in range(4):
        pick[0,32*g,:]=1; pick[1,32*g+1,:]=1
    tok=np.arange(1024)
    q=np.arange(16,dtype=np.float32)
    inv=(1.0/(np.float32(10000.0)**(q/np.float32(16)))).astype(np.float32)
    rope=np.zeros((P,2,8,64),np.float32)
    for half,pos in enumerate((tok//64,tok%64)):
        ang=pos.astype(np.float32)[:,None]*inv[None]
        c=np.cos(ang).astype(np.float32); s=np.sin(ang).astype(np.float32)
        c=c.reshape(8,P,16).transpose(1,0,2); s=s.reshape(8,P,16).transpose(1,0,2)
        for p2 in range(2):
            rope[:,0,:,half*32+p2*16:half*32+p2*16+16]=c
            rope[:,1,:,half*32+p2*16:half*32+p2*16+16]=s if p2 else -s
    BIG=np.float32(1e30)
    rm=np.zeros((P,9),np.float32); rm[:64,8]=BIG; rm[64:,0]=BIG
    qc=np.arange(P)%64; kc=np.arange(64); cs=np.clip(qc-8,0,48)
    cm=np.where((kc[None]>=cs[:,None])&(kc[None]<cs[:,None]+16),0,BIG).astype(np.float32)
    i=np.arange(P)[:,None]; j=np.arange(P)[None]
    band=np.zeros((P,9,P),np.float32); band[:,2]=np.where(j>=i,0,BIG); band[:,4]=band[:,8]=np.where(j<=i,0,BIG)
    same=(i//64)==(j//64)
    mix=np.zeros((P,4*P+2),np.float32)
    mix[:,0:P]=np.where(same&(i<=j),1/16,0); mix[:,P:2*P]=np.where(same&(i>j),1/16,0)
    keep=same&(i<=j); FM=np.finfo(np.float32).max
    mix[:,2*P:3*P]=np.where(keep,FM,0); mix[:,3*P:4*P]=np.where(keep,-FM,0)
    mix[:64,4*P]=1/16; mix[64:,4*P+1]=1/16
    return {"k_mix":mix,"k_ident":np.eye(P,dtype=np.float32),"k_pick":pick,"k_rope":rope,"k_row_mask":rm,"k_col_mask":cm,"k_band":band}


NAMES = ["x", "c", "ctx", "c_ctx", "w_mod", "b_mod", "norm1_g", "w_in", "qn_a", "kn_a", "sink_a", "qn_b", "kn_b", "rpb_b",
         "on_a", "on_b", "w_out", "norm2_g", "w_gate", "w_up", "w_down", "pre_mix_g_2", "w_in_2", "gmlp_ln_g_2", "gmlp_ln_b_2",
         "gmlp_ws_2", "gmlp_bs_2", "gmlp_out_g_2", "gla_gate_w_2", "gla_gate_b_2", "gla_out_g_2", "w_out_2", "post_mix_g_2",
         "pre_ff_g_2", "w_ff1_2", "w_ff2_2", "post_ff_g_2"]


def kernel(**inputs):
    import concourse.bacc as bacc
    from concourse.bass_utils import run_bass_kernel_spmd

    nc = bacc.Bacc("TRN2", target_bir_lowering=False, num_devices=1)
    arrays = {name: np.ascontiguousarray(inputs[name]) for name in NAMES}
    arrays.update(constants())
    t = {name: nc.dram_tensor(name, a.shape, F32, kind="ExternalInput").ap() for name, a in arrays.items()}
    out = nc.dram_tensor("out", (1, S, D), F32, kind="ExternalOutput").ap()
    program(nc, t, out)
    r = run_bass_kernel_spmd(nc, [arrays], core_ids=[0])
    return r.results[0]["out"]
```
